# Optimizing a Trainium2 kernel written in Bass

```python
import math
import jax, jax.numpy as jnp
from jax import lax
import numpy as np

D_MODEL = 1024
BATCH = 1
SEQ = 512
DEPTH = 2

N_A = DEPTH // 2
N_B = DEPTH - N_A

H_A = 4
DK_A = D_MODEL // H_A
DV_A = 2 * DK_A
WIDTH_A = H_A * DV_A
CHUNK = 128
ROPE_BASE_A = 10000.0

H_B = 16
QK_NOPE = 128
QK_ROPE = 64
V_HEAD = 128
Q_LORA = 768
KV_LORA = 512
WIDTH_B = H_B * V_HEAD
Q_BLOCK = 128
ROPE_BASE_B = 10000.0

IN_A = H_A * DK_A * 2 + WIDTH_A + WIDTH_A
IN_B = Q_LORA + WIDTH_B

DEEPNORM_ALPHA = (2.0 * DEPTH) ** 0.25
DEEPNORM_BETA = (8.0 * DEPTH) ** -0.25


def _layer_norm(x, g, b, eps=1e-5):
    xf = x.astype(jnp.float32)
    mu = jnp.mean(xf, axis=-1, keepdims=True)
    var = jnp.mean(jnp.square(xf - mu), axis=-1, keepdims=True)
    return ((xf - mu) * lax.rsqrt(var + eps)).astype(x.dtype) * g + b

def _rms_norm(x, g, eps=1e-6):
    xf = x.astype(jnp.float32)
    return (xf * lax.rsqrt(jnp.mean(jnp.square(xf), axis=-1, keepdims=True) + eps)).astype(x.dtype) * g

def _rope(x, base):
    s, d = x.shape[1], x.shape[-1]
    half = d // 2
    inv = base ** (-jnp.arange(half, dtype=jnp.float32) / half)
    ang = jnp.arange(s, dtype=jnp.float32)[:, None] * inv[None, :]
    shp = (s,) + (1,) * (x.ndim - 3) + (half,)
    cos = jnp.cos(ang).reshape(shp).astype(x.dtype)
    sin = jnp.sin(ang).reshape(shp).astype(x.dtype)
    x1, x2 = x[..., :half], x[..., half:]
    return jnp.concatenate([x1 * cos - x2 * sin, x2 * cos + x1 * sin], axis=-1)

def _chunkwise_retention(q, k, v):
    b, s, h, dk = q.shape
    dv = v.shape[-1]
    n = s // CHUNK

    def to_chunks(t):
        return t.astype(jnp.float32).reshape(b, n, CHUNK, h, t.shape[-1]).transpose(1, 0, 3, 2, 4)

    qc, kc, vc = to_chunks(q), to_chunks(k), to_chunks(v)
    lg = jnp.log1p(-jnp.exp2(-5.0 - jnp.arange(h, dtype=jnp.float32)))
    idx = jnp.arange(CHUNK, dtype=jnp.float32)
    diff = idx[:, None] - idx[None, :]
    causal = diff >= 0
    dmat = jnp.where(causal, jnp.exp(jnp.where(causal, diff, 0.0)[None] * lg[:, None, None]), 0.0)
    qdec = jnp.exp((idx + 1.0)[None, :] * lg[:, None])
    kdec = jnp.exp((CHUNK - 1.0 - idx)[None, :] * lg[:, None])
    cdec = jnp.exp(CHUNK * lg)

    def step(state, inp):
        qi, ki, vi = inp
        scores = jnp.einsum('bhcd,bhed->bhce', qi, ki) * dmat
        inner = jnp.einsum('bhce,bhev->bhcv', scores, vi)
        cross = jnp.einsum('bhcd,bhdv->bhcv', qi * qdec[None, :, :, None], state)
        state = state * cdec[None, :, None, None] + jnp.einsum(
            'bhcd,bhcv->bhdv', ki * kdec[None, :, :, None], vi)
        return state, inner + cross

    init = jnp.zeros((b, h, dk, dv), jnp.float32)
    _, out = lax.scan(step, init, (qc, kc, vc))
    return out.transpose(1, 0, 3, 2, 4).reshape(b, s, h, dv)

def _retention_layer(x, w_in, w_out):
    b, s, _ = x.shape
    hproj = x @ w_in
    qk = H_A * DK_A
    q = hproj[..., :qk].reshape(b, s, H_A, DK_A)
    k = hproj[..., qk:2 * qk].reshape(b, s, H_A, DK_A)
    v = hproj[..., 2 * qk:2 * qk + WIDTH_A].reshape(b, s, H_A, DV_A)
    gate = hproj[..., 2 * qk + WIDTH_A:]
    q = _rope(q, ROPE_BASE_A)
    k = _rope(k, ROPE_BASE_A) * (DK_A ** -0.5)
    o = _chunkwise_retention(q, k, v)
    mu = jnp.mean(o, axis=-1, keepdims=True)
    var = jnp.mean(jnp.square(o - mu), axis=-1, keepdims=True)
    o = ((o - mu) * lax.rsqrt(var + 1e-5)).astype(x.dtype).reshape(b, s, WIDTH_A)
    return (o * jax.nn.silu(gate)) @ w_out

def _shared_latent_kv(x, w_down, kv_norm, w_up):
    b, s, _ = x.shape
    c = x @ w_down
    lat = _rms_norm(c[..., :KV_LORA], kv_norm)
    k_rope = _rope(c[..., KV_LORA:], ROPE_BASE_B)
    kv = (lat @ w_up).reshape(b, s, H_B, QK_NOPE + V_HEAD)
    return kv[..., :QK_NOPE], k_rope, kv[..., QK_NOPE:]

def _causal_block_attention(q_nope, q_rope, k_nope, k_rope, v):
    b, s, h, _ = q_nope.shape
    nb = s // Q_BLOCK
    scale = (QK_NOPE + QK_ROPE) ** -0.5
    qn_b = q_nope.reshape(b, nb, Q_BLOCK, h, QK_NOPE).transpose(1, 0, 2, 3, 4)
    qr_b = q_rope.reshape(b, nb, Q_BLOCK, h, QK_ROPE).transpose(1, 0, 2, 3, 4)
    kpos = jnp.arange(s)

    def block(args):
        qn_i, qr_i, i = args
        sc = (jnp.einsum('bqhd,bkhd->bhqk', qn_i, k_nope)
              + jnp.einsum('bqhr,bkr->bhqk', qr_i, k_rope)).astype(jnp.float32) * scale
        qpos = i * Q_BLOCK + jnp.arange(Q_BLOCK)
        sc = jnp.where(kpos[None, :] <= qpos[:, None], sc, -jnp.inf)
        p = jax.nn.softmax(sc, axis=-1).astype(v.dtype)
        return jnp.einsum('bhqk,bkhd->bqhd', p, v)

    out = lax.map(block, (qn_b, qr_b, jnp.arange(nb)))
    return out.transpose(1, 0, 2, 3, 4).reshape(b, s, h, V_HEAD)

def _mla_layer(x, w_in, q_norm, w_uq, w_out, k_nope, k_rope, v):
    b, s, _ = x.shape
    hproj = x @ w_in
    q_lat, gate = hproj[..., :Q_LORA], hproj[..., Q_LORA:]
    q = (_rms_norm(q_lat, q_norm) @ w_uq).reshape(b, s, H_B, QK_NOPE + QK_ROPE)
    q_nope = q[..., :QK_NOPE]
    q_rope = _rope(q[..., QK_NOPE:], ROPE_BASE_B)
    o = _causal_block_attention(q_nope, q_rope, k_nope, k_rope, v).reshape(b, s, WIDTH_B)
    return (o * jax.nn.silu(gate)) @ w_out

def first_inputs(seed: int = 0) -> dict:
    key = jax.random.key(seed)
    ks = jax.random.split(key, 16)
    nrm = jax.random.normal
    f32 = jnp.float32
    return {
        "x": nrm(ks[0], (BATCH, SEQ, D_MODEL), f32),
        "a_w_in": nrm(ks[1], (N_A, D_MODEL, IN_A), f32) * D_MODEL ** -0.5,
        "a_w_out": nrm(ks[2], (N_A, WIDTH_A, D_MODEL), f32) * (WIDTH_A ** -0.5 * DEEPNORM_BETA),
        "b_w_in": nrm(ks[3], (N_B, D_MODEL, IN_B), f32) * D_MODEL ** -0.5,
        "b_q_norm": 1.0 + 0.02 * nrm(ks[4], (N_B, Q_LORA), f32),
        "b_w_uq": nrm(ks[5], (N_B, Q_LORA, H_B * (QK_NOPE + QK_ROPE)), f32) * Q_LORA ** -0.5,
        "b_w_out": nrm(ks[6], (N_B, WIDTH_B, D_MODEL), f32) * (WIDTH_B ** -0.5 * DEEPNORM_BETA),
        "kv_w_down": nrm(ks[7], (D_MODEL, KV_LORA + QK_ROPE), f32) * D_MODEL ** -0.5,
        "kv_norm": 1.0 + 0.02 * nrm(ks[8], (KV_LORA,), f32),
        "kv_w_up": nrm(ks[9], (KV_LORA, H_B * (QK_NOPE + V_HEAD)), f32) * KV_LORA ** -0.5,
        "ln_g": 1.0 + 0.02 * nrm(ks[10], (DEPTH, D_MODEL), f32),
        "ln_b": 0.02 * nrm(ks[11], (DEPTH, D_MODEL), f32),
    }

def first_block(x, a_w_in, a_w_out, b_w_in, b_q_norm, b_w_uq, b_w_out,
              kv_w_down, kv_norm, kv_w_up, ln_g, ln_b):
    shared = None
    for layer in range(DEPTH):
        if layer < N_A:
            y = _retention_layer(x, a_w_in[layer], a_w_out[layer])
        else:
            j = layer - N_A
            if j == 0:
                shared = _shared_latent_kv(x, kv_w_down, kv_norm, kv_w_up)
            y = _mla_layer(x, b_w_in[j], b_q_norm[j], b_w_uq[j], b_w_out[j], *shared)
        x = _layer_norm(DEEPNORM_ALPHA * x + y, ln_g[layer], ln_b[layer])
    return x


DEPTH_2 = 1

MIX_WIDTH = D_MODEL
POOL_WIDTH = MIX_WIDTH // 2
POOL_WINDOWS = (2, 4, 8, 16)
N_POOL_GROUPS = len(POOL_WINDOWS)
POOL_GROUP = POOL_WIDTH // N_POOL_GROUPS
NA_WIDTH = MIX_WIDTH - POOL_WIDTH
NA_HEAD_DIM = 64
NA_HEADS = NA_WIDTH // NA_HEAD_DIM
GRID_W = 64
WIN_ROWS = 8
WIN_COLS = 16
COL_BLOCK = 16
COL_BAND = 2 * WIN_COLS
N_COL_BLOCKS = GRID_W // COL_BLOCK
D_FF = 4 * D_MODEL
IN_WIDTH = POOL_WIDTH + 3 * NA_WIDTH
EPS = 1e-6


def rmsnorm(x, g):
    x32 = x.astype(jnp.float32)
    y = x32 * lax.rsqrt(jnp.mean(jnp.square(x32), axis=-1, keepdims=True) + EPS)
    return y.astype(x.dtype) * g

def pool_mixer(u, w_pool, pool_scale):
    B, T, _ = u.shape
    u32 = u.astype(jnp.float32)
    cs = jnp.concatenate([jnp.zeros((B, 1, POOL_WIDTH), jnp.float32),
                          jnp.cumsum(u32, axis=1)], axis=1)
    t = jnp.arange(T)
    outs = []
    for gi, w in enumerate(POOL_WINDOWS):
        sl = slice(gi * POOL_GROUP, (gi + 1) * POOL_GROUP)
        lo = jnp.clip(t - w // 2, 0, T)
        hi = jnp.clip(t - w // 2 + w, 0, T)
        cs_g = cs[:, :, sl]
        win_sum = jnp.take(cs_g, hi, axis=1) - jnp.take(cs_g, lo, axis=1)
        mean = win_sum / (hi - lo).astype(jnp.float32)[None, :, None]
        outs.append(mean - u32[:, :, sl])
    pooled = jnp.stack(outs, axis=2).astype(u.dtype)
    mixed = jnp.einsum('btgc,gcd->btgd', pooled, w_pool)
    return mixed.reshape(B, T, POOL_WIDTH) * pool_scale

def neighbourhood_attention(q, k, v, rpb):
    B, T, H, dh = q.shape
    rows = T // GRID_W
    kr = min(WIN_ROWS, rows)
    scale = dh ** -0.5

    def to_grid(a):
        return a.reshape(B, rows, GRID_W, H, dh).transpose(0, 3, 1, 2, 4)

    q_g, k_g, v_g = to_grid(q), to_grid(k), to_grid(v)

    cols = np.arange(GRID_W)
    c0 = np.clip(cols - WIN_COLS // 2, 0, GRID_W - WIN_COLS)
    band_start = np.clip(np.arange(N_COL_BLOCKS) * COL_BLOCK - WIN_COLS // 2, 0, GRID_W - COL_BAND)
    key_cols = band_start[:, None] + np.arange(COL_BAND)
    q_cols = (np.arange(N_COL_BLOCKS) * COL_BLOCK)[:, None] + np.arange(COL_BLOCK)
    qc0 = c0[q_cols][:, :, None]
    kc = key_cols[:, None, :]
    col_ok = (kc >= qc0) & (kc < qc0 + WIN_COLS)
    dc_idx = np.clip(kc - q_cols[:, :, None] + WIN_COLS - 1, 0, 2 * WIN_COLS - 2)
    bias_c = rpb[:, :, dc_idx]
    col_ok_b = jnp.asarray(col_ok)[:, :, None, :]

    def row_block(r):
        r0 = jnp.clip(r - kr // 2, 0, rows - kr)
        k_rows = lax.dynamic_slice_in_dim(k_g, r0, kr, axis=2)
        v_rows = lax.dynamic_slice_in_dim(v_g, r0, kr, axis=2)
        k_band = jnp.take(k_rows, key_cols, axis=3)
        v_band = jnp.take(v_rows, key_cols, axis=3)
        q_row = lax.dynamic_index_in_dim(q_g, r, axis=2, keepdims=False)
        q_row = q_row.reshape(B, H, N_COL_BLOCKS, COL_BLOCK, dh)
        s = jnp.einsum('bhjqd,bhijkd->bhjqik', q_row, k_band).astype(jnp.float32) * scale
        dr_idx = r0 + jnp.arange(kr) - r + (WIN_ROWS - 1)
        bias = jnp.take(bias_c, dr_idx, axis=1).transpose(0, 2, 3, 1, 4)
        s = s + bias[None].astype(jnp.float32)
        s = jnp.where(col_ok_b, s, -jnp.inf)
        p = jax.nn.softmax(s.reshape(B, H, N_COL_BLOCKS, COL_BLOCK, kr * COL_BAND), axis=-1)
        p = p.reshape(B, H, N_COL_BLOCKS, COL_BLOCK, kr, COL_BAND).astype(v.dtype)
        o = jnp.einsum('bhjqik,bhijkd->bhjqd', p, v_band)
        return o.reshape(B, H, GRID_W, dh)

    out = lax.map(row_block, jnp.arange(rows))
    return out.transpose(1, 0, 3, 2, 4).reshape(B, T, H * dh)

def second_inputs(seed: int = 0) -> dict:
    key = jax.random.key(seed)
    ks = jax.random.split(key, 12)
    f32 = jnp.float32
    x = jax.random.normal(ks[0], (BATCH, SEQ, D_MODEL), f32)
    norm_mix_g = 1.0 + 0.02 * jax.random.normal(ks[1], (DEPTH_2, D_MODEL), f32)
    w_in = jax.random.normal(ks[2], (DEPTH_2, D_MODEL, IN_WIDTH), f32) * D_MODEL ** -0.5
    w_pool = jax.random.normal(ks[3], (DEPTH_2, N_POOL_GROUPS, POOL_GROUP, POOL_GROUP), f32) * POOL_GROUP ** -0.5
    pool_scale = 1.0 + 0.1 * jax.random.normal(ks[4], (DEPTH_2, POOL_WIDTH), f32)
    rpb = 0.5 * jax.random.normal(ks[5], (DEPTH_2, NA_HEADS, 2 * WIN_ROWS - 1, 2 * WIN_COLS - 1), f32)
    w_out = jax.random.normal(ks[6], (DEPTH_2, MIX_WIDTH, D_MODEL), f32) * MIX_WIDTH ** -0.5
    norm_mlp_g = 1.0 + 0.02 * jax.random.normal(ks[7], (DEPTH_2, D_MODEL), f32)
    w_up = jax.random.normal(ks[8], (DEPTH_2, D_MODEL, D_FF), f32) * D_MODEL ** -0.5
    w_down = jax.random.normal(ks[9], (DEPTH_2, D_FF, D_MODEL), f32) * D_FF ** -0.5
    final_g = 1.0 + 0.02 * jax.random.normal(ks[10], (D_MODEL,), f32)
    return {"x": x, "norm_mix_g": norm_mix_g, "w_in": w_in, "w_pool": w_pool,
            "pool_scale": pool_scale, "rpb": rpb, "w_out": w_out,
            "norm_mlp_g": norm_mlp_g, "w_up": w_up, "w_down": w_down,
            "final_g": final_g}

def second_block(x, norm_mix_g, w_in, w_pool, pool_scale, rpb, w_out,
              norm_mlp_g, w_up, w_down, final_g):
    B, T, _ = x.shape
    for l in range(DEPTH_2):
        h = rmsnorm(x, norm_mix_g[l])
        proj = h @ w_in[l]
        u = proj[..., :POOL_WIDTH]
        q, k, v = jnp.split(proj[..., POOL_WIDTH:], 3, axis=-1)
        q = q.reshape(B, T, NA_HEADS, NA_HEAD_DIM)
        k = k.reshape(B, T, NA_HEADS, NA_HEAD_DIM)
        v = v.reshape(B, T, NA_HEADS, NA_HEAD_DIM)
        a = pool_mixer(u, w_pool[l], pool_scale[l])
        b = neighbourhood_attention(q, k, v, rpb[l])
        x = x + jnp.concatenate([a, b], axis=-1) @ w_out[l]
        h = rmsnorm(x, norm_mlp_g[l])
        x = x + jnp.square(jax.nn.relu(h @ w_up[l])) @ w_down[l]
    return rmsnorm(x, final_g)


def setup_inputs(seed=0):
    out = dict(first_inputs(seed))
    for name, value in second_inputs(seed + 1).items():
        if name != "x":
            out[name + "_2"] = value
    return out


def reference(
    x, a_w_in, a_w_out, b_w_in, b_q_norm, b_w_uq, b_w_out, kv_w_down, kv_norm, kv_w_up, ln_g,
    ln_b, norm_mix_g_2, w_in_2, w_pool_2, pool_scale_2, rpb_2, w_out_2, norm_mlp_g_2, w_up_2,
    w_down_2, final_g_2,
):
    x = first_block(
        x, a_w_in, a_w_out, b_w_in, b_q_norm, b_w_uq, b_w_out, kv_w_down, kv_norm, kv_w_up,
        ln_g, ln_b,
    )
    return second_block(
        x, norm_mix_g_2, w_in_2, w_pool_2, pool_scale_2, rpb_2, w_out_2, norm_mlp_g_2, w_up_2,
        w_down_2, final_g_2,
    )


_drawn_inputs = setup_inputs


def setup_inputs(seed=0):
    import zlib

    import numpy as np

    out = dict(_drawn_inputs(seed))
    spreads = {}
    factors = {'b_q_norm': 8.0,
     'kv_norm': 8.0,
     'norm_mix_g_2': 4.723,
     'norm_mlp_g_2': 3.364,
     'final_g_2': 2.868}
    for name, (base, spread) in spreads.items():
        noise = np.random.default_rng([zlib.crc32(name.encode()), seed]).standard_normal(out[name].shape)
        drawn = base * np.exp(spread * noise) if base else spread * noise
        out[name] = __import__('jax').numpy.asarray(drawn.astype(out[name].dtype))
    for name, factor in factors.items():
        out[name] = (out[name] * factor).astype(out[name].dtype)
    return out
```

```python
from contextlib import ExitStack

import numpy as np

import concourse.bass as bass
from concourse import mybir

F32 = mybir.dt.float32
F32R = mybir.dt.float32r
ALU = mybir.AluOpType
ACT = mybir.ActivationFunctionType
AX = mybir.AxisListType.X

P = 128
SEQ = 512
DM = 1024
TT = SEQ // P
KX = DM // P
ALPHA = 4.0 ** 0.25
LN_EPS = 1e-5
RMS_EPS = 1e-6
MASKED = -1e30

HA, DKA, DVA = 4, 256, 512
VT = DVA // P
HB, NOPE, ROPE, VH = 16, 128, 64, 128
QLORA, KVLORA = 768, 512
KQ, KC = QLORA // P, KVLORA // P
PAIRS = HB // 2
SCALE_B = float(NOPE + ROPE) ** -0.5
WINDOWS = (2, 4, 8, 16)
HN, DHN = 8, 64
GRID = 64
ROWS = SEQ // GRID
BLK = 16
BAND = 32
NBLK = GRID // BLK
SCALE_N = float(DHN) ** -0.5
BAND_START = [min(max(j * BLK - 8, 0), GRID - BAND) for j in range(NBLK)]
BIAS_W = BAND + 16
DFF = 4 * DM
KF = DFF // P
PAD = 8

PANEL = 2304
PAN = 2048
A0 = 0
AO = A0 + 6 * HA
B0 = AO + 8
M0 = B0 + 5
BO = M0 + 3 * PAIRS
L0 = BO + 8
WO = L0 + 8
UP = WO + 4
DN = UP + 16
PANELS = DN + 16

COL_CG, COL_QG, COL_MIX, COL_MLP, COL_PS = 0, KC, KC + KQ, KC + KQ + KX, KC + KQ + 2 * KX
COLS = COL_PS + 4

KT_AT = [0, 512, 896, 1152]
TRI = 1280


class Own:

    def __init__(self, eng, sem):
        self.eng, self.sem, self.n, self.i, self.per = eng, sem, 0, 0, 0

    def mark(self, ins):
        ins.then_inc(self.sem, 1)
        self.n += 1

    def settle(self):
        self.eng.wait_ge(self.sem, self.i * self.per + self.n)

    def enter(self, i, per):
        self.i, self.per, self.first = i, per, self.n

    def leave(self, times):
        assert self.n - self.first == self.per, (self.n - self.first, self.per)
        self.n, self.i, self.per = self.first + self.per * times, 0, 0


def program(nc, t, out, last_stage=99):
    with ExitStack() as ctx:
        def sb(name, shape, dt=F32, where=ctx):
            return where.enter_context(nc.sbuf_tensor(name, shape, dt))

        def sem(name):
            return ctx.enter_context(nc.semaphore(name))

        bank = [ctx.enter_context(nc.psum_tensor(f"bank{i}", [P, 512], F32)) for i in range(8)]

        stage = [sb(f"stage{i}", [P, PANEL]) for i in range(2)]
        whi = [sb(f"whi{i}", [P, PANEL], F32R) for i in range(2)]
        wlo = [sb(f"wlo{i}", [P, PANEL], F32R) for i in range(2)]
        xhi = sb("xhi", [P, KX, SEQ], F32R)
        xlo = sb("xlo", [P, KX, SEQ], F32R)
        xres = sb("xres", [P, TT, DM])
        ident = sb("ident", [P, P])
        cols = sb("cols", [P, COLS])
        stat = sb("stat", [P, TT, 2, 6])
        mv = sb("mv", [P, TT, 2])
        small = sb("small", [P, 4, 8])
        mark = ctx.enter_context(ExitStack())

        oT = sb("oT", [P, HA * VT, SEQ], F32, mark)
        with ExitStack() as h:
            qk_hi = sb("qk_hi", [P, 4, SEQ], F32R, h)
            qk_lo = sb("qk_lo", [P, 4, SEQ], F32R, h)
            v_hi = sb("v_hi", [P, TT, DVA], F32R, h)
            v_lo = sb("v_lo", [P, TT, DVA], F32R, h)
            gate = sb("gate", [P, VT, SEQ], F32, h)
            s_hi = sb("s_hi", [P, TRI], F32R, h)
            s_lo = sb("s_lo", [P, TRI], F32R, h)
            decay = sb("decay", [P, SEQ], F32, h)
            rope_a = sb("rope_a", [P, 2, SEQ], F32, h)
            work = sb("work", [P, 4, SEQ], F32, h)
        with ExitStack() as h:
            ar_hi = sb("ar_hi", [P, 4, SEQ], F32R, h)
            ar_lo = sb("ar_lo", [P, 4, SEQ], F32R, h)
            rows = sb("rows", [P, 2, DM], F32, h)
        mark.close()
        with ExitStack() as h:
            c_hi = sb("c_hi", [P, KC, SEQ], F32R, h)
            c_lo = sb("c_lo", [P, KC, SEQ], F32R, h)
            ql_hi = sb("ql_hi", [P, KQ, SEQ], F32R, h)
            ql_lo = sb("ql_lo", [P, KQ, SEQ], F32R, h)
            kr_hi = sb("kr_hi", [P, SEQ], F32R, h)
            kr_lo = sb("kr_lo", [P, SEQ], F32R, h)
            rope_b = sb("rope_b", [P, 2, SEQ], F32, h)
            id_r = sb("id_r", [P, P], F32R, h)
            mask_r = sb("mask_r", [P, P], F32R, h)
            rtmp = sb("rtmp", [P, 2, SEQ], F32, h)
            with ExitStack() as g:
                c_tok = sb("c_tok", [P, TT, KVLORA], F32, g)
                q_tok = sb("q_tok", [P, TT, QLORA], F32, g)
                wkr = sb("wkr", [P, KX, P], F32, g)
                wkr_hi = sb("wkr_hi", [P, KX, P], F32R, g)
                wkr_lo = sb("wkr_lo", [P, KX, P], F32R, g)
                mask_f = sb("mask_f", [P, P], F32, g)
            with ExitStack() as g:
                qn_hi = sb("qn_hi", [P, 2, SEQ], F32R, g)
                qn_lo = sb("qn_lo", [P, 2, SEQ], F32R, g)
                qr_hi = sb("qr_hi", [P, SEQ], F32R, g)
                qr_lo = sb("qr_lo", [P, SEQ], F32R, g)
                kn_hi = sb("kn_hi", [P, 2, SEQ], F32R, g)
                kn_lo = sb("kn_lo", [P, 2, SEQ], F32R, g)
                vb_hi = sb("vb_hi", [P, TT, 2 * VH], F32R, g)
                vb_lo = sb("vb_lo", [P, TT, 2 * VH], F32R, g)
                gt = sb("gt", [P, 2, SEQ], F32, g)
                prob = sb("prob", [P, TRI], F32, g)
                pt_hi = sb("pt_hi", [P, TRI], F32R, g)
                pt_lo = sb("pt_lo", [P, TRI], F32R, g)
                og = sb("og", [P, 2, SEQ], F32, g)
                sm = sb("sm", [P, 4, 8], F32, g)
        with ExitStack() as h:
            bT = sb("bT", [P, HB, SEQ], F32, h)
            br_hi = sb("br_hi", [P, 4, SEQ], F32R, h)
            br_lo = sb("br_lo", [P, 4, SEQ], F32R, h)
            rows2 = sb("rows2", [P, 2, DM], F32, h)
        with ExitStack() as h:
            mixT = sb("mixT", [P, KX, SEQ], F32, h)
            with ExitStack() as f:
                h_tok = sb("h_tok", [P, TT, DM], F32, f)
                vband = h_tok[:, :, :].rearrange("p t (a n) -> p (t a) n", a=2)
                nq_hi = sb("nq_hi", [P, 4, SEQ], F32R, f)
                nq_lo = sb("nq_lo", [P, 4, SEQ], F32R, f)
                nk_hi = sb("nk_hi", [P, 4, SEQ], F32R, f)
                nk_lo = sb("nk_lo", [P, 4, SEQ], F32R, f)
                bias = sb("bias", [P, HN, ROWS, BIAS_W], F32, f)
                nmask = sb("nmask", [P, NBLK, BAND], F32, f)
                nmask_r = sb("nmask_r", [P, NBLK, BAND], F32R, f)
                id_n = sb("id_n", [P, P], F32R, f)
                with ExitStack() as g:
                    v_tok = sb("v_tok", [P, TT, SEQ], F32, g)
                with ExitStack() as g:
                    upad = sb("upad", [P, 4, SEQ + 2 * PAD], F32, g)
                    win = sb("win", [P, 2, SEQ + 2 * PAD], F32, g)
                    pool_hi = sb("pool_hi", [P, SEQ], F32R, g)
                    pool_lo = sb("pool_lo", [P, SEQ], F32R, g)
                    wp = sb("wp", [P, 4, P], F32, g)
                    wp_hi = sb("wp_hi", [P, 4, P], F32R, g)
                    wp_lo = sb("wp_lo", [P, 4, P], F32R, g)
                    edge = sb("edge", [P, 4, 2 * PAD], F32, g)
                with ExitStack() as g:
                    nt = sb("nt", [P, 2, 2, 256], F32, g)
                    npt_hi = sb("npt_hi", [P, 2, SEQ], F32R, g)
                    npt_lo = sb("npt_lo", [P, 2, SEQ], F32R, g)
                    nsm = sb("nsm", [P, 2, 3, 2], F32, g)
            with ExitStack() as f:
                h2_tok = sb("h2_tok", [P, TT, DM], F32, f)
                cr_hi = sb("cr_hi", [P, 4, SEQ], F32R, f)
                cr_lo = sb("cr_lo", [P, 4, SEQ], F32R, f)
        with ExitStack() as h:
            hid = sb("hid", [P, KF, SEQ], F32, h)
            relu = sb("relu", [P, 4, SEQ], F32, h)
            dr_hi = sb("dr_hi", [P, 4, SEQ], F32R, h)
            dr_lo = sb("dr_lo", [P, 4, SEQ], F32R, h)
            frow = sb("frow", [P, DM], F32, h)

        landed = [sem(f"landed{i}") for i in range(2)]
        w_hi = sem("w_hi")
        w_lo = sem("w_lo")
        half_done = sem("half_done")
        aux = {n: sem(f"ld_{n}") for n in ("xT", "x", "const", "decay", "kr", "rows", "rows2", "ropeb", "bias",
                                           "edge", "wp", "nmask", "idn", "frow")}
        vst = sem("vst")
        vld = [sem(f"vld{i}") for i in range(8)]
        bld = [sem(f"bld{i}") for i in range(4)]
        dv = sem("dve_step")
        ac = sem("act_step")
        xt_t, xt_hi, xt_lo = sem("xt_t"), sem("xt_hi"), sem("xt_lo")
        a_qk, a_q32, a_qkhi, a_qklo = sem("a_qk"), sem("a_q32"), sem("a_qkhi"), sem("a_qklo")
        a_v, a_vhi, a_vlo = sem("a_v"), sem("a_vhi"), sem("a_vlo")
        a_s, a_dec, a_shi, a_slo = sem("a_s"), sem("a_dec"), sem("a_shi"), sem("a_slo")
        a_g, a_th, a_gt = sem("a_g"), sem("a_th"), sem("a_gt")
        a_o, a_var, a_sd, a_on, a_t, a_ot = (sem("a_o"), sem("a_var"), sem("a_sd"), sem("a_on"), sem("a_t"),
                                             sem("a_ot"))
        y_done = sem("y_done")
        ar_h, ar_l = sem("ar_h"), sem("ar_l")
        n_var, n_sd, n_rs, n_nm, n_x = sem("n_var"), sem("n_sd"), sem("n_rs"), sem("n_nm"), sem("n_x")
        r_sum, r_ss, r_ms, r_sd, r_rs, r_h = (sem("r_sum"), sem("r_ss"), sem("r_ms"), sem("r_sd"), sem("r_rs"),
                                              sem("r_h"))
        b_c, b_ql, b_kr, b_ct, b_qt = sem("b_c"), sem("b_ql"), sem("b_kr"), sem("b_ct"), sem("b_qt")
        b_css, b_cms, b_csd, b_crs, b_ctok = sem("b_css"), sem("b_cms"), sem("b_csd"), sem("b_crs"), sem("b_ctok")
        b_qss, b_qms, b_qsd, b_qrs, b_qtok = sem("b_qss"), sem("b_qms"), sem("b_qsd"), sem("b_qrs"), sem("b_qtok")
        b_chi, b_clo, b_qhi, b_qlo = sem("b_chi"), sem("b_clo"), sem("b_qhi"), sem("b_qlo")
        b_kr32, b_krhi, b_krlo, b_w, b_wl = sem("b_kr32"), sem("b_krhi"), sem("b_krlo"), sem("b_w"), sem("b_wl")
        m_q, m_kv, m_s, m_g, m_t, m_o = (sem("m_q"), sem("m_kv"), sem("m_s"), sem("m_g"), sem("m_t"), sem("m_o"))
        m_qr32, m_qhi, m_qlo, m_kvhi, m_kvlo = (sem("m_qr32"), sem("m_qhi"), sem("m_qlo"), sem("m_kvhi"),
                                                sem("m_kvlo"))
        m_nb, m_exp, m_p, m_th, m_gt, m_pthi, m_ptlo, m_og = (
            sem("m_nb"), sem("m_exp"), sem("m_p"), sem("m_th"), sem("m_gt"), sem("m_pthi"), sem("m_ptlo"),
            sem("m_og"))
        m_st = [sem("m_st0"), sem("m_st1")]
        l_v, l_vt, l_q, l_qhi, l_qlo, l_u, l_up = (sem("l_v"), sem("l_vt"), sem("l_q"), sem("l_qhi"), sem("l_qlo"),
                                                   sem("l_u"), sem("l_up"))
        l_pool, l_phi, l_plo, l_mix, l_mo, l_w, l_wl = (sem("l_pool"), sem("l_phi"), sem("l_plo"), sem("l_mix"),
                                                        sem("l_mo"), sem("l_w"), sem("l_wl"))
        l_bhi, l_blo, l_mk = sem("l_bhi"), sem("l_blo"), sem("l_mk")
        e_s, e_nb, e_exp, e_p, e_t, e_thi, e_tlo, e_o, e_oc = (
            sem("e_s"), sem("e_nb"), sem("e_exp"), sem("e_p"), sem("e_t"), sem("e_thi"), sem("e_tlo"), sem("e_o"),
            sem("e_oc"))
        u_m, u_r, u_s = sem("u_m"), sem("u_r"), sem("u_s")
        o_ready, o_st = sem("o_ready"), sem("o_st")

        def by_block(x):
            return x.rearrange("p (j r c) -> p j r c", j=NBLK, r=ROWS)

        def from_rows(x):
            return x.rearrange("p (r j c) -> p j r c", j=NBLK, r=ROWS)

        def split_dots(pe, dst, a_hi, a_lo, b_hi, b_lo, start, stop):
            pe.matmul(dst, a_hi, b_hi, start=start, stop=False)
            pe.matmul(dst, a_hi, b_lo, start=False, stop=False)
            return pe.matmul(dst, a_lo, b_hi, start=False, stop=stop)

        block = ctx.enter_context(nc.Block())

        @block.sync
        def _(sp):
            def load(p, width=PAN, n=0):
                if p >= 2:
                    sp.wait_ge(w_lo, n + (p - 1))
                sp.dma_start(stage[p % 2][:, 0:width],
                             t["w"][bass.ds(n + p, 1), :, 0:width].rearrange("a p n -> (a p) n")
                             ).then_inc(landed[p % 2], 16)

            xt_view = xres[:, :, :].rearrange("p t (a n) -> p (t a) n", a=2)
            sp.dma_start(xt_view, t["xT"]).then_inc(aux["xT"], 16)
            load(0)
            load(1)
            sp.dma_start(cols[:, :], t["cols"]).then_inc(aux["const"], 16)
            sp.dma_start(ident[:, :], t["ident"]).then_inc(aux["const"], 16)
            sp.dma_start(rope_a[:, :, :], t["rope_a"]).then_inc(aux["const"], 16)
            with sp.Fori(0, 17) as i:
                for j in range(2):
                    load(2 + j, PAN, 2 * i)
            load(36)
            with sp.Fori(0, PAIRS // 2) as i:
                for j in range(6):
                    load(M0 + j, PANEL if j % 3 == 0 else PAN, 6 * i)
            load(BO)
            with sp.Fori(0, 25) as i:
                for j in range(2):
                    load(BO + 1 + j, PAN, 2 * i)
            load(PANELS - 1)
            for q in range(TT):
                sp.wait_ge(o_ready, q + 1)
                sp.dma_start(out[q * P:(q + 1) * P, :], xres[:, q, :]).then_inc(o_st, 16)
            sp.wait_ge(o_st, 16 * TT)

        @block.gpsimd
        def _(pool):
            def split_lo(p, width=PAN, n=0):
                pool.wait_ge(w_hi, n + (p + 1))
                pool.tensor_tensor(wlo[p % 2][:, 0:width], stage[p % 2][:, 0:width],
                                   whi[p % 2][:, 0:width].bitcast(F32), ALU.subtract).then_inc(w_lo, 1)

            with pool.Fori(0, 18) as i:
                for j in range(2):
                    split_lo(j, PAN, 2 * i)
            split_lo(36)
            with pool.Fori(0, PAIRS // 2) as i:
                for j in range(6):
                    split_lo(M0 + j, PANEL if j % 3 == 0 else PAN, 6 * i)
            with pool.Fori(0, 26) as i:
                for j in range(2):
                    split_lo(BO + j, PAN, 2 * i)

        @block.tensor
        def _(pe):
            def panel(p, n=0):
                pe.wait_ge(w_lo, n + (p + 1))
                return whi[p % 2], wlo[p % 2]

            def tiles(p, n, nk, width, parts, moving, lo, hi, before, signal):
                wh, wl = panel(p, n)
                wh, wl = (w[:, 0:nk * width].rearrange("p (k n) -> p k n", k=nk) for w in (wh, wl))
                for m in range(lo, hi):
                    before(m)
                    for k in range(nk):
                        c = slice(m * P, (m + 1) * P)
                        last = split_dots(pe, parts[m][:, :], wh[:, k, c], wl[:, k, c],
                                          moving[0][:, k, :], moving[1][:, k, :], k == 0, k == nk - 1)
                    last.then_inc(signal, 1)

            def token_tiles(p, n, nk, k0, width, dst, start, stop, before, signal):
                wh, wl = panel(p, n)
                wh, wl = (w[:, 0:nk * width].rearrange("p (k n) -> p k n", k=nk) for w in (wh, wl))
                for q in range(TT):
                    before(q)
                    for k in range(nk):
                        r = slice(q * P, (q + 1) * P)
                        last = split_dots(pe, dst(q), xhi[:, k0 + k, r], xlo[:, k0 + k, r],
                                          wh[:, k, :], wl[:, k, :], start and k == 0, stop and k == nk - 1)
                    if stop:
                        last.then_inc(signal, 1)
                if not stop:
                    last.then_inc(half_done, 1)

            def nothing(_):
                pass

            def transpose_x(src):
                for k in range(KX):
                    for q in range(TT):
                        last = pe.transpose(bank[k][:, q * P:(q + 1) * P], src[:, q, k * P:(k + 1) * P],
                                            ident[:, :])
                    last.then_inc(xt_t, 1)

            def project_out(p0, nk, hi, lo, a0):
                def half(n, j, first):
                    wh, wl = panel(p0 + j, n)
                    for b in range(2):
                        kk = 2 * j + b
                        pe.wait_ge(ar_l, 2 * n + (a0 + kk + 1))
                        for q in range(TT):
                            for c in range(2):
                                w = slice(b * DM + c * 512, b * DM + c * 512 + 512)
                                r = slice(q * P, (q + 1) * P)
                                last = split_dots(pe, bank[2 * q + c][:, :], hi[:, kk % 4, r], lo[:, kk % 4, r],
                                                  wh[:, w], wl[:, w], first and kk == 0, False)
                    last.then_inc(half_done, 1)

                half(0, 0, True)
                half(0, 1, False)
                if nk > 8:
                    with pe.Fori(1, nk // 4 - 1) as i:
                        half(2 * i, 0, False)
                        half(2 * i, 1, False)
                n = nk // 2 - 2
                w_ = [panel(p0 + n + j) for j in range(2)]
                pe.wait_ge(ar_l, a0 + nk)
                for q in range(TT):
                    for kk in range(4):
                        wh, wl = w_[kk // 2]
                        for c in range(2):
                            w = slice(kk % 2 * DM + c * 512, kk % 2 * DM + c * 512 + 512)
                            r = slice(q * P, (q + 1) * P)
                            last = split_dots(pe, bank[2 * q + c][:, :], hi[:, kk, r], lo[:, kk, r],
                                              wh[:, w], wl[:, w], False, kk == 3)
                    last.then_inc(y_done, 1)

            A, B = bank[0:4], bank[4:8]
            pe.wait_ge(aux["const"], 48)
            pe.wait_ge(xt_lo, KX)
            with pe.Fori(0, HA) as h:
                n = 6 * h
                tiles(A0, n, KX, 256, B, (xhi, xlo), 0, 2, lambda m: pe.wait_ge(a_ot, 4 * h + (m + 1)), a_qk)
                tiles(A0 + 1, n, KX, 256, B[2:], (xhi, xlo), 0, 2, lambda m: pe.wait_ge(a_ot, 4 * h + (m + 3)),
                      a_qk)
                token_tiles(A0 + 2, n, 4, 0, 512, lambda q: A[q][:, :], True, False,
                            lambda q: pe.wait_ge(a_gt, 4 * h + (q + 1)), a_v)
                token_tiles(A0 + 3, n, 4, 4, 512, lambda q: A[q][:, :], False, True, nothing, a_v)
                pe.wait_ge(a_qklo, 4 * h + 4)
                for kt in range(TT):
                    for d in range(2):
                        r = slice(kt * P, (kt + 1) * P)
                        last = split_dots(pe, B[kt][:, 0:SEQ - kt * P], qk_hi[:, 2 + d, r], qk_lo[:, 2 + d, r],
                                          qk_hi[:, d, kt * P:], qk_lo[:, d, kt * P:], d == 0, d == 1)
                    last.then_inc(a_s, 1)
                tiles(A0 + 4, n, KX, 256, A, (xhi, xlo), 0, 2, lambda m: pe.wait_ge(a_vlo, 4 * h + (m + 1)), a_g)
                pe.wait_ge(a_vlo, 4 * h + 4)
                for q in range(TT):
                    pe.wait_ge(a_slo, 4 * h + (q + 1))
                    for kt in range(q + 1):
                        r = slice(KT_AT[kt] + (q - kt) * P, KT_AT[kt] + (q - kt + 1) * P)
                        last = split_dots(pe, B[q][:, :], s_hi[:, r], s_lo[:, r], v_hi[:, kt, :], v_lo[:, kt, :],
                                          kt == 0, kt == q)
                    last.then_inc(a_o, 1)
                tiles(A0 + 5, n, KX, 256, A[2:], (xhi, xlo), 0, 2, nothing, a_g)
                pe.wait_ge(a_on, 4 * h + 4)
                for j in range(VT):
                    for q in range(TT):
                        last = pe.transpose(B[j][:, q * P:(q + 1) * P], work[:, q, j * P:(j + 1) * P], ident[:, :])
                    last.then_inc(a_t, 1)
            pe.wait_ge(a_gt, 4 * HA + 4)
            pe.wait_ge(a_ot, 4 * HA + 4)
            project_out(AO, HA * VT, ar_hi, ar_lo, 0)
            pe.wait_ge(n_x, TT)
            transpose_x(xres)

            if last_stage < 2:
                return
            pe.wait_ge(xt_lo, 2 * KX)
            token_tiles(B0, 0, 4, 0, 512, lambda q: A[q][:, :], True, False, nothing, b_c)
            token_tiles(B0 + 1, 0, 4, 4, 512, lambda q: A[q][:, :], False, True, nothing, b_c)
            pe.wait_ge(b_wl, 1)
            for k in range(KX):
                last = split_dots(pe, bank[7][:, :], wkr_hi[:, k, :], wkr_lo[:, k, :], xhi[:, k, :], xlo[:, k, :],
                                  k == 0, k == KX - 1)
            last.then_inc(b_kr, 1)
            token_tiles(B0 + 2, 0, 4, 0, 512, lambda q: B[q][:, :], True, False,
                        lambda q: pe.wait_ge(b_kr32, 1) if q == 3 else None, b_ql)
            pe.wait_ge(b_ctok, TT)
            for j in range(KC):
                for q in range(TT):
                    last = pe.transpose(A[j][:, q * P:(q + 1) * P], c_tok[:, q, j * P:(j + 1) * P], ident[:, :])
                last.then_inc(b_ct, 1)
            token_tiles(B0 + 3, 0, 4, 4, 512, lambda q: B[q][:, :], False, True, nothing, b_ql)
            token_tiles(B0 + 4, 0, KX, 0, 256, lambda q: A[q][:, 0:256], True, True,
                        lambda q: pe.wait_ge(b_clo, q + 1), b_ql)
            pe.wait_ge(b_qtok, 2 * TT)
            for j in range(KQ):
                for q in range(TT):
                    last = pe.transpose(bank[j][:, q * P:(q + 1) * P], q_tok[:, q, j * P:(j + 1) * P], ident[:, :])
                last.then_inc(b_qt, 1)
            pe.wait_ge(b_qlo, KQ)
            pe.wait_ge(b_krlo, 1)
            pe.wait_ge(b_w, 3)

            with pe.Fori(0, PAIRS // 2) as it:
                for s in range(2):
                    n = 6 * it
                    p = M0 + 3 * s

                    def c(per, k):
                        return 2 * per * it + (per * s + k)

                    tiles(p, n, KQ, 384, bank[4:7], (ql_hi, ql_lo), 0, 3, nothing, m_q)
                    pe.wait_ge(m_gt, c(2, 2))
                    pe.wait_ge(m_og, c(2, 1))
                    tiles(p + 1, n, KC, 512, bank[0:2], (c_hi, c_lo), 0, 2, nothing, m_kv)
                    wh, wl = (w[:, 0:PAN].rearrange("p (k n) -> p k n", k=KC) for w in panel(p + 1, n))
                    for q in range(TT):
                        for k in range(KC):
                            r = slice(q * P, (q + 1) * P)
                            last = split_dots(pe, bank[2 + q // 2][:, q % 2 * 256:q % 2 * 256 + 256],
                                              c_hi[:, k, r], c_lo[:, k, r], wh[:, k, 256:512], wl[:, k, 256:512],
                                              k == 0, k == KC - 1)
                        if q % 2:
                            last.then_inc(m_kv, 1)

                    def scores(e):
                        for q in range(TT):
                            w = (q + 1) * P
                            r = slice(q * P, w)
                            dst = bank[4 + q]
                            f = slice(ROPE * e, ROPE * e + ROPE)
                            pe.matmul(dst[:, 0:w], qn_hi[:, e, r], kn_hi[:, e, 0:w], start=True, stop=False)
                            pe.matmul(dst[:, r], id_r[:, :], mask_r[:, :], start=False, stop=False)
                            pe.matmul(dst[:, 0:w], qn_hi[:, e, r], kn_lo[:, e, 0:w], start=False, stop=False)
                            pe.matmul(dst[:, 0:w], qn_lo[:, e, r], kn_hi[:, e, 0:w], start=False, stop=False)
                            split_dots(pe, dst[:, 0:w], qr_hi[f, r], qr_lo[f, r], kr_hi[f, 0:w], kr_lo[f, 0:w],
                                       False, True).then_inc(m_s, 1)

                    def turn(e):
                        dst = [bank[1], bank[2], bank[3]] if e == 0 else [bank[2], bank[3], bank[4]]
                        for kt in range(TT):
                            for q in range(kt, TT):
                                at = (q - kt) * P + (256 if kt == 3 else 0)
                                src = q * (q + 1) // 2 * P + kt * P
                                last = pe.transpose(dst[min(kt, 2)][:, at:at + P], prob[:, src:src + P], ident[:, :])
                            if kt != 2:
                                last.then_inc(m_t, 1)

                    def attend(e, dst):
                        for kt in range(TT):
                            r = slice(KT_AT[kt], KT_AT[kt] + SEQ - kt * P)
                            last = split_dots(pe, dst[:, kt * P:], vb_hi[:, kt, e * VH:(e + 1) * VH],
                                              vb_lo[:, kt, e * VH:(e + 1) * VH], pt_hi[:, r], pt_lo[:, r],
                                              kt == 0, kt == TT - 1)
                        last.then_inc(m_o, 1)

                    def gate_part(m, k0, k1):
                        wh, wl = (w[:, 0:PAN].rearrange("p (k n) -> p k n", k=KX) for w in panel(p + 2, n))
                        for k in range(k0, k1):
                            f = slice(m * P, (m + 1) * P)
                            last = split_dots(pe, bank[0][:, :], wh[:, k, f], wl[:, k, f], xhi[:, k, :],
                                              xlo[:, k, :], k == 0, k == KX - 1)
                        return last

                    pe.wait_ge(m_qlo, c(3, 3))
                    pe.wait_ge(m_kvlo, c(4, 1))
                    pe.wait_ge(m_og, c(2, 2))
                    scores(0)
                    gate_part(0, 0, KX).then_inc(m_g, 1)
                    pe.wait_ge(m_kvlo, c(4, 4))
                    pe.wait_ge(m_p, c(8, 4))
                    turn(0)
                    scores(1)
                    pe.wait_ge(m_gt, c(2, 3))
                    gate_part(1, 0, KX // 2)
                    pe.wait_ge(m_ptlo, c(6, 3))
                    attend(0, bank[1])
                    pe.wait_ge(m_p, c(8, 8))
                    turn(1)
                    gate_part(1, KX // 2, KX).then_inc(m_g, 1)
                    pe.wait_ge(m_ptlo, c(6, 6))
                    attend(1, bank[7])
            pe.wait_ge(m_gt, 2 * PAIRS + 2)
            pe.wait_ge(m_og, 2 * PAIRS + 2)
            project_out(BO, HB, br_hi, br_lo, HA * VT)

            pe.wait_ge(r_h, TT)
            transpose_x(h_tok)
            if last_stage < 3:
                return
            pe.wait_ge(xt_lo, 3 * KX)
            token_tiles(L0, 0, 4, 0, 512, lambda q: A[q][:, :], True, False, nothing, l_v)
            token_tiles(L0 + 1, 0, 4, 4, 512, lambda q: A[q][:, :], False, True, nothing, l_v)
            for a in range(2):
                tiles(L0 + 2 + a, 0, KX, 256, B[2 * a:], (xhi, xlo), 0, 2, nothing, l_q)
            for a in range(2):
                tiles(L0 + 4 + a, 0, KX, 256, A[2 * a:], (xhi, xlo), 0, 2,
                      lambda m: pe.wait_ge(l_vt, 2 * a + m + 1), l_q)
            for a in range(2):
                tiles(L0 + 6 + a, 0, KX, 256, B[2 * a:], (xhi, xlo), 0, 2,
                      lambda m: pe.wait_ge(l_qlo, 2 * a + m + 1), l_u)
            pe.wait_ge(l_qlo, 8)
            pe.wait_ge(l_wl, 1)
            for g in range(4):
                pe.wait_ge(l_plo, g + 1)
                split_dots(pe, A[g][:, :], wp_hi[:, g, :], wp_lo[:, g, :], pool_hi[:, :], pool_lo[:, :], True, True
                           ).then_inc(l_mix, 1)
            pe.wait_ge(l_mo, 4)
            pe.wait_ge(l_up, 4)
            pe.wait_ge(l_mk, 2)
            steps = [(hp, j) for j in range(NBLK) for hp in range(HN // 2)]
            for i in range(len(steps) + 2):
                if i < len(steps):
                    hp, j = steps[i]
                    if i >= 2:
                        pe.wait_ge(e_nb, i - 1)
                    for e in range(2):
                        f = slice(DHN * e, DHN * e + DHN)
                        o = bank[2 * (i % 2) + e][:, 0:256]
                        q_ = [x[f, hp, j * P:(j + 1) * P] for x in (nq_hi, nq_lo)]
                        k_ = [x[f, hp, :].rearrange("p (r c) -> p r c", r=ROWS)[
                              :, :, BAND_START[j]:BAND_START[j] + BAND] for x in (nk_hi, nk_lo)]
                        pe.matmul(o, id_n[:, :], nmask_r[:, j:j + 1, :].to_broadcast([P, ROWS, BAND]),
                                  start=True, stop=False)
                        last = split_dots(pe, o, q_[0], q_[1], k_[0], k_[1], False, True)
                    last.then_inc(e_s, 1)
                if 1 <= i <= len(steps):
                    m = i - 1
                    pe.wait_ge(e_p, m + 1)
                    if m >= 2:
                        pe.wait_ge(e_tlo, m - 1)
                    for e in range(2):
                        for half in range(2):
                            a = (2 * e + half) * P
                            last = pe.transpose(bank[4 + m % 2][:, a:a + P],
                                                nt[:, m % 2, e, half * P:(half + 1) * P], ident[:, :])
                    last.then_inc(e_t, 1)
                if i >= 2:
                    m = i - 2
                    hp, j = steps[m]
                    pe.wait_ge(e_tlo, m + 1)
                    if hp == 0:
                        pe.wait_ge(l_blo, 2 * j + 2)
                    if m >= 2:
                        pe.wait_ge(e_oc, 2 * (m - 1))
                    for e in range(2):
                        for half in range(2):
                            a = (2 * e + half) * P
                            last = split_dots(pe, bank[6 + m % 2][:, e * P:(e + 1) * P],
                                              xhi[:, 2 * j + half, hp * P:(hp + 1) * P],
                                              xlo[:, 2 * j + half, hp * P:(hp + 1) * P],
                                              npt_hi[:, m % 2, a:a + P], npt_lo[:, m % 2, a:a + P],
                                              half == 0, half == 1)
                    last.then_inc(e_o, 1)
            pe.wait_ge(e_oc, 2 * len(steps))
            project_out(WO, KX, cr_hi, cr_lo, HA * VT + HB)
            pe.wait_ge(r_h, 2 * TT)
            transpose_x(h2_tok)
            if last_stage < 4:
                return
            pe.wait_ge(xt_lo, 4 * KX)
            with pe.Fori(0, 8) as i:
                for a in range(2):
                    tiles(UP + a, 2 * i, KX, 256, bank[2 * a:], (xhi, xlo), 0, 2,
                          lambda m: pe.wait_ge(u_r, 4 * i + (2 * a + m + 1)), u_m)
            pe.wait_ge(u_r, KF + 4)
            project_out(DN, KF, dr_hi, dr_lo, HA * VT + HB + KX)

        @block.scalar
        def _(act):
            own = Own(act, ac)

            def split_hi(p, used=None, count=0, width=PAN, n=0):
                act.wait_ge(landed[p % 2], 8 * n + 16 * (p // 2 + 1))
                if used is not None:
                    act.wait_ge(used, count)
                act.activation(whi[p % 2][:, 0:width], stage[p % 2][:, 0:width], ACT.Copy).then_inc(w_hi, 1)

            def copy(dst, src, signal, scale=1.0):
                act.activation(dst, src, ACT.Copy, scale=scale).then_inc(signal, 1)

            def transposed_x(round_, col=None):
                for k in range(KX):
                    act.wait_ge(xt_t, KX * (round_ - 1) + k + 1)
                    copy(xhi[:, k, :], bank[k][:, :], xt_hi, 1.0 if col is None else cols[:, col + k:col + k + 1])

            def project_out(p0, nk, src, hi, done, ready):
                for kk in range(4):
                    ready(kk)
                    copy(hi[:, kk, :], src[:, kk, :], ar_h)

                def half(j, n, k):
                    split_hi(p0 + j, half_done, n + (done + j - 1), PAN, n)
                    for b in range(2):
                        copy(hi[:, (2 * j + b) % 4, :], src[:, bass.ds(k + (2 * j + b), 1), :].rearrange(
                            "p a n -> p (a n)"), ar_h)

                for c in range(1, min(4, nk // 4)):
                    ready(4 * c)
                with act.Fori(1, nk // 4) as i:
                    for j in range(2):
                        half(j, 2 * i, 4 * i)

            def root(q, row0, wait, signal):
                wait()
                act.activation(small[:, 1, row0 + q:row0 + q + 1], small[:, 0, row0 + q:row0 + q + 1],
                               ACT.Sqrt).then_inc(signal, 1)

            def layer_norm(round_, next_panel):
                def normalise(q):
                    act.wait_ge(n_rs, TT * round_ + q + 1)
                    act.activation(xres[:, q, :], xres[:, q, :], ACT.Identity, scale=small[:, 2, q:q + 1],
                                   bias=small[:, 3, q:q + 1]).then_inc(n_nm, 1)

                for q in range(TT):
                    root(q, 0, lambda: act.wait_ge(n_var, TT * round_ + q + 1), n_sd)
                    if q:
                        normalise(q - 1)
                split_hi(next_panel, y_done, TT * (round_ + 1))
                split_hi(next_panel + 1)
                normalise(TT - 1)

            def rms_norm(round_, xs, dst, next_panel=None):
                def squares(q):
                    act.wait_ge(n_x, xs + q + 1)
                    act.activation(dst[:, q, :], xres[:, q, :], ACT.Square, accum_out=small[:, 3, 4 + q:5 + q]
                                   ).then_inc(r_ss, 1)

                def scale(q):
                    root(q, 4, lambda: act.wait_ge(r_ms, TT * round_ + q + 1), r_sd)
                    act.wait_ge(r_rs, TT * round_ + q + 1)
                    copy(dst[:, q, :], xres[:, q, :], r_h, small[:, 2, 4 + q:5 + q])

                squares(0)
                for q in range(1, TT):
                    if q == TT - 1 and next_panel:
                        split_hi(next_panel, y_done, xs + TT)
                        split_hi(next_panel + 1)
                    squares(q)
                    scale(q - 1)
                scale(TT - 1)

            xt_view = xres[:, :, :].rearrange("p t (a n) -> p (t a) n", a=2)
            act.wait_ge(aux["xT"], 16)
            for k in range(KX):
                copy(xhi[:, k, :], xt_view[:, k, :], xt_hi)
            split_hi(0)
            split_hi(1)
            act.wait_ge(xt_lo, KX)
            act.dma_start(xres[:, :, :], t["x"]).then_inc(aux["x"], 16)
            A, B = bank[0:4], bank[4:8]
            with act.Fori(0, HA) as h:
                n = 6 * h
                act.wait_ge(a_dec, 4 * h + 4)
                act.dma_start(decay[:, :], t["decay"][bass.ds(h, 1), :, :].rearrange("a p n -> (a p) n")
                              ).then_inc(aux["decay"], 16)
                for m in range(4):
                    if m % 2 == 0:
                        split_hi(A0 + 2 + m // 2, a_qk, 4 * h + (m + 2), PAN, n)
                    act.wait_ge(a_q32, 4 * h + (m + 1))
                    copy(qk_hi[:, m, :], work[:, m % 2 * 2, :], a_qkhi)
                split_hi(A0 + 4, half_done, h + 1, PAN, n)
                for q in range(TT):
                    act.wait_ge(a_v, 4 * h + (q + 1))
                    copy(v_hi[:, q, :], A[q][:, :], a_vhi)
                split_hi(A0 + 5, a_v, 4 * h + 4, PAN, n)
                for kt in range(TT):
                    act.wait_ge(a_dec, 4 * h + (kt + 5))
                    copy(s_hi[:, KT_AT[kt]:KT_AT[kt] + SEQ - kt * P], work[:, kt, 0:SEQ - kt * P], a_shi)

                def tanh(m):
                    act.wait_ge(a_g, 4 * h + (m + 1))
                    act.activation(gate[:, m, :], A[m][:, :], ACT.Tanh, scale=0.5).then_inc(a_th, 1)

                tanh(0)
                tanh(1)
                split_hi(A0 + 6, a_g, 4 * h + 2, PAN, n)
                act.wait_ge(a_var, h + 1)
                act.activation(small[:, 1, 0:TT], small[:, 0, 0:TT], ACT.Sqrt).then_inc(a_sd, 1)
                tanh(2)
                tanh(3)
                split_hi(A0 + 7, a_g, 4 * h + 4, PAN, n)
            act.wait_ge(a_ot, 4 * HA + 4)
            act.dma_start(rows[:, :, :], t["ln"][0]).then_inc(aux["rows"], 16)
            project_out(AO, HA * VT, oT, ar_hi, HA, lambda k: None)
            layer_norm(0, B0)
            if last_stage < 2:
                return
            act.wait_ge(n_x, TT)
            act.dma_start(wkr[:, :, :], t["wkr"]).then_inc(aux["kr"], 16)
            act.dma_start(mask_f[:, :], t["mask"]).then_inc(aux["kr"], 16)
            act.dma_start(rope_b[:, :, :], t["rope_b"]).then_inc(aux["ropeb"], 16)
            transposed_x(1)

            act.wait_ge(aux["kr"], 32)
            copy(wkr_hi[:, :, :], wkr[:, :, :], b_w)
            copy(mask_r[:, :], mask_f[:, :], b_w)
            copy(id_r[:, :], ident[:, :], b_w)
            split_hi(B0 + 2, half_done, 11)
            for q in range(TT):
                act.wait_ge(b_c, q + 1)
                act.activation(c_tok[:, q, :], A[q][:, :], ACT.Square, accum_out=small[:, 3, q:q + 1]
                               ).then_inc(b_css, 1)
            act.wait_ge(b_cms, 1)
            act.activation(small[:, 1, 0:TT], small[:, 0, 0:TT], ACT.Sqrt).then_inc(b_csd, 1)
            act.wait_ge(b_crs, 1)
            for q in range(TT):
                copy(c_tok[:, q, :], A[q][:, :], b_ctok, small[:, 2, q:q + 1])
            split_hi(B0 + 3, b_c, TT)
            act.wait_ge(b_kr32, 1)
            copy(kr_hi[:, :], rtmp[:, 0, :], b_krhi)
            for j in range(KC):
                act.wait_ge(b_ct, j + 1)
                copy(c_hi[:, j, :], A[j][:, :], b_chi, cols[:, COL_CG + j:COL_CG + j + 1])
            split_hi(B0 + 4, half_done, 12)
            for q in range(TT):
                act.wait_ge(b_ql, q + 1)
                act.activation(q_tok[:, q, 0:512], B[q][:, :], ACT.Square, accum_out=small[:, 3, 4 + q:5 + q]
                               ).then_inc(b_qss, 1)
            split_hi(M0, b_ql, TT, PANEL)
            for q in range(TT):
                act.wait_ge(b_ql, TT + q + 1)
                act.activation(q_tok[:, q, 512:768], A[q][:, 0:256], ACT.Square, accum_out=small[:, 3, q:q + 1]
                               ).then_inc(b_qss, 1)
            act.wait_ge(b_qms, 1)
            act.activation(small[:, 1, 4:8], small[:, 0, 4:8], ACT.Sqrt).then_inc(b_qsd, 1)
            act.wait_ge(b_qrs, 1)
            for q in range(TT):
                copy(q_tok[:, q, 0:512], B[q][:, :], b_qtok, small[:, 2, 4 + q:5 + q])
                copy(q_tok[:, q, 512:768], A[q][:, 0:256], b_qtok, small[:, 2, 4 + q:5 + q])
            split_hi(M0 + 1, b_ql, 2 * TT)
            for j in range(KQ):
                act.wait_ge(b_qt, j + 1)
                copy(ql_hi[:, j, :], bank[j][:, :], b_qhi, cols[:, COL_QG + j:COL_QG + j + 1])

            with act.Fori(0, PAIRS // 2) as it:
                for s in range(2):
                    n = 6 * it
                    p = M0 + 3 * s

                    def c(per, k):
                        return 2 * per * it + (per * s + k)

                    for m in range(2):
                        act.wait_ge(m_q, c(3, m + 1))
                        copy(qn_hi[:, m, :], bank[4 + m][:, :], m_qhi)
                    split_hi(p + 2, m_q, c(3, 3), PAN, n)
                    act.wait_ge(m_qr32, c(1, 1))
                    copy(qr_hi[:, :], rtmp[:, 0, :], m_qhi)
                    for m in range(2):
                        act.wait_ge(m_kv, c(4, m + 1))
                        copy(kn_hi[:, m, :], bank[m][:, :], m_kvhi)
                    for m in range(2):
                        act.wait_ge(m_kv, c(4, m + 3))
                        copy(vb_hi[:, 2 * m:2 * m + 2, :].rearrange("p t n -> p (t n)"), bank[2 + m][:, :], m_kvhi)
                    split_hi(p + 3, m_kv, c(4, 4), PANEL, n)

                    def exps(e):
                        for q in range(TT):
                            w = (q + 1) * P
                            at = q * (q + 1) // 2 * P
                            act.wait_ge(m_nb, c(8, 4 * e + q + 1))
                            act.activation(prob[:, at:at + w], bank[4 + q][:, 0:w], ACT.Exp, scale=SCALE_B,
                                           bias=sm[:, 1, 4 * e + q:4 * e + q + 1],
                                           accum_out=sm[:, 2, 4 * e + q:4 * e + q + 1]).then_inc(m_exp, 1)

                    def turned(e):
                        for b in range(3):
                            w = (512, 384, 384)[b]
                            act.wait_ge(m_t, c(6, 3 * e + b + 1))
                            copy(pt_hi[:, (0, 512, 896)[b]:(0, 512, 896)[b] + w], bank[1 + e + b][:, 0:w], m_pthi)

                    def tanh(m):
                        act.wait_ge(m_g, c(2, m + 1))
                        act.activation(gt[:, m, :], bank[0][:, :], ACT.Tanh, scale=0.5).then_inc(m_th, 1)

                    def store(e):
                        act.wait_ge(m_og, c(2, e + 3))
                        act.dma_start(t["o_spill"][bass.ds(4 * it + (2 * s + e), 1), :, :].rearrange(
                            "a p n -> (a p) n"), og[:, e, :]).then_inc(m_st[e], 16)

                    exps(0)
                    tanh(0)
                    turned(0)
                    exps(1)
                    turned(1)
                    store(0)
                    tanh(1)
                    split_hi(p + 4, m_g, c(2, 2), PAN, n)
                    store(1)
            for e in range(2):
                act.wait_ge(m_st[e], 16 * PAIRS + 16)
            for c4 in range(4):
                act.dma_start(bT[:, 4 * c4:4 * c4 + 4, :], t["o_spill"][4 * c4:4 * c4 + 4, :, :].rearrange(
                    "k p n -> p k n")).then_inc(bld[c4], 16)
            act.dma_start(rows2[:, :, :], t["ln"][1]).then_inc(aux["rows2"], 16)
            act.dma_start(bias[:, :, :, :], t["bias"]).then_inc(aux["bias"], 16)
            act.dma_start(nmask[:, :, :], t["nmask"]).then_inc(aux["nmask"], 16)
            act.dma_start(wp[:, :, :], t["wp"]).then_inc(aux["wp"], 16)
            act.dma_start(edge[:, :, :], t["edge"]).then_inc(aux["edge"], 16)
            project_out(BO, HB, bT, br_hi, 12, lambda k: act.wait_ge(bld[k // 4], 16))
            layer_norm(1, L0)
            rms_norm(0, TT, h_tok)
            transposed_x(2, COL_MIX)
            if last_stage < 3:
                return

            act.wait_ge(aux["nmask"], 16)
            copy(nmask_r[:, :, :], nmask[:, :, :], l_mk)
            copy(id_n[:, :], ident[:, :], l_mk)
            act.wait_ge(aux["wp"], 16)
            copy(wp_hi[:, :, :], wp[:, :, :], l_w)
            split_hi(L0 + 2, half_done, 19)
            for q in range(TT):
                act.wait_ge(l_v, q + 1)
                copy(v_tok[:, q, :], A[q][:, :], l_vt)
            act.wait_ge(l_vt, TT)
            act.dma_start(t["v_spill"].rearrange("(t p) n -> p t n", p=P), v_tok[:, :, :]).then_inc(vst, 16)
            split_hi(L0 + 3, l_v, TT)
            for m in range(8):
                act.wait_ge(l_q, m + 1)
                if m < 4:
                    copy(by_block(nq_hi[:, m, :]), from_rows(B[m][:, :]), l_qhi)
                else:
                    copy(nk_hi[:, m - 4, :], A[m - 4][:, :], l_qhi)
                if m % 2:
                    split_hi(L0 + 4 + m // 2, l_q, m + 1)
                if m == 1:
                    act.wait_ge(vst, 16)
                    grid = t["v_spill"].rearrange("(r c) n -> r c n", c=GRID)
                    for j in range(NBLK):
                        for half in range(2):
                            for r in range(4):
                                act.dma_start(vband[r * BAND:(r + 1) * BAND, 2 * j + half, :],
                                              grid[4 * half + r, BAND_START[j]:BAND_START[j] + BAND, :]
                                              ).then_inc(vld[2 * j + half], 16)
            for g in range(4):
                act.wait_ge(l_u, g + 1)
                copy(upad[:, g, PAD:PAD + SEQ], B[g][:, :], l_up)
                if g % 2:
                    split_hi(WO + g // 2, l_u, g + 1)
            for b in range(8):
                act.wait_ge(vld[b], 64)
                copy(xhi[:, b, :], vband[:, b, :], l_bhi)
            for g in range(4):
                act.wait_ge(l_pool, g + 1)
                if g:
                    act.wait_ge(l_mix, g)
                copy(pool_hi[:, :], win[:, 0, 0:SEQ], l_phi)
                act.wait_ge(l_mix, g + 1)
                copy(mixT[:, g, :], A[g][:, :], l_mo, cols[:, COL_PS + g:COL_PS + g + 1])

            steps = [(hp, j) for j in range(NBLK) for hp in range(HN // 2)]
            for i in range(len(steps) + 2):
                if i < len(steps):
                    act.wait_ge(e_nb, i + 1)
                    for e in range(2):
                        act.activation(nt[:, i % 2, e, :], nt[:, i % 2, e, :], ACT.Exp, bias=nsm[:, i % 2, 0, e:e + 1],
                                       accum_out=nsm[:, i % 2, 1, e:e + 1]).then_inc(e_exp, 1)
                if 1 <= i <= len(steps):
                    m = i - 1
                    act.wait_ge(e_t, m + 1)
                    if m >= 2:
                        act.wait_ge(e_o, m - 1)
                    copy(npt_hi[:, m % 2, :], bank[4 + m % 2][:, :], e_thi)
                if i >= 2:
                    m = i - 2
                    hp, j = steps[m]
                    act.wait_ge(e_o, m + 1)
                    for e in range(2):
                        f = slice(DHN * e, DHN * e + DHN)
                        dst = mixT[f, 4 + hp, :].rearrange("p (r c) -> p r c", r=ROWS)[:, :, j * BLK:(j + 1) * BLK]
                        copy(dst, bank[6 + m % 2][f, e * P:(e + 1) * P].rearrange("p (r c) -> p r c", r=ROWS), e_oc)
            act.wait_ge(e_oc, 2 * len(steps))
            project_out(WO, KX, mixT, cr_hi, 19, lambda k: None)
            rms_norm(1, 2 * TT, h2_tok, UP)
            transposed_x(3, COL_MLP)
            if last_stage < 4:
                return

            act.dma_start(frow[:, :], t["frow"]).then_inc(aux["frow"], 16)
            with act.Fori(0, 8) as i:
                for m in range(4):
                    act.wait_ge(u_m, 4 * i + (m + 1))
                    act.wait_ge(u_s, 4 * i + (m + 1))
                    act.activation(relu[:, m, :], bank[m][:, :], ACT.Relu).then_inc(u_r, 1)
                    if m % 2:
                        split_hi(UP + 2 + m // 2, u_m, 4 * i + (m + 1), PAN, 2 * i)
            act.wait_ge(u_s, KF + 4)
            project_out(DN, KF, hid, dr_hi, 21, lambda k: None)
            rms_norm(2, 3 * TT, hid[:, 0:2 * TT, :].rearrange("p (t a) n -> p t (a n)", a=2))

        @block.vector
        def _(dve):
            own = Own(dve, dv)

            def lo_of(dst, src, hi, signal):
                dve.tensor_tensor(dst, src, hi.bitcast(F32), ALU.subtract).then_inc(signal, 1)

            def lo_scaled(dst, src, scale, hi, signal):
                dve.scalar_tensor_tensor(out=dst, in0=src, scalar=scale, in1=hi.bitcast(F32), op0=ALU.mult,
                                         op1=ALU.subtract).then_inc(signal, 1)

            def transposed_x(round_, col=None):
                for k in range(KX):
                    dve.wait_ge(xt_hi, KX * round_ + k + 1)
                    if col is None:
                        lo_of(xlo[:, k, :], bank[k][:, :], xhi[:, k, :], xt_lo)
                    else:
                        lo_scaled(xlo[:, k, :], bank[k][:, :], cols[:, col + k:col + k + 1], xhi[:, k, :], xt_lo)

            def project_out(nk, src, hi, lo, a0):
                for kk in range(4):
                    dve.wait_ge(ar_h, a0 + kk + 1)
                    lo_of(lo[:, kk, :], src[:, kk, :], hi[:, kk, :], ar_l)
                with dve.Fori(1, nk // 4) as i:
                    for kk in range(4):
                        dve.wait_ge(ar_h, 4 * i + (a0 + kk + 1))
                        lo_of(lo[:, kk, :], src[:, bass.ds(4 * i + kk, 1), :].rearrange("p a n -> p (a n)"),
                              hi[:, kk, :], ar_l)

            def layer_norm(y0, round_, gb):
                def gather(q):
                    dve.wait_ge(y_done, y0 + q + 1)
                    for c in range(2):
                        w = slice(c * 512, (c + 1) * 512)
                        own.mark(dve.scalar_tensor_tensor(out=xres[:, q, w], in0=xres[:, q, w], scalar=ALPHA,
                                                          in1=bank[2 * q + c][:, :], op0=ALU.mult, op1=ALU.add))
                    own.settle()
                    for c in range(2):
                        own.mark(dve.bn_stats(stat[:, q, c, :], xres[:, q, c * 512:(c + 1) * 512]))
                    own.settle()
                    own.mark(dve.bn_aggr(mv[:, q, :], stat[:, q, :, :]))
                    own.settle()
                    dve.tensor_scalar(small[:, 0, q:q + 1], mv[:, q, 1:2], LN_EPS, None, ALU.add).then_inc(n_var, 1)

                def shift(q):
                    dve.wait_ge(n_sd, TT * round_ + q + 1)
                    own.mark(dve.reciprocal(small[:, 2, q:q + 1], small[:, 1, q:q + 1]))
                    own.settle()
                    dve.scalar_tensor_tensor(out=small[:, 3, q:q + 1], in0=mv[:, q, 0:1], scalar=-1.0,
                                             in1=small[:, 2, q:q + 1], op0=ALU.mult, op1=ALU.mult
                                             ).then_inc(n_rs, 1)

                def affine(q):
                    dve.wait_ge(n_nm, TT * round_ + q + 1)
                    own.mark(dve.tensor_tensor(xres[:, q, :], xres[:, q, :], gb[:, 0, :], ALU.mult))
                    own.settle()
                    dve.tensor_tensor(xres[:, q, :], xres[:, q, :], gb[:, 1, :], ALU.add).then_inc(n_x, 1)

                for q in range(TT + 2):
                    if q < TT:
                        gather(q)
                    if 1 <= q <= TT:
                        shift(q - 1)
                    if q >= 2:
                        affine(q - 2)

            def rms_small(round_, q):
                dve.wait_ge(r_ss, TT * round_ + q + 1)
                dve.tensor_scalar(small[:, 0, 4 + q:5 + q], small[:, 3, 4 + q:5 + q], 1.0 / DM, RMS_EPS, ALU.mult,
                                  ALU.add).then_inc(r_ms, 1)
                dve.wait_ge(r_sd, TT * round_ + q + 1)
                dve.reciprocal(small[:, 2, 4 + q:5 + q], small[:, 1, 4 + q:5 + q]).then_inc(r_rs, 1)

            def add_y(y0, q):
                dve.wait_ge(y_done, y0 + q + 1)
                own.mark(dve.tensor_tensor(xres[:, q, 0:512], xres[:, q, 0:512], bank[2 * q][:, :], ALU.add))
                own.settle()
                dve.tensor_tensor(xres[:, q, 512:DM], xres[:, q, 512:DM], bank[2 * q + 1][:, :], ALU.add
                                  ).then_inc(n_x, 1)

            dve.sem_inc(a_ot, 4)
            dve.sem_inc(a_gt, 4)
            dve.sem_inc(a_dec, 4)
            dve.sem_inc(m_gt, 2)
            dve.sem_inc(m_og, 2)
            dve.sem_inc(m_st[0], 16)
            dve.sem_inc(m_st[1], 16)
            dve.sem_inc(u_s, 4)
            dve.sem_inc(u_r, 4)

            xt_view = xres[:, :, :].rearrange("p t (a n) -> p (t a) n", a=2)
            for k in range(KX):
                dve.wait_ge(xt_hi, k + 1)
                lo_of(xlo[:, k, :], xt_view[:, k, :], xhi[:, k, :], xt_lo)
            A, B = bank[0:4], bank[4:8]
            dve.wait_ge(aux["const"], 48)
            cos, sin = rope_a[:, 0, :], rope_a[:, 1, :]
            with dve.Fori(0, HA) as h:
                own.enter(h, 17)
                for a in range(2):
                    b0, b1 = B[2 * a][:, :], B[2 * a + 1][:, :]
                    dve.wait_ge(a_qk, 4 * h + (2 * a + 2))
                    if a:
                        dve.wait_ge(a_qklo, 4 * h + 2)
                    own.mark(dve.tensor_tensor(work[:, 0, :], b0, cos, ALU.mult))
                    own.mark(dve.tensor_tensor(work[:, 1, :], b1, sin, ALU.mult))
                    own.mark(dve.tensor_tensor(work[:, 2, :], b1, cos, ALU.mult))
                    own.mark(dve.tensor_tensor(work[:, 3, :], b0, sin, ALU.mult))
                    own.settle()
                    dve.tensor_tensor(work[:, 0, :], work[:, 0, :], work[:, 1, :], ALU.subtract).then_inc(a_q32, 1)
                    dve.tensor_tensor(work[:, 2, :], work[:, 2, :], work[:, 3, :], ALU.add).then_inc(a_q32, 1)
                    for m in range(2):
                        dve.wait_ge(a_qkhi, 4 * h + (2 * a + m + 1))
                        lo_of(qk_lo[:, 2 * a + m, :], work[:, 2 * m, :], qk_hi[:, 2 * a + m, :], a_qklo)
                for q in range(TT):
                    dve.wait_ge(a_vhi, 4 * h + (q + 1))
                    lo_of(v_lo[:, q, :], A[q][:, :], v_hi[:, q, :], a_vlo)
                dve.wait_ge(aux["decay"], 16 * h + 16)
                dve.wait_ge(a_qklo, 4 * h + 4)
                for kt in range(TT):
                    w = SEQ - kt * P
                    dve.wait_ge(a_s, 4 * h + (kt + 1))
                    dve.tensor_tensor(work[:, kt, 0:w], B[kt][:, 0:w], decay[:, 0:w], ALU.mult).then_inc(a_dec, 1)
                for kt in range(TT):
                    w = SEQ - kt * P
                    dve.wait_ge(a_shi, 4 * h + (kt + 1))
                    lo_of(s_lo[:, KT_AT[kt]:KT_AT[kt] + w], work[:, kt, 0:w], s_hi[:, KT_AT[kt]:KT_AT[kt] + w], a_slo)

                def gates(m):
                    dve.wait_ge(a_th, 4 * h + (m + 1))
                    dve.scalar_tensor_tensor(out=gate[:, m, :], in0=gate[:, m, :], scalar=1.0, in1=A[m][:, :],
                                             op0=ALU.add, op1=ALU.mult).then_inc(a_gt, 1)

                gates(0)
                gates(1)
                for q in range(TT):
                    dve.wait_ge(a_o, 4 * h + (q + 1))
                    own.mark(dve.bn_stats(stat[:, q, 0, :], B[q][:, :]))
                own.settle()
                dve.memset(small[:, 3, 0:1], 0.0)
                for q in range(TT):
                    own.mark(dve.bn_aggr(mv[:, q, :], stat[:, q, 0, :]))
                own.settle()
                dve.tensor_scalar(small[:, 0, 0:TT], mv[:, :, 1], LN_EPS, 4.0, ALU.add, ALU.mult).then_inc(a_var, 1)
                dve.wait_ge(a_sd, h + 1)
                own.mark(dve.reciprocal(small[:, 2, 0:TT], small[:, 1, 0:TT]))
                own.settle()
                dve.wait_ge(a_slo, 4 * h + 4)
                for q in range(TT):
                    dve.tensor_scalar(work[:, q, :], B[q][:, :], mv[:, q, 0:1], small[:, 2, q:q + 1], ALU.subtract,
                                      ALU.mult).then_inc(a_on, 1)
                gates(2)
                gates(3)
                dve.wait_ge(a_gt, 4 * h + 8)
                for j in range(VT):
                    dve.wait_ge(a_t, 4 * h + (j + 1))
                    dve.tensor_tensor(oT[:, bass.ds(4 * h + j, 1), :].rearrange("p a n -> p (a n)"), B[j][:, :],
                                      gate[:, j, :], ALU.mult).then_inc(a_ot, 1)
            own.leave(HA)
            project_out(HA * VT, oT, ar_hi, ar_lo, 0)
            dve.wait_ge(aux["rows"], 16)
            dve.wait_ge(aux["x"], 16)
            layer_norm(0, 0, rows)

            if last_stage < 2:
                dve.wait_ge(n_x, TT)
                dve.sem_inc(o_ready, TT)
                return
            transposed_x(1)
            dve.wait_ge(b_w, 1)
            lo_of(wkr_lo[:, :, :], wkr[:, :, :], wkr_hi[:, :, :], b_wl)
            dve.wait_ge(b_css, TT)
            dve.tensor_scalar(small[:, 0, 0:TT], small[:, 3, 0:TT], 1.0 / KVLORA, RMS_EPS, ALU.mult, ALU.add
                              ).then_inc(b_cms, 1)
            dve.wait_ge(b_csd, 1)
            dve.reciprocal(small[:, 2, 0:TT], small[:, 1, 0:TT]).then_inc(b_crs, 1)
            dve.wait_ge(aux["ropeb"], 16)

            def rotate(src, signal):
                own.mark(dve.tensor_tensor(rtmp[:, 0, :], src, rope_b[:, 0, :], ALU.mult))
                for g in range(4):
                    a, b = 32 * g, 32 * (g ^ 1)
                    own.mark(dve.tensor_tensor(rtmp[b:b + 32, 1, :], src[a:a + 32, :], rope_b[a:a + 32, 1, :],
                                               ALU.mult))
                own.settle()
                dve.tensor_tensor(rtmp[:, 0, :], rtmp[:, 0, :], rtmp[:, 1, :], ALU.add).then_inc(signal, 1)

            dve.wait_ge(b_kr, 1)
            rotate(bank[7][:, :], b_kr32)
            dve.wait_ge(b_krhi, 1)
            lo_of(kr_lo[:, :], rtmp[:, 0, :], kr_hi[:, :], b_krlo)
            for j in range(KC):
                dve.wait_ge(b_chi, j + 1)
                lo_scaled(c_lo[:, j, :], A[j][:, :], cols[:, COL_CG + j:COL_CG + j + 1], c_hi[:, j, :], b_clo)
            dve.wait_ge(b_qss, 2 * TT)
            own.mark(dve.tensor_tensor(small[:, 0, 4:8], small[:, 3, 4:8], small[:, 3, 0:4], ALU.add))
            own.settle()
            dve.tensor_scalar(small[:, 0, 4:8], small[:, 0, 4:8], 1.0 / QLORA, RMS_EPS, ALU.mult, ALU.add
                              ).then_inc(b_qms, 1)
            dve.wait_ge(b_qsd, 1)
            dve.reciprocal(small[:, 2, 4:8], small[:, 1, 4:8]).then_inc(b_qrs, 1)
            for j in range(KQ):
                dve.wait_ge(b_qhi, j + 1)
                lo_scaled(ql_lo[:, j, :], bank[j][:, :], cols[:, COL_QG + j:COL_QG + j + 1], ql_hi[:, j, :], b_qlo)

            with dve.Fori(0, PAIRS // 2) as it:
                own.enter(it, 2 * 21)
                for s in range(2):
                    def c(per, k):
                        return 2 * per * it + (per * s + k)

                    for m in range(2):
                        dve.wait_ge(m_qhi, c(3, m + 1))
                        lo_of(qn_lo[:, m, :], bank[4 + m][:, :], qn_hi[:, m, :], m_qlo)
                    dve.wait_ge(m_q, c(3, 3))
                    rotate(bank[6][:, :], m_qr32)
                    dve.wait_ge(m_qhi, c(3, 3))
                    lo_of(qr_lo[:, :], rtmp[:, 0, :], qr_hi[:, :], m_qlo)
                    for m in range(2):
                        dve.wait_ge(m_kvhi, c(4, m + 1))
                        lo_of(kn_lo[:, m, :], bank[m][:, :], kn_hi[:, m, :], m_kvlo)
                    for m in range(2):
                        dve.wait_ge(m_kvhi, c(4, m + 3))
                        lo_of(vb_lo[:, 2 * m:2 * m + 2, :].rearrange("p t n -> p (t n)"), bank[2 + m][:, :],
                              vb_hi[:, 2 * m:2 * m + 2, :].rearrange("p t n -> p (t n)"), m_kvlo)

                    def softmax(e):
                        for q in range(TT):
                            x = 4 * e + q
                            dve.wait_ge(m_s, c(8, x + 1))
                            own.mark(dve.tensor_reduce(sm[:, 0, x:x + 1], bank[4 + q][:, 0:(q + 1) * P], AX, ALU.max))
                            own.settle()
                            dve.tensor_scalar(sm[:, 1, x:x + 1], sm[:, 0, x:x + 1], -SCALE_B, None, ALU.mult
                                              ).then_inc(m_nb, 1)
                        for q in range(TT):
                            x = 4 * e + q
                            at, w = q * (q + 1) // 2 * P, (q + 1) * P
                            dve.wait_ge(m_exp, c(8, x + 1))
                            own.mark(dve.reciprocal(sm[:, 3, x:x + 1], sm[:, 2, x:x + 1]))
                            own.settle()
                            dve.tensor_scalar(prob[:, at:at + w], prob[:, at:at + w], sm[:, 3, x:x + 1], 0.5,
                                              ALU.mult, ALU.mult).then_inc(m_p, 1)

                    def turned(e):
                        for b in range(3):
                            r = slice((0, 512, 896)[b], (512, 896, 1280)[b])
                            dve.wait_ge(m_pthi, c(6, 3 * e + b + 1))
                            lo_of(pt_lo[:, r], bank[1 + e + b][:, 0:r.stop - r.start], pt_hi[:, r], m_ptlo)

                    def gates(m):
                        dve.wait_ge(m_th, c(2, m + 1))
                        dve.scalar_tensor_tensor(out=gt[:, m, :], in0=gt[:, m, :], scalar=1.0, in1=bank[0][:, :],
                                                 op0=ALU.add, op1=ALU.mult).then_inc(m_gt, 1)

                    def gated(e, src):
                        dve.wait_ge(m_o, c(2, e + 1))
                        dve.wait_ge(m_gt, c(2, e + 3))
                        dve.wait_ge(m_st[e], 32 * it + (16 * s + 16))
                        dve.tensor_tensor(og[:, e, :], src[:, :], gt[:, e, :], ALU.mult).then_inc(m_og, 1)

                    softmax(0)
                    turned(0)
                    gates(0)
                    softmax(1)
                    gated(0, bank[1])
                    turned(1)
                    gates(1)
                    gated(1, bank[7])
            own.leave(PAIRS // 2)
            project_out(HB, bT, br_hi, br_lo, HA * VT)
            dve.wait_ge(aux["rows2"], 16)
            layer_norm(TT, 1, rows2)
            if last_stage < 3:
                dve.wait_ge(n_x, 2 * TT)
                dve.sem_inc(o_ready, TT)
            for q in range(TT):
                rms_small(0, q)
            transposed_x(2, COL_MIX)
            if last_stage < 3:
                return

            dve.wait_ge(l_w, 1)
            lo_of(wp_lo[:, :, :], wp[:, :, :], wp_hi[:, :, :], l_wl)
            dve.wait_ge(vst, 16)
            own.mark(dve.memset(upad[:, :, 0:PAD], 0.0))
            own.mark(dve.memset(upad[:, :, PAD + SEQ:], 0.0))
            for m in range(8):
                dve.wait_ge(l_qhi, m + 1)
                if m < 4:
                    lo_of(by_block(nq_lo[:, m, :]), from_rows(B[m][:, :]), by_block(nq_hi[:, m, :]), l_qlo)
                else:
                    lo_of(nk_lo[:, m - 4, :], A[m - 4][:, :], nk_hi[:, m - 4, :], l_qlo)
            own.settle()
            dve.wait_ge(aux["edge"], 16)

            def pooled(g):
                dve.wait_ge(l_up, g + 1)
                if g:
                    dve.wait_ge(l_plo, g)
                src, lo, hi = upad[:, g, :], 0, SEQ + 2 * PAD
                for level in range(g + 1):
                    dst = win[:, (g + 1 + level) % 2, :]
                    back = 1 if level == 0 else 2 ** (level - 1)
                    ahead = 0 if level == 0 else back
                    lo, hi = lo + back, hi - ahead
                    own.mark(dve.tensor_tensor(dst[:, lo:hi], src[:, lo - back:hi - back],
                                               src[:, lo + ahead:hi + ahead], ALU.add))
                    own.settle()
                    src = dst
                u = upad[:, g, PAD:PAD + SEQ]
                out_ = win[:, 0, 0:SEQ]
                own.mark(dve.tensor_tensor(src[:, PAD:2 * PAD], src[:, PAD:2 * PAD], edge[:, g, 0:PAD], ALU.mult))
                own.mark(dve.tensor_tensor(src[:, SEQ:SEQ + PAD], src[:, SEQ:SEQ + PAD], edge[:, g, PAD:], ALU.mult))
                own.settle()
                dve.scalar_tensor_tensor(out=out_, in0=src[:, PAD:PAD + SEQ], scalar=1.0 / WINDOWS[g], in1=u,
                                         op0=ALU.mult, op1=ALU.subtract).then_inc(l_pool, 1)
                dve.wait_ge(l_phi, g + 1)
                lo_of(pool_lo[:, :], out_, pool_hi[:, :], l_plo)

            for b in range(8):
                if b % 2 == 0 and False:
                    pass
                dve.wait_ge(l_bhi, b + 1)
                lo_of(xlo[:, b, :], vband[:, b, :], xhi[:, b, :], l_blo)
            for g in range(4):
                pooled(g)

            dve.wait_ge(aux["bias"], 16)
            dve.wait_ge(l_mix, 4)
            steps = [(hp, j) for j in range(NBLK) for hp in range(HN // 2)]
            for i in range(len(steps) + 2):
                if i < len(steps):
                    hp, j = steps[i]
                    at = BAND_START[j] - BLK * j + 16
                    dve.wait_ge(e_s, i + 1)
                    if i >= 2:
                        dve.wait_ge(e_t, i - 1)
                    for e in range(2):
                        own.mark(dve.scalar_tensor_tensor(
                            out=nt[:, i % 2, e, :].rearrange("p (r c) -> p r c", r=ROWS),
                            in0=bank[2 * (i % 2) + e][:, 0:256].rearrange("p (r c) -> p r c", r=ROWS),
                            scalar=SCALE_N, in1=bias[:, 2 * hp + e, :, at:at + BAND], op0=ALU.mult, op1=ALU.add))
                    own.settle()
                    dve.tensor_reduce(nsm[:, i % 2, 0, :], nt[:, i % 2, :, :], AX, ALU.max, negate=True
                                      ).then_inc(e_nb, 1)
                if 1 <= i <= len(steps):
                    m = i - 1
                    dve.wait_ge(e_exp, 2 * m + 2)
                    own.mark(dve.reciprocal(nsm[:, m % 2, 2, :], nsm[:, m % 2, 1, :]))
                    own.settle()
                    for e in range(2):
                        last = dve.tensor_scalar(nt[:, m % 2, e, :], nt[:, m % 2, e, :], nsm[:, m % 2, 2, e:e + 1],
                                                 None, ALU.mult)
                        if e == 0:
                            own.mark(last)
                            own.settle()
                    last.then_inc(e_p, 1)
                if i >= 2:
                    m = i - 2
                    dve.wait_ge(e_thi, m + 1)
                    lo_of(npt_lo[:, m % 2, :], bank[4 + m % 2][:, :], npt_hi[:, m % 2, :], e_tlo)
            project_out(KX, mixT, cr_hi, cr_lo, HA * VT + HB)
            for q in range(TT):
                add_y(2 * TT, q)
                if q:
                    rms_small(1, q - 1)
            rms_small(1, TT - 1)
            if last_stage < 4:
                dve.wait_ge(n_x, 3 * TT)
                dve.sem_inc(o_ready, TT)
            transposed_x(3, COL_MLP)
            if last_stage < 4:
                return

            with dve.Fori(0, 8) as i:
                for m in range(4):
                    dve.wait_ge(u_r, 4 * i + (m + 5))
                    dve.tensor_tensor(hid[:, bass.ds(4 * i + m, 1), :].rearrange("p a n -> p (a n)"), relu[:, m, :],
                                      relu[:, m, :], ALU.mult).then_inc(u_s, 1)
            project_out(KF, hid, dr_hi, dr_lo, HA * VT + HB + KX)
            dve.wait_ge(aux["frow"], 16)
            for q in range(TT):
                add_y(3 * TT, q)
                if q:
                    rms_small(2, q - 1)
            rms_small(2, TT - 1)
            final = hid[:, 0:2 * TT, :].rearrange("p (t a) n -> p t (a n)", a=2)
            for q in range(TT):
                dve.wait_ge(r_h, 2 * TT + q + 1)
                dve.tensor_tensor(xres[:, q, :], final[:, q, :], frow[:, :], ALU.mult).then_inc(o_ready, 1)


def panels(w, nk, width):
    k, n = w.shape
    x = w.reshape(k // (nk * P), nk, P, n // width, width).transpose(3, 0, 2, 1, 4)
    return x.reshape(-1, P, nk * width)


def kernel(**inputs):
    import concourse.bacc as bacc
    from concourse.bass_utils import run_bass_kernel_spmd

    f = {k: np.asarray(v) for k, v in inputs.items()}
    a_in, b_in, n_in = f["a_w_in"][0], f["b_w_in"][0], f["w_in_2"][0]
    groups = []
    for h in range(HA):
        q, k = a_in[:, h * DKA:(h + 1) * DKA], a_in[:, (HA + h) * DKA:(HA + h + 1) * DKA]
        v = a_in[:, 2 * HA * DKA + h * DVA:2 * HA * DKA + (h + 1) * DVA]
        g = a_in[:, 2 * HA * DKA + HA * DVA + h * DVA:2 * HA * DKA + HA * DVA + (h + 1) * DVA]
        groups += [panels(q, KX, 256), panels(k, KX, 256), panels(v, 4, 512), panels(g, KX, 256)]
    groups += [panels(f["a_w_out"][0], 2, DM)]
    groups += [panels(f["kv_w_down"][:, :KVLORA], 4, 512), panels(b_in[:, :512], 4, 512),
               panels(b_in[:, 512:QLORA], KX, 256)]
    uq = f["b_w_uq"][0].reshape(QLORA, HB, NOPE + ROPE)
    up = f["kv_w_up"].reshape(KVLORA, HB, NOPE + VH)
    for n in range(PAIRS):
        a, b = 2 * n, 2 * n + 1
        groups += [panels(np.concatenate([uq[:, a, :NOPE], uq[:, b, :NOPE], uq[:, a, NOPE:], uq[:, b, NOPE:]], 1),
                          KQ, 384),
                   panels(np.concatenate([up[:, a, :NOPE], up[:, b, :NOPE], up[:, a, NOPE:], up[:, b, NOPE:]], 1),
                          KC, 512),
                   panels(b_in[:, QLORA + n * 256:QLORA + (n + 1) * 256], KX, 256)]
    groups += [panels(f["b_w_out"][0], 2, DM)]
    groups += [panels(n_in[:, 1536:2048], 4, 512), panels(n_in[:, 512:1536], KX, 256), panels(n_in[:, :512], KX, 256)]
    groups += [panels(f["w_out_2"][0], 2, DM), panels(f["w_up_2"][0], KX, 256), panels(f["w_down_2"][0], 2, DM)]
    w = np.zeros((PANELS, P, PANEL), np.float32)
    at = 0
    for g in groups:
        w[at:at + len(g), :, :g.shape[2]] = g
        at += len(g)
    assert at == PANELS

    def column(v):
        return v.reshape(-1, P).T

    x = f["x"].reshape(SEQ, DM)
    a = {"w": w, "x": x.reshape(TT, P, DM).transpose(1, 0, 2), "xT": x.T.reshape(KX, P, SEQ).transpose(1, 0, 2)}
    a["cols"] = np.concatenate([column(f["kv_norm"]), column(f["b_q_norm"][0]), column(f["norm_mix_g_2"][0]),
                                column(f["norm_mlp_g_2"][0]), column(f["pool_scale_2"][0])], 1)
    a["ln"] = np.broadcast_to(np.stack([f["ln_g"], f["ln_b"]], 1)[:, None], (2, P, 2, DM))
    a["frow"] = np.broadcast_to(f["final_g_2"], (P, DM))
    kr = f["kv_w_down"][:, KVLORA:]
    a["wkr"] = np.concatenate([kr, kr], 1).reshape(KX, P, P).transpose(1, 0, 2)
    a["wp"] = f["w_pool_2"][0].transpose(1, 0, 2)
    rpb = np.pad(f["rpb_2"][0], ((0, 0), (0, 0), (16, 16)))
    strip = np.zeros((ROWS, BLK, HN, ROWS, BIAS_W), np.float32)
    for r in range(ROWS):
        for c in range(BLK):
            strip[r, c] = rpb[:, 7 - r:7 - r + ROWS, 15 - c:15 - c + BIAS_W]
    a["bias"] = strip.reshape(P, HN, ROWS, BIAS_W)

    def angles(half):
        inv = np.float32(10000.0) ** (-np.arange(half, dtype=np.float32) / np.float32(half))
        return (inv[:, None] * np.arange(SEQ, dtype=np.float32)[None, :]).astype(np.float64)

    ang = angles(DKA // 2)
    a["rope_a"] = np.stack([np.cos(ang), np.sin(ang)], 1)
    ang = np.tile(angles(ROPE // 2), (4, 1))
    sign = np.where(np.arange(P) % ROPE < ROPE // 2, 1.0, -1.0)[:, None]
    a["rope_b"] = np.stack([np.cos(ang), np.sin(ang) * sign], 1)
    dist = np.arange(SEQ)[None, :] - np.arange(P)[:, None]
    log_gamma = np.log1p(-np.exp2(-5.0 - np.arange(HA)))
    a["decay"] = np.where(dist >= 0, np.exp(np.maximum(dist, 0)[None] * log_gamma[:, None, None]), 0.0) * DKA ** -0.5
    a["ident"] = np.eye(P)
    a["mask"] = np.where(np.arange(P)[None, :] > np.arange(P)[:, None], MASKED, 0.0)
    q = np.arange(P) % BLK
    nmask = np.zeros((P, NBLK, BAND))
    for j in range(NBLK):
        c0 = np.clip(j * BLK + q - 8, 0, GRID - BLK)[:, None]
        key = BAND_START[j] + np.arange(BAND)[None, :]
        nmask[:, j] = np.where((key >= c0) & (key < c0 + BLK), 0.0, MASKED)
    a["nmask"] = nmask
    tok = np.arange(SEQ)
    edge = np.zeros((4, 2 * PAD))
    for g, wd in enumerate(WINDOWS):
        count = np.clip(tok - wd // 2 + wd, 0, SEQ) - np.clip(tok - wd // 2, 0, SEQ)
        ratio = wd / count
        edge[g] = np.concatenate([ratio[:PAD], ratio[-PAD:]])
    a["edge"] = np.broadcast_to(edge, (P, 4, 2 * PAD))

    nc = bacc.Bacc("TRN2", target_bir_lowering=False, num_devices=1)
    arrays, t = {}, {}
    for name, v in a.items():
        v = np.ascontiguousarray(v, dtype=np.float32)
        arrays[f"in_{name}"] = v
        t[name] = nc.dram_tensor(f"in_{name}", v.shape, F32, kind="ExternalInput").ap()
    t["o_spill"] = nc.dram_tensor("o_spill", (HB, P, SEQ), F32).ap()
    t["v_spill"] = nc.dram_tensor("v_spill", (SEQ, SEQ), F32).ap()
    out = nc.dram_tensor("out_0", (SEQ, DM), F32, kind="ExternalOutput").ap()
    program(nc, t, out, 99)
    r = run_bass_kernel_spmd(nc, [arrays], core_ids=[0])
    return r.results[0]["out_0"].reshape(1, SEQ, DM)
```

```python
from contextlib import ExitStack

import numpy as np

import concourse.bass as bass
from concourse import mybir

F32 = mybir.dt.float32
F32R = mybir.dt.float32r
ALU = mybir.AluOpType
ACT = mybir.ActivationFunctionType
AX = mybir.AxisListType.X

P = 128
SEQ = 512
DM = 1024
TT = SEQ // P
KX = DM // P
ALPHA = 4.0 ** 0.25
LN_EPS = 1e-5
RMS_EPS = 1e-6
MASKED = -1e30

HA, DKA, DVA = 4, 256, 512
VT = DVA // P
HB, NOPE, ROPE, VH = 16, 128, 64, 128
QLORA, KVLORA = 768, 512
KQ, KC = QLORA // P, KVLORA // P
PAIRS = HB // 2
SCALE_B = float(NOPE + ROPE) ** -0.5
WINDOWS = (2, 4, 8, 16)
HN, DHN = 8, 64
GRID = 64
ROWS = SEQ // GRID
BLK = 16
BAND = 32
NBLK = GRID // BLK
SCALE_N = float(DHN) ** -0.5
BAND_START = [min(max(j * BLK - 8, 0), GRID - BAND) for j in range(NBLK)]
BIAS_W = BAND + 16
DFF = 4 * DM
KF = DFF // P
PAD = 8

PANEL = 2304
PAN = 2048
A0 = 0
AO = A0 + 6 * HA
B0 = AO + 8
M0 = B0 + 5
BO = M0 + 3 * PAIRS
L0 = BO + 8
WO = L0 + 8
UP = WO + 4
DN = UP + 16
PANELS = DN + 16

COL_CG, COL_QG, COL_PS = 0, KC, KC + KQ
COLS = COL_PS + 4

KT_AT = [0, 512, 896, 1152]
TRI = 1280


class Own:

    def __init__(self, eng, sem):
        self.eng, self.sem, self.n, self.i, self.per = eng, sem, 0, 0, 0

    def mark(self, ins):
        ins.then_inc(self.sem, 1)
        self.n += 1

    def settle(self):
        self.eng.wait_ge(self.sem, self.i * self.per + self.n)

    def enter(self, i, per):
        self.i, self.per, self.first = i, per, self.n

    def leave(self, times):
        assert self.n - self.first == self.per, (self.n - self.first, self.per)
        self.n, self.i, self.per = self.first + self.per * times, 0, 0


def program(nc, t, out):
    with ExitStack() as ctx:
        def sb(name, shape, dt=F32, where=ctx):
            return where.enter_context(nc.sbuf_tensor(name, shape, dt))

        def sem(name):
            return ctx.enter_context(nc.semaphore(name))

        bank = [ctx.enter_context(nc.psum_tensor(f"bank{i}", [P, 512], F32)) for i in range(8)]

        stage = [sb(f"stage{i}", [P, PANEL]) for i in range(2)]
        whi = [sb(f"whi{i}", [P, PANEL], F32R) for i in range(2)]
        wlo = [sb(f"wlo{i}", [P, PANEL], F32R) for i in range(2)]
        xhi = sb("xhi", [P, KX, SEQ], F32R)
        xlo = sb("xlo", [P, KX, SEQ], F32R)
        xres = sb("xres", [P, TT, DM])
        grow = sb("grow", [P, DM])
        ident = sb("ident", [P, P])
        cols = sb("cols", [P, COLS])
        stat = sb("stat", [P, TT, 2, 6])
        mv = sb("mv", [P, TT, 2])
        small = sb("small", [P, 4, 8])
        eps = sb("eps", [P, 2])
        mark = ctx.enter_context(ExitStack())

        oT = sb("oT", [P, HA * VT, SEQ], F32, mark)
        with ExitStack() as h:
            qk_hi = sb("qk_hi", [P, 4, SEQ], F32R, h)
            qk_lo = sb("qk_lo", [P, 4, SEQ], F32R, h)
            v_hi = sb("v_hi", [P, TT, DVA], F32R, h)
            v_lo = sb("v_lo", [P, TT, DVA], F32R, h)
            gate = sb("gate", [P, VT, SEQ], F32, h)
            s_hi = sb("s_hi", [P, TRI], F32R, h)
            s_lo = sb("s_lo", [P, TRI], F32R, h)
            decay = sb("decay", [P, SEQ], F32, h)
            rope_a = sb("rope_a", [P, 2, SEQ], F32, h)
            work = sb("work", [P, 4, SEQ], F32, h)
        with ExitStack() as h:
            ar_hi = sb("ar_hi", [P, 4, SEQ], F32R, h)
            ar_lo = sb("ar_lo", [P, 4, SEQ], F32R, h)
            rows = sb("rows", [P, 2, DM], F32, h)
        mark.close()
        with ExitStack() as h:
            c_hi = sb("c_hi", [P, KC, SEQ], F32R, h)
            c_lo = sb("c_lo", [P, KC, SEQ], F32R, h)
            ql_hi = sb("ql_hi", [P, KQ, SEQ], F32R, h)
            ql_lo = sb("ql_lo", [P, KQ, SEQ], F32R, h)
            kr_hi = sb("kr_hi", [P, SEQ], F32R, h)
            kr_lo = sb("kr_lo", [P, SEQ], F32R, h)
            rope_b = sb("rope_b", [P, 2, SEQ], F32, h)
            id_r = sb("id_r", [P, P], F32R, h)
            mask_r = sb("mask_r", [P, P], F32R, h)
            rtmp = sb("rtmp", [P, 2, SEQ], F32, h)
            with ExitStack() as g:
                c_tok = sb("c_tok", [P, TT, KVLORA], F32, g)
                q_tok = sb("q_tok", [P, TT, QLORA], F32, g)
                wkr = sb("wkr", [P, KX, P], F32, g)
                wkr_hi = sb("wkr_hi", [P, KX, P], F32R, g)
                wkr_lo = sb("wkr_lo", [P, KX, P], F32R, g)
                mask_f = sb("mask_f", [P, P], F32, g)
            with ExitStack() as g:
                qn_hi = sb("qn_hi", [P, 2, SEQ], F32R, g)
                qn_lo = sb("qn_lo", [P, 2, SEQ], F32R, g)
                qr_hi = sb("qr_hi", [P, SEQ], F32R, g)
                qr_lo = sb("qr_lo", [P, SEQ], F32R, g)
                kn_hi = sb("kn_hi", [P, 2, SEQ], F32R, g)
                kn_lo = sb("kn_lo", [P, 2, SEQ], F32R, g)
                vb_hi = sb("vb_hi", [P, TT, 2 * VH], F32R, g)
                vb_lo = sb("vb_lo", [P, TT, 2 * VH], F32R, g)
                gt = sb("gt", [P, 2, SEQ], F32, g)
                prob = sb("prob", [P, TRI], F32, g)
                pt_hi = sb("pt_hi", [P, TRI], F32R, g)
                pt_lo = sb("pt_lo", [P, TRI], F32R, g)
                sm = sb("sm", [P, 4, 8], F32, g)
        with ExitStack() as h:
            bT = sb("bT", [P, HB, SEQ], F32, h)
            br_hi = sb("br_hi", [P, 4, SEQ], F32R, h)
            br_lo = sb("br_lo", [P, 4, SEQ], F32R, h)
            rows2 = sb("rows2", [P, 2, DM], F32, h)
        with ExitStack() as h:
            mixT = sb("mixT", [P, KX, SEQ], F32, h)
            with ExitStack() as f:
                h_tok = sb("h_tok", [P, TT, DM], F32, f)
                vband = h_tok[:, :, :].rearrange("p t (a n) -> p (t a) n", a=2)
                nq_hi = sb("nq_hi", [P, 4, SEQ], F32R, f)
                nq_lo = sb("nq_lo", [P, 4, SEQ], F32R, f)
                nk_hi = sb("nk_hi", [P, 4, SEQ], F32R, f)
                nk_lo = sb("nk_lo", [P, 4, SEQ], F32R, f)
                bias = sb("bias", [P, HN, ROWS, BIAS_W], F32, f)
                nmask = sb("nmask", [P, NBLK, BAND], F32, f)
                nmask_r = sb("nmask_r", [P, NBLK, BAND], F32R, f)
                id_n = sb("id_n", [P, P], F32R, f)
                nsm = sb("nsm", [P, 3, 3, 2], F32, f)
                with ExitStack() as g:
                    v_tok = sb("v_tok", [P, TT, SEQ], F32, g)
                with ExitStack() as g:
                    upad = sb("upad", [P, 4, SEQ + 2 * PAD], F32, g)
                    win = sb("win", [P, 2, SEQ + 2 * PAD], F32, g)
                    pool_hi = sb("pool_hi", [P, SEQ], F32R, g)
                    pool_lo = sb("pool_lo", [P, SEQ], F32R, g)
                    wp = sb("wp", [P, 4, P], F32, g)
                    wp_hi = sb("wp_hi", [P, 4, P], F32R, g)
                    wp_lo = sb("wp_lo", [P, 4, P], F32R, g)
                    edge = sb("edge", [P, 4, 2 * PAD], F32, g)
                with ExitStack() as g:
                    nt = sb("nt", [P, 3, 2, 256], F32, g)
                    npt_hi = sb("npt_hi", [P, 2, SEQ], F32R, g)
                    npt_lo = sb("npt_lo", [P, 2, SEQ], F32R, g)
            with ExitStack() as f:
                h2_tok = sb("h2_tok", [P, TT, DM], F32, f)
                cr_hi = sb("cr_hi", [P, 4, SEQ], F32R, f)
                cr_lo = sb("cr_lo", [P, 4, SEQ], F32R, f)
        with ExitStack() as h:
            hid = sb("hid", [P, KF, SEQ], F32, h)
            relu = sb("relu", [P, 4, SEQ], F32, h)
            dr_hi = sb("dr_hi", [P, 4, SEQ], F32R, h)
            dr_lo = sb("dr_lo", [P, 4, SEQ], F32R, h)

        landed = [sem(f"landed{i}") for i in range(2)]
        w_hi = sem("w_hi")
        w_lo = sem("w_lo")
        half_done = sem("half_done")
        aux = {n: sem(f"ld_{n}") for n in ("x", "const", "decay", "kr", "rows", "rows2", "ropeb", "bias",
                                           "edge", "wp", "nmask", "grow")}
        xt_ld = [sem(f"xt_ld{k}") for k in range(KX)]
        vst = sem("vst")
        vld = [sem(f"vld{i}") for i in range(8)]
        bld = [sem(f"bld{i}") for i in range(4)]
        dv = sem("dve_step")
        ac = sem("act_step")
        xt_t, xt_hi, xt_lo = sem("xt_t"), sem("xt_hi"), sem("xt_lo")
        a_qk, a_q32, a_qkhi, a_qklo = sem("a_qk"), sem("a_q32"), sem("a_qkhi"), sem("a_qklo")
        a_v, a_vhi, a_vlo = sem("a_v"), sem("a_vhi"), sem("a_vlo")
        a_s, a_dec, a_shi, a_slo = sem("a_s"), sem("a_dec"), sem("a_shi"), sem("a_slo")
        a_g, a_th, a_gt = sem("a_g"), sem("a_th"), sem("a_gt")
        a_o, a_var, a_sd, a_on, a_t, a_ot = (sem("a_o"), sem("a_var"), sem("a_sd"), sem("a_on"), sem("a_t"),
                                             sem("a_ot"))
        y_done = sem("y_done")
        ar_h, ar_l = sem("ar_h"), sem("ar_l")
        n_mu, n_ss, n_sd, n_x = sem("n_mu"), sem("n_ss"), sem("n_sd"), sem("n_x")
        r_ss, r_sd, r_h = sem("r_ss"), sem("r_sd"), sem("r_h")
        b_c, b_ql, b_kr, b_ct, b_qt = sem("b_c"), sem("b_ql"), sem("b_kr"), sem("b_ct"), sem("b_qt")
        b_css, b_cms, b_csd, b_crs, b_ctok = sem("b_css"), sem("b_cms"), sem("b_csd"), sem("b_crs"), sem("b_ctok")
        b_qss, b_qms, b_qsd, b_qrs, b_qtok = sem("b_qss"), sem("b_qms"), sem("b_qsd"), sem("b_qrs"), sem("b_qtok")
        b_qtl = sem("b_qtl")
        b_chi, b_clo, b_qhi, b_qlo = sem("b_chi"), sem("b_clo"), sem("b_qhi"), sem("b_qlo")
        b_kr32, b_krhi, b_krlo, b_w, b_wl = sem("b_kr32"), sem("b_krhi"), sem("b_krlo"), sem("b_w"), sem("b_wl")
        m_q, m_kv, m_s, m_g, m_t, m_o = (sem("m_q"), sem("m_kv"), sem("m_s"), sem("m_g"), sem("m_t"), sem("m_o"))
        m_qr32, m_qhi, m_qlo, m_kvhi, m_kvlo = (sem("m_qr32"), sem("m_qhi"), sem("m_qlo"), sem("m_kvhi"),
                                                sem("m_kvlo"))
        m_nb, m_exp, m_p, m_th, m_gt, m_pthi, m_ptlo, m_og = (
            sem("m_nb"), sem("m_exp"), sem("m_p"), sem("m_th"), sem("m_gt"), sem("m_pthi"), sem("m_ptlo"),
            sem("m_og"))
        m_st = [sem("m_st0"), sem("m_st1")]
        l_v, l_vt, l_q, l_qhi, l_qlo, l_u, l_up = (sem("l_v"), sem("l_vt"), sem("l_q"), sem("l_qhi"), sem("l_qlo"),
                                                   sem("l_u"), sem("l_up"))
        l_pool, l_phi, l_plo, l_mix, l_mo, l_w, l_wl = (sem("l_pool"), sem("l_phi"), sem("l_plo"), sem("l_mix"),
                                                        sem("l_mo"), sem("l_w"), sem("l_wl"))
        l_bhi, l_blo, l_blo1, l_mk = sem("l_bhi"), sem("l_blo"), sem("l_blo1"), sem("l_mk")
        steps = [(hp, j) for j in range(NBLK) for hp in range(HN // 2)]
        e_s, e_tk, e_nb, e_exp, e_rc, e_p, e_q, e_t, e_thi, e_tlo, e_o, e_oc = (
            sem("e_s"), sem("e_tk"), sem("e_nb"), sem("e_exp"), sem("e_rc"), sem("e_p"), sem("e_q"), sem("e_t"), sem("e_thi"), sem("e_tlo"), sem("e_o"),
            sem("e_oc"))
        u_m, u_r, u_s = sem("u_m"), sem("u_r"), sem("u_s")
        o_st = sem("o_st")

        def by_block(x):
            return x.rearrange("p (j r c) -> p j r c", j=NBLK, r=ROWS)

        def from_rows(x):
            return x.rearrange("p (r j c) -> p j r c", j=NBLK, r=ROWS)

        def split_dots(pe, dst, a_hi, a_lo, b_hi, b_lo, start, stop):
            pe.matmul(dst, a_hi, b_hi, start=start, stop=False)
            pe.matmul(dst, a_hi, b_lo, start=False, stop=False)
            return pe.matmul(dst, a_lo, b_hi, start=False, stop=stop)

        block = ctx.enter_context(nc.Block())

        @block.sync
        def _(sp):
            def load(p, width=PAN, n=0):
                if p >= 2:
                    sp.wait_ge(w_lo, n + (p - 1))
                sp.dma_start(stage[p % 2][:, 0:width],
                             t["w"][bass.ds(n + p, 1), :, 0:width].rearrange("a p n -> (a p) n")
                             ).then_inc(landed[p % 2], 16)

            xt_view = xres[:, :, :].rearrange("p t (a n) -> p (t a) n", a=2)
            load(0)
            for k in range(KX):
                sp.dma_start(xt_view[:, k, :], t["xT"][:, k, :]).then_inc(xt_ld[k], 16)
            load(1)
            sp.dma_start(rope_a[:, :, :], t["rope_a"]).then_inc(aux["const"], 16)
            sp.dma_start(ident[:, :], t["ident"]).then_inc(aux["const"], 16)
            sp.dma_start(cols[:, :], t["cols"]).then_inc(aux["const"], 16)
            sp.dma_start(grow[:, :], t["grow"][0]).then_inc(aux["grow"], 16)
            with sp.Fori(0, 17) as i:
                for j in range(2):
                    load(2 + j, PAN, 2 * i)
            load(36)
            with sp.Fori(0, PAIRS // 2) as i:
                for j in range(6):
                    load(M0 + j, PANEL if j % 3 == 0 else PAN, 6 * i)
            load(BO)
            sp.wait_ge(m_kv, 4 * PAIRS)
            for e in range(2):
                sp.wait_ge(m_st[e], 16 * (PAIRS - 2) + 16)
            for c4 in range(3):
                sp.dma_start(bT[:, 4 * c4:4 * c4 + 4, :], t["o_spill"][4 * c4:4 * c4 + 4, :, :].rearrange(
                    "k p n -> p k n")).then_inc(bld[c4], 16)
            with sp.Fori(0, 25) as i:
                for j in range(2):
                    load(BO + 1 + j, PAN, 2 * i)
            load(PANELS - 1)
            for q in range(TT):
                sp.wait_ge(r_h, 2 * TT + q + 1)
                sp.dma_start(out[q * P:(q + 1) * P, :], xres[:, q, :]).then_inc(o_st, 16)
            sp.wait_ge(o_st, 16 * TT)

        @block.gpsimd
        def _(pool):
            def split_lo(p, width=PAN, n=0):
                pool.wait_ge(w_hi, n + (p + 1))
                pool.tensor_tensor(wlo[p % 2][:, 0:width], stage[p % 2][:, 0:width],
                                   whi[p % 2][:, 0:width].bitcast(F32), ALU.subtract).then_inc(w_lo, 1)

            with pool.Fori(0, AO // 2) as i:
                for j in range(2):
                    split_lo(j, PAN, 2 * i)
            split_lo(AO)
            for kk in range(4):
                pool.wait_ge(ar_h, kk + 1)
                pool.tensor_tensor(ar_lo[:, kk, :], oT[:, kk, :], ar_hi[:, kk, :].bitcast(F32), ALU.subtract
                                   ).then_inc(ar_l, 1)
            split_lo(AO + 1)
            with pool.Fori(0, 5) as i:
                for j in range(2):
                    split_lo(AO + 2 + j, PAN, 2 * i)
            split_lo(36)
            with pool.Fori(0, PAIRS // 2) as i:
                for j in range(6):
                    split_lo(M0 + j, PANEL if j % 3 == 0 else PAN, 6 * i)
            with pool.Fori(0, (WO - BO) // 2) as i:
                for j in range(2):
                    split_lo(BO + j, PAN, 2 * i)
            split_lo(WO)

            def band_lo(b):
                pool.wait_ge(l_bhi, b + 1)
                pool.tensor_tensor(xlo[:, b, :], vband[:, b, :], xhi[:, b, :].bitcast(F32), ALU.subtract
                                   ).then_inc(l_blo, 1)

            for m in range(len(steps)):
                pool.wait_ge(e_rc, m + 1)
                pool.tensor_scalar(nt[:, m % 3, 0, :], nt[:, m % 3, 0, :], nsm[:, m % 3, 2, 0:1], None, ALU.mult
                                   ).then_inc(e_p, 1)
                if m == 1:
                    band_lo(0)
                if 2 <= m < 8:
                    band_lo(m)
                if 9 <= m < 13:
                    r = slice((m - 9) * 512, (m - 8) * 512)
                    w = (WO + 1) % 2
                    pool.wait_ge(w_hi, WO + 2)
                    last = pool.tensor_tensor(wlo[w][:, r], stage[w][:, r], whi[w][:, r].bitcast(F32), ALU.subtract)
                    if m == 12:
                        last.then_inc(w_lo, 1)
            with pool.Fori(0, (PANELS - WO - 2) // 2) as i:
                for j in range(2):
                    split_lo(WO + 2 + j, PAN, 2 * i)

        @block.tensor
        def _(pe):
            def panel(p, n=0):
                pe.wait_ge(w_lo, n + (p + 1))
                return whi[p % 2], wlo[p % 2]

            def tiles(p, n, nk, width, parts, moving, lo, hi, before, signal, each=False):
                wh, wl = panel(p, n)
                wh, wl = (w[:, 0:nk * width].rearrange("p (k n) -> p k n", k=nk) for w in (wh, wl))
                for m in range(lo, hi):
                    before(m)
                    for k in range(nk):
                        if each and m == 0:
                            pe.wait_ge(xt_lo, k + 1)
                        c = slice(m * P, (m + 1) * P)
                        last = split_dots(pe, parts[m][:, :], wh[:, k, c], wl[:, k, c],
                                          moving[0][:, k, :], moving[1][:, k, :], k == 0, k == nk - 1)
                    last.then_inc(signal, 1)

            def token_tiles(p, n, nk, k0, width, dst, start, stop, before, signal):
                wh, wl = panel(p, n)
                wh, wl = (w[:, 0:nk * width].rearrange("p (k n) -> p k n", k=nk) for w in (wh, wl))
                for q in range(TT):
                    before(q)
                    for k in range(nk):
                        r = slice(q * P, (q + 1) * P)
                        last = split_dots(pe, dst(q), xhi[:, k0 + k, r], xlo[:, k0 + k, r],
                                          wh[:, k, :], wl[:, k, :], start and k == 0, stop and k == nk - 1)
                    if stop:
                        last.then_inc(signal, 1)
                if not stop:
                    last.then_inc(half_done, 1)

            def nothing(_):
                pass

            def turn_x(src, ready, count, q):
                pe.wait_ge(ready, count + q + 1)
                for k in range(KX):
                    last = pe.transpose(bank[2 * q + k // 4][:, k % 4 * P:k % 4 * P + P],
                                        src[:, q, k * P:(k + 1) * P], ident[:, :])
                    if k % 4 == 3:
                        last.then_inc(xt_t, 1)

            def first_product(src, ready, count, round_, p, signal):
                def half(c, q):
                    wh, wl = (w[:, 0:PAN].rearrange("p (k n) -> p k n", k=4) for w in panel(p + c))
                    pe.wait_ge(xt_lo, KX * round_ + 2 * q + c + 1)
                    for k in range(4):
                        r = slice(q * P, (q + 1) * P)
                        last = split_dots(pe, bank[2 * q][:, :], xhi[:, 4 * c + k, r], xlo[:, 4 * c + k, r],
                                          wh[:, k, :], wl[:, k, :], c == 0 and k == 0, c == 1 and k == 3)
                    return last

                def turn(q):
                    turn_x(src, ready, count, q)

                turn(0)
                half(0, 0)
                turn(1)
                half(0, 1)
                turn(2)
                half(1, 0).then_inc(signal, 1)
                half(0, 2)
                turn(3)
                half(1, 1).then_inc(signal, 1)
                half(0, 3).then_inc(half_done, 1)
                half(1, 2).then_inc(signal, 1)
                half(1, 3).then_inc(signal, 1)

            def project_out(p0, nk, hi, lo, a0, free=None, turn=None):
                def half(n, j, first):
                    wh, wl = panel(p0 + j, n)
                    for b in range(2):
                        kk = 2 * j + b
                        pe.wait_ge(ar_l, 2 * n + (a0 + kk + 1))
                        for q in range(TT):
                            if first and b == 0 and free:
                                free(q)
                            for c in range(2):
                                w = slice(b * DM + c * 512, b * DM + c * 512 + 512)
                                r = slice(q * P, (q + 1) * P)
                                last = split_dots(pe, bank[2 * q + c][:, :], hi[:, kk % 4, r], lo[:, kk % 4, r],
                                                  wh[:, w], wl[:, w], first and kk == 0, False)
                    last.then_inc(half_done, 1)

                half(0, 0, True)
                if nk > 8:
                    with pe.Fori(0, nk // 4 - 1) as i:
                        half(2 * i, 1, False)
                        half(2 * i, 2, False)
                else:
                    half(0, 1, False)
                    half(0, 2, False)
                wh, wl = panel(p0 + nk // 2 - 1)
                pe.wait_ge(ar_l, a0 + nk)
                for q in range(TT):
                    if q == TT - 1 and turn:
                        turn(0)
                    for c in range(2):
                        for kk in range(2):
                            w = slice(kk * DM + c * 512, kk * DM + c * 512 + 512)
                            r = slice(q * P, (q + 1) * P)
                            last = split_dots(pe, bank[2 * q + c][:, :], hi[:, 2 + kk, r], lo[:, 2 + kk, r],
                                              wh[:, w], wl[:, w], False, kk == 1)
                        last.then_inc(y_done, 1)

            A, B, E, O = bank[0:4], bank[4:8], bank[0::2], bank[1::2]
            with pe.Fori(0, HA) as h:
                n = 6 * h
                tiles(A0, n, KX, 256, B, (xhi, xlo), 0, 2, lambda m: pe.wait_ge(a_ot, 4 * h + (m + 1)), a_qk,
                      each=True)
                tiles(A0 + 1, n, KX, 256, B[2:], (xhi, xlo), 0, 2, lambda m: pe.wait_ge(a_ot, 4 * h + (m + 3)),
                      a_qk)
                token_tiles(A0 + 2, n, 4, 0, 512, lambda q: A[q][:, :], True, False,
                            lambda q: pe.wait_ge(a_gt, 4 * h + (q + 1)), a_v)
                token_tiles(A0 + 3, n, 4, 4, 512, lambda q: A[q][:, :], False, True, nothing, a_v)
                pe.wait_ge(a_qklo, 4 * h + 4)
                for kt in range(TT):
                    for d in range(2):
                        r = slice(kt * P, (kt + 1) * P)
                        last = split_dots(pe, B[kt][:, 0:SEQ - kt * P], qk_hi[:, 2 + d, r], qk_lo[:, 2 + d, r],
                                          qk_hi[:, d, kt * P:], qk_lo[:, d, kt * P:], d == 0, d == 1)
                    last.then_inc(a_s, 1)
                tiles(A0 + 4, n, KX, 256, A, (xhi, xlo), 0, 2, lambda m: pe.wait_ge(a_vlo, 4 * h + (m + 1)), a_g)
                pe.wait_ge(a_vlo, 4 * h + 4)
                for q in range(TT):
                    pe.wait_ge(a_slo, 4 * h + (q + 1))
                    for kt in range(q + 1):
                        r = slice(KT_AT[kt] + (q - kt) * P, KT_AT[kt] + (q - kt + 1) * P)
                        last = split_dots(pe, B[q][:, :], s_hi[:, r], s_lo[:, r], v_hi[:, kt, :], v_lo[:, kt, :],
                                          kt == 0, kt == q)
                    last.then_inc(a_o, 1)
                tiles(A0 + 5, n, KX, 256, A[2:], (xhi, xlo), 0, 2, nothing, a_g)
                pe.wait_ge(aux["const"], 48)
                pe.wait_ge(a_on, 4 * h + 4)
                for j in range(VT):
                    for q in range(TT):
                        last = pe.transpose(B[j][:, q * P:(q + 1) * P], work[:, q, j * P:(j + 1) * P], ident[:, :])
                    last.then_inc(a_t, 1)
            project_out(AO, HA * VT, ar_hi, ar_lo, 0,
                        lambda q: pe.wait_ge(a_gt if q < 2 else a_ot, 4 * HA + 2 + 2 * (q % 2)))

            first_product(xres, n_x, 0, 1, B0, b_c)
            token_tiles(B0 + 2, 0, 4, 0, 512, lambda q: O[q][:, :], True, False, nothing, b_ql)
            pe.wait_ge(b_ctok, TT)
            for j in range(KC):
                for q in range(TT):
                    last = pe.transpose(E[j][:, q * P:(q + 1) * P], c_tok[:, q, j * P:(j + 1) * P], ident[:, :])
                last.then_inc(b_ct, 1)
            token_tiles(B0 + 3, 0, 4, 4, 512, lambda q: O[q][:, :], False, True, nothing, b_ql)
            token_tiles(B0 + 4, 0, KX, 0, 256, lambda q: E[q][:, 0:256], True, True,
                        lambda q: pe.wait_ge(b_clo, q + 1), b_ql)
            pe.wait_ge(b_qtok, 3)
            pe.wait_ge(b_qtl, 3)
            for q in range(TT):
                if q == TT - 1:
                    pe.wait_ge(b_qtok, TT)
                    pe.wait_ge(b_qtl, TT)
                for j in range(KQ):
                    last = pe.transpose(bank[j][:, q * P:(q + 1) * P], q_tok[:, q, j * P:(j + 1) * P], ident[:, :])
                    if q == TT - 1:
                        last.then_inc(b_qt, 1)
            pe.wait_ge(b_wl, 1)
            for k in range(KX):
                last = split_dots(pe, bank[7][:, :], wkr_hi[:, k, :], wkr_lo[:, k, :], xhi[:, k, :], xlo[:, k, :],
                                  k == 0, k == KX - 1)
            last.then_inc(b_kr, 1)
            pe.wait_ge(b_qlo, KQ)
            pe.wait_ge(b_w, 3)

            with pe.Fori(0, PAIRS // 2) as it:
                for s in range(2):
                    n = 6 * it
                    p = M0 + 3 * s

                    def c(per, k):
                        return 2 * per * it + (per * s + k)

                    tiles(p, n, KQ, 384, bank[4:7], (ql_hi, ql_lo), 0, 3, nothing, m_q)
                    pe.wait_ge(m_gt, c(2, 2))
                    pe.wait_ge(m_og, c(2, 1))
                    tiles(p + 1, n, KC, 512, bank[0:2], (c_hi, c_lo), 0, 2, nothing, m_kv)
                    wh, wl = (w[:, 0:PAN].rearrange("p (k n) -> p k n", k=KC) for w in panel(p + 1, n))
                    for q in range(TT):
                        for k in range(KC):
                            r = slice(q * P, (q + 1) * P)
                            last = split_dots(pe, bank[2 + q // 2][:, q % 2 * 256:q % 2 * 256 + 256],
                                              c_hi[:, k, r], c_lo[:, k, r], wh[:, k, 256:512], wl[:, k, 256:512],
                                              k == 0, k == KC - 1)
                        if q % 2:
                            last.then_inc(m_kv, 1)

                    def scores(e):
                        for q in range(TT):
                            w = (q + 1) * P
                            r = slice(q * P, w)
                            dst = bank[4 + q]
                            f = slice(ROPE * e, ROPE * e + ROPE)
                            pe.matmul(dst[:, 0:w], qn_hi[:, e, r], kn_hi[:, e, 0:w], start=True, stop=False)
                            pe.matmul(dst[:, r], id_r[:, :], mask_r[:, :], start=False, stop=False)
                            pe.matmul(dst[:, 0:w], qn_hi[:, e, r], kn_lo[:, e, 0:w], start=False, stop=False)
                            pe.matmul(dst[:, 0:w], qn_lo[:, e, r], kn_hi[:, e, 0:w], start=False, stop=False)
                            split_dots(pe, dst[:, 0:w], qr_hi[f, r], qr_lo[f, r], kr_hi[f, 0:w], kr_lo[f, 0:w],
                                       False, True).then_inc(m_s, 1)

                    def turn(e):
                        dst = [bank[1], bank[2], bank[3]] if e == 0 else [bank[2], bank[3], bank[4]]
                        for kt in range(TT):
                            for q in range(kt, TT):
                                at = (q - kt) * P + (256 if kt == 3 else 0)
                                src = q * (q + 1) // 2 * P + kt * P
                                last = pe.transpose(dst[min(kt, 2)][:, at:at + P], prob[:, src:src + P], ident[:, :])
                            if kt != 2:
                                last.then_inc(m_t, 1)

                    def attend(e, dst):
                        for kt in range(TT):
                            r = slice(KT_AT[kt], KT_AT[kt] + SEQ - kt * P)
                            last = split_dots(pe, dst[:, kt * P:], vb_hi[:, kt, e * VH:(e + 1) * VH],
                                              vb_lo[:, kt, e * VH:(e + 1) * VH], pt_hi[:, r], pt_lo[:, r],
                                              kt == 0, kt == TT - 1)
                        last.then_inc(m_o, 1)

                    def gate_part(m, k0, k1):
                        wh, wl = (w[:, 0:PAN].rearrange("p (k n) -> p k n", k=KX) for w in panel(p + 2, n))
                        for k in range(k0, k1):
                            f = slice(m * P, (m + 1) * P)
                            last = split_dots(pe, bank[0][:, :], wh[:, k, f], wl[:, k, f], xhi[:, k, :],
                                              xlo[:, k, :], k == 0, k == KX - 1)
                        return last

                    pe.wait_ge(b_krlo, 1)
                    pe.wait_ge(m_qlo, c(3, 3))
                    pe.wait_ge(m_kvlo, c(4, 1))
                    pe.wait_ge(m_og, c(2, 2))
                    scores(0)
                    gate_part(0, 0, KX).then_inc(m_g, 1)
                    pe.wait_ge(m_kvlo, c(4, 4))
                    pe.wait_ge(m_p, c(8, 4))
                    turn(0)
                    scores(1)
                    pe.wait_ge(m_gt, c(2, 3))
                    gate_part(1, 0, KX // 2)
                    pe.wait_ge(m_ptlo, c(6, 3))
                    attend(0, bank[1])
                    pe.wait_ge(m_p, c(8, 8))
                    turn(1)
                    gate_part(1, KX // 2, KX).then_inc(m_g, 1)
                    pe.wait_ge(m_ptlo, c(6, 6))
                    attend(1, bank[7])
            pe.wait_ge(m_gt, 2 * PAIRS + 2)
            project_out(BO, HB, br_hi, br_lo, HA * VT, lambda q: pe.wait_ge(m_og, 2 * PAIRS + (2 if q == 3 else 1)))

            first_product(h_tok, r_h, 0, 2, L0, l_v)
            for a in range(2):
                tiles(L0 + 2 + a, 0, KX, 256, O[2 * a:], (xhi, xlo), 0, 2, nothing, l_u)
            for a in range(2):
                tiles(L0 + 4 + a, 0, KX, 256, E[2 * a:], (xhi, xlo), 0, 2,
                      lambda m: pe.wait_ge(l_vt, 2 * a + m + 1), l_q)
            pe.wait_ge(l_wl, 1)
            pe.wait_ge(l_mk, 2)

            def keys(g):
                tiles(L0 + 6 + g // 2, 0, KX, 256, O[g // 2 * 2:], (xhi, xlo), g % 2, g % 2 + 1,
                      lambda m: pe.wait_ge(l_up, g + 1), l_q)
                pe.wait_ge(l_qlo, g + 1)
                pe.wait_ge(l_plo, g + 1)
                split_dots(pe, E[g][:, :], wp_hi[:, g, :], wp_lo[:, g, :], pool_hi[:, :], pool_lo[:, :], True, True
                           ).then_inc(l_mix, 1)

            for g in range(3):
                keys(g)
            for i in range(len(steps) + 3):
                if i == 2:
                    keys(3)
                if i < len(steps):
                    hp, j = steps[i]
                    if i < 2:
                        pe.wait_ge(l_mo, i + 1)
                    else:
                        pe.wait_ge(e_tk, i - 1)
                    if i < 4:
                        pe.wait_ge(l_qlo, 5 + hp)
                    for e in range(2):
                        f = slice(DHN * e, DHN * e + DHN)
                        o = bank[2 * (i % 2) + e][:, 0:256]
                        q_ = [x[f, hp, j * P:(j + 1) * P] for x in (nq_hi, nq_lo)]
                        k_ = [x[f, hp, :].rearrange("p (r c) -> p r c", r=ROWS)[
                              :, :, BAND_START[j]:BAND_START[j] + BAND] for x in (nk_hi, nk_lo)]
                        pe.matmul(o, id_n[:, :], nmask_r[:, j:j + 1, :].to_broadcast([P, ROWS, BAND]),
                                  start=True, stop=False)
                        last = split_dots(pe, o, q_[0], q_[1], k_[0], k_[1], False, True)
                    last.then_inc(e_s, 1)
                if 2 <= i < len(steps) + 2:
                    m = i - 2
                    if m == 0:
                        pe.wait_ge(l_mo, 4)
                    pe.wait_ge(e_p, m + 1)
                    pe.wait_ge(e_q, m + 1)
                    if m >= 2:
                        pe.wait_ge(e_tlo, m - 1)
                    for e in range(2):
                        for half in range(2):
                            a = (2 * e + half) * P
                            last = pe.transpose(bank[4 + m % 2][:, a:a + P],
                                                nt[:, m % 3, e, half * P:(half + 1) * P], ident[:, :])
                    last.then_inc(e_t, 1)
                if i >= 3:
                    m = i - 3
                    hp, j = steps[m]
                    pe.wait_ge(e_tlo, m + 1)
                    if hp == 0:
                        pe.wait_ge(l_blo, 2 * j + 1)
                        pe.wait_ge(l_blo1, 1)
                    if m >= 2:
                        pe.wait_ge(e_oc, 2 * (m - 1))
                    for half in range(2):
                        p_ = [x[:, m % 2, :].rearrange("p (e a n) -> p e a n", e=2, a=2)[:, :, half, :]
                              for x in (npt_hi, npt_lo)]
                        last = split_dots(pe, bank[6 + m % 2][:, 0:2 * P],
                                          xhi[:, 2 * j + half, hp * P:(hp + 1) * P],
                                          xlo[:, 2 * j + half, hp * P:(hp + 1) * P],
                                          p_[0], p_[1], half == 0, half == 1)
                    last.then_inc(e_o, 1)
            project_out(WO, KX, cr_hi, cr_lo, HA * VT + HB,
                        free=lambda q: pe.wait_ge((e_tk, e_tk, e_tlo, e_oc)[q], len(steps) * (1, 1, 1, 2)[q]), turn=lambda q: turn_x(h2_tok, r_h, TT, q))
            turn_x(h2_tok, r_h, TT, 1)
            for s in range(2):
                pe.wait_ge(xt_lo, 3 * KX + 4 * (s + 1))
                r = slice(256 * s, 256 * s + 256)
                for m in range(3):
                    if s == 0 and m == 2:
                        turn_x(h2_tok, r_h, TT, 2)
                        turn_x(h2_tok, r_h, TT, 3)
                    wh, wl = (w[:, 0:PAN].rearrange("p (k n) -> p k n", k=KX) for w in panel(UP + m // 2))
                    for k in range(KX):
                        f = slice(m % 2 * P, m % 2 * P + P)
                        last = split_dots(pe, bank[m][:, r], wh[:, k, f], wl[:, k, f], xhi[:, k, r], xlo[:, k, r],
                                          k == 0, k == KX - 1)
                    if s:
                        last.then_inc(u_m, 1)
            tiles(UP + 1, 0, KX, 256, bank[2:], (xhi, xlo), 1, 2, nothing, u_m)
            with pe.Fori(1, 8) as i:
                for a in range(2):
                    tiles(UP + a, 2 * i, KX, 256, bank[2 * a:], (xhi, xlo), 0, 2,
                          lambda m: pe.wait_ge(u_r, 4 * i + (2 * a + m + 1)), u_m)
            project_out(DN, KF, dr_hi, dr_lo, HA * VT + HB + KX,
                        lambda q: pe.wait_ge(u_r, KF + min(4, 2 * q + 2)))

        @block.scalar
        def _(act):
            own = Own(act, ac)

            def split_hi(p, used=None, count=0, width=PAN, n=0):
                act.wait_ge(landed[p % 2], 8 * n + 16 * (p // 2 + 1))
                if used is not None:
                    act.wait_ge(used, count)
                act.activation(whi[p % 2][:, 0:width], stage[p % 2][:, 0:width], ACT.Copy).then_inc(w_hi, 1)

            def copy(dst, src, signal, scale=1.0):
                act.activation(dst, src, ACT.Copy, scale=scale).then_inc(signal, 1)

            def first_tiles(src, hi):
                for kk in range(4):
                    copy(hi[:, kk, :], src[:, kk, :], ar_h)

            def project_out(p0, nk, src, hi, done, ready=None):
                if ready:
                    ready(0)
                    first_tiles(src, hi)
                    for c in range(1, nk // 4):
                        ready(4 * c)

                def half(j, n, k):
                    split_hi(p0 + j, half_done, n + (done + j - 1), PAN, n)
                    for b in range(2):
                        copy(hi[:, (2 * j + b) % 4, :], src[:, bass.ds(k + (2 * j + b), 1), :].rearrange(
                            "p a n -> p (a n)"), ar_h)

                with act.Fori(1, nk // 4) as i:
                    for j in range(2):
                        half(j, 2 * i, 4 * i)

            def norms(y0, ln=None, rms=None, squares_to=None, scratch=None, round_=None, next_panel=None, done=0):
                def deviation(q):
                    act.wait_ge(n_mu, TT * ln + q + 1)
                    act.activation(scratch[:, q % 2, :], xres[:, q, :], ACT.Square, bias=small[:, 0, q:q + 1],
                                   accum_out=small[:, 3, q:q + 1]).then_inc(n_ss, 1)
                    act.wait_ge(n_ss, TT * ln + q + 1)
                    act.activation(small[:, 1, q:q + 1], small[:, 3, q:q + 1], ACT.Sqrt, scale=1.0 / DM,
                                   bias=eps[:, 0:1]).then_inc(n_sd, 1)

                def root_mean_square(q):
                    act.wait_ge(n_x, y0 + q + 1)
                    act.activation(squares_to[:, q, :], xres[:, q, :], ACT.Square, accum_out=small[:, 3, 4 + q:5 + q]
                                   ).then_inc(r_ss, 1)
                    act.wait_ge(r_ss, TT * rms + q + 1)
                    act.activation(small[:, 1, 4 + q:5 + q], small[:, 3, 4 + q:5 + q], ACT.Sqrt, scale=1.0 / DM,
                                   bias=eps[:, 1:2]).then_inc(r_sd, 1)

                def transposed(q):
                    for c in range(2):
                        act.wait_ge(xt_t, KX * (round_ - 1) + 2 * q + c + 1)
                        copy(xhi[:, 4 * c:4 * c + 4, q * P:(q + 1) * P],
                             bank[2 * q + c][:, :].rearrange("p (k n) -> p k n", k=4), xt_hi)

                if next_panel:
                    split_hi(next_panel, half_done, done)
                if ln is None:
                    root_mean_square(0)
                    root_mean_square(1)
                    if round_:
                        transposed(0)
                    root_mean_square(2)
                    if round_:
                        transposed(1)
                    root_mean_square(3)
                    if next_panel:
                        split_hi(next_panel + 1, y_done, 2 * (y0 + TT))
                    if round_:
                        transposed(2)
                        transposed(3)
                else:
                    for q in range(TT + 1):
                        if rms is None and q:
                            transposed(q - 1)
                        if q < TT:
                            deviation(q)
                        if rms is not None and q:
                            transposed(q - 1)
                        if q == 1:
                            split_hi(next_panel + 1, y_done, 2 * (y0 + TT))
                        if rms is not None and q < TT:
                            root_mean_square(q)

            xt_view = xres[:, :, :].rearrange("p t (a n) -> p (t a) n", a=2)
            split_hi(0)
            for k in range(KX):
                act.wait_ge(xt_ld[k], 16)
                copy(xhi[:, k, :], xt_view[:, k, :], xt_hi)
            split_hi(1)
            act.wait_ge(xt_lo, KX)
            act.dma_start(xres[:, :, :], t["x"]).then_inc(aux["x"], 16)
            A, B, E, O = bank[0:4], bank[4:8], bank[0::2], bank[1::2]
            with act.Fori(0, HA) as h:
                n = 6 * h
                act.wait_ge(a_dec, 4 * h + 4)
                act.dma_start(decay[:, :], t["decay"][bass.ds(h, 1), :, :].rearrange("a p n -> (a p) n")
                              ).then_inc(aux["decay"], 16)
                for m in range(4):
                    if m % 2 == 0:
                        split_hi(A0 + 2 + m // 2, a_qk, 4 * h + (m + 2), PAN, n)
                    act.wait_ge(a_q32, 4 * h + (m + 1))
                    copy(qk_hi[:, m, :], work[:, m % 2 * 2, :], a_qkhi)
                split_hi(A0 + 4, half_done, h + 1, PAN, n)
                for q in range(TT):
                    act.wait_ge(a_v, 4 * h + (q + 1))
                    copy(v_hi[:, q, :], A[q][:, :], a_vhi)
                split_hi(A0 + 5, a_v, 4 * h + 4, PAN, n)
                for kt in range(TT):
                    act.wait_ge(a_dec, 4 * h + (kt + 5))
                    copy(s_hi[:, KT_AT[kt]:KT_AT[kt] + SEQ - kt * P], work[:, kt, 0:SEQ - kt * P], a_shi)

                def tanh(m):
                    act.wait_ge(a_g, 4 * h + (m + 1))
                    act.activation(gate[:, m, :], A[m][:, :], ACT.Tanh, scale=0.5).then_inc(a_th, 1)

                tanh(0)
                tanh(1)
                split_hi(A0 + 6, a_g, 4 * h + 2, PAN, n)
                act.wait_ge(a_var, h + 1)
                act.activation(small[:, 1, 0:TT], small[:, 0, 0:TT], ACT.Sqrt).then_inc(a_sd, 1)
                tanh(2)
                tanh(3)
                split_hi(A0 + 7, a_g, 4 * h + 4, PAN, n)
            act.wait_ge(a_o, 4 * HA)
            act.dma_start(rows[:, :, :], t["ln"][0]).then_inc(aux["rows"], 16)

            def outputs(k):
                if k == HA * VT - 4:
                    act.wait_ge(a_ot, 4 * HA + 4)
                elif k == 0:
                    act.wait_ge(a_ot, 4 * HA)

            project_out(AO, HA * VT, oT, ar_hi, HA, outputs)
            norms(0, ln=0, scratch=gate[:, :, :].rearrange("p (t a) n -> p t (a n)", a=2), round_=1, next_panel=B0,
                  done=HA + 7)
            act.wait_ge(n_x, TT)
            act.dma_start(wkr[:, :, :], t["wkr"]).then_inc(aux["kr"], 16)
            act.dma_start(mask_f[:, :], t["mask"]).then_inc(aux["kr"], 16)
            act.dma_start(rope_b[:, :, :], t["rope_b"]).then_inc(aux["ropeb"], 16)

            act.wait_ge(aux["kr"], 32)
            copy(wkr_hi[:, :, :], wkr[:, :, :], b_w)
            copy(mask_r[:, :], mask_f[:, :], b_w)
            copy(id_r[:, :], ident[:, :], b_w)
            split_hi(B0 + 2, half_done, HA + 8)
            for q in range(TT):
                act.wait_ge(b_c, q + 1)
                act.activation(c_tok[:, q, :], E[q][:, :], ACT.Square, accum_out=small[:, 3, q:q + 1]
                               ).then_inc(b_css, 1)
            act.wait_ge(b_cms, 1)
            act.activation(small[:, 1, 0:TT], small[:, 0, 0:TT], ACT.Sqrt).then_inc(b_csd, 1)
            act.wait_ge(b_crs, 1)
            for q in range(TT):
                copy(c_tok[:, q, :], E[q][:, :], b_ctok, small[:, 2, q:q + 1])
            split_hi(B0 + 3, b_c, TT)
            for j in range(KC):
                act.wait_ge(b_ct, j + 1)
                copy(c_hi[:, j, :], E[j][:, :], b_chi, cols[:, COL_CG + j:COL_CG + j + 1])
            split_hi(B0 + 4, half_done, HA + 9)
            for q in range(TT):
                act.wait_ge(b_ql, q + 1)
                act.activation(q_tok[:, q, 0:512], O[q][:, :], ACT.Square, accum_out=small[:, 3, 4 + q:5 + q]
                               ).then_inc(b_qss, 1)
            split_hi(M0, b_ql, TT, PANEL)
            for q in range(TT):
                act.wait_ge(b_ql, TT + q + 1)
                act.activation(q_tok[:, q, 512:768], E[q][:, 0:256], ACT.Square, accum_out=small[:, 3, q:q + 1]
                               ).then_inc(b_qss, 1)
                act.wait_ge(b_qms, q + 1)
                act.activation(small[:, 1, 4 + q:5 + q], small[:, 0, 4 + q:5 + q], ACT.Sqrt).then_inc(b_qsd, 1)
                act.wait_ge(b_qrs, q + 1)
                copy(q_tok[:, q, 0:512], O[q][:, :], b_qtok, small[:, 2, 4 + q:5 + q])
            for j in range(KQ):
                act.wait_ge(b_qt, j + 1)
                copy(ql_hi[:, j, :], bank[j][:, :], b_qhi, cols[:, COL_QG + j:COL_QG + j + 1])
                if j == 1:
                    split_hi(M0 + 1, b_ql, 2 * TT)
            act.wait_ge(b_kr32, 1)
            copy(kr_hi[:, :], rtmp[:, 0, :], b_krhi)

            with act.Fori(0, PAIRS // 2) as it:
                for s in range(2):
                    n = 6 * it
                    p = M0 + 3 * s

                    def c(per, k):
                        return 2 * per * it + (per * s + k)

                    for m in range(2):
                        act.wait_ge(m_q, c(3, m + 1))
                        copy(qn_hi[:, m, :], bank[4 + m][:, :], m_qhi)
                    split_hi(p + 2, m_q, c(3, 3), PAN, n)
                    act.wait_ge(m_qr32, c(1, 1))
                    copy(qr_hi[:, :], rtmp[:, 0, :], m_qhi)
                    for m in range(2):
                        act.wait_ge(m_kv, c(4, m + 1))
                        copy(kn_hi[:, m, :], bank[m][:, :], m_kvhi)
                    for m in range(2):
                        act.wait_ge(m_kv, c(4, m + 3))
                        copy(vb_hi[:, 2 * m:2 * m + 2, :].rearrange("p t n -> p (t n)"), bank[2 + m][:, :], m_kvhi)
                    split_hi(p + 3, m_kv, c(4, 4), PANEL, n)

                    def exps(e):
                        for q in range(TT):
                            w = (q + 1) * P
                            at = q * (q + 1) // 2 * P
                            act.wait_ge(m_nb, c(8, 4 * e + q + 1))
                            act.activation(prob[:, at:at + w], bank[4 + q][:, 0:w], ACT.Exp, scale=SCALE_B,
                                           bias=sm[:, 1, 4 * e + q:4 * e + q + 1],
                                           accum_out=sm[:, 2, 4 * e + q:4 * e + q + 1]).then_inc(m_exp, 1)

                    def turned(e):
                        for b in range(3):
                            w = (512, 384, 384)[b]
                            act.wait_ge(m_t, c(6, 3 * e + b + 1))
                            copy(pt_hi[:, (0, 512, 896)[b]:(0, 512, 896)[b] + w], bank[1 + e + b][:, 0:w], m_pthi)

                    def tanh(m):
                        act.wait_ge(m_g, c(2, m + 1))
                        act.wait_ge(m_st[m], 32 * it + (16 * s + 16))
                        act.activation(gt[:, m, :], bank[0][:, :], ACT.Tanh, scale=0.5).then_inc(m_th, 1)

                    def store(e):
                        act.wait_ge(m_og, c(2, e + 3))
                        act.dma_start(t["o_spill"][bass.ds(4 * it + (2 * s + e), 1), :, :].rearrange(
                            "a p n -> (a p) n"), gt[:, e, :]).then_inc(m_st[e], 16)

                    exps(0)
                    tanh(0)
                    turned(0)
                    exps(1)
                    turned(1)
                    store(0)
                    tanh(1)
                    split_hi(p + 4, m_g, c(2, 2), PAN, n)
                    store(1)

            def outputs_b(k):
                if k == 4:
                    for e in range(2):
                        act.wait_ge(m_st[e], 16 * PAIRS + 16)
                    act.dma_start(bT[:, 12:16, :], t["o_spill"][12:16, :, :].rearrange("k p n -> p k n")
                                  ).then_inc(bld[3], 16)
                    act.dma_start(rows2[:, :, :], t["ln"][1]).then_inc(aux["rows2"], 16)
                    act.dma_start(bias[:, :, :, :], t["bias"]).then_inc(aux["bias"], 16)
                    act.dma_start(nmask[:, :, :], t["nmask"]).then_inc(aux["nmask"], 16)
                    act.dma_start(wp[:, :, :], t["wp"]).then_inc(aux["wp"], 16)
                    act.dma_start(edge[:, :, :], t["edge"]).then_inc(aux["edge"], 16)
                act.wait_ge(bld[k // 4], 16)

            project_out(BO, HB, bT, br_hi, HA + 9, outputs_b)
            norms(TT, ln=1, rms=0, squares_to=h_tok, scratch=mixT[:, 0:4, :].rearrange("p (t a) n -> p t (a n)", a=2),
                  round_=2, next_panel=L0, done=HA + 16)
            act.wait_ge(r_h, TT)
            act.dma_start(grow[:, :], t["grow"][1]).then_inc(aux["grow"], 16)

            act.wait_ge(aux["nmask"], 16)
            copy(nmask_r[:, :, :], nmask[:, :, :], l_mk)
            copy(id_n[:, :], ident[:, :], l_mk)
            act.wait_ge(aux["wp"], 16)
            copy(wp_hi[:, :, :], wp[:, :, :], l_w)
            split_hi(L0 + 2, half_done, HA + 17)
            for q in range(TT):
                act.wait_ge(l_v, q + 1)
                copy(v_tok[:, q, :], E[q][:, :], l_vt)
            act.wait_ge(l_vt, TT)
            act.dma_start(t["v_spill"].rearrange("(t p) n -> p t n", p=P), v_tok[:, :, :]).then_inc(vst, 16)
            split_hi(L0 + 3, l_v, TT)
            act.wait_ge(vst, 16)
            for g in range(4):
                act.wait_ge(l_u, g + 1)
                copy(upad[:, g, PAD:PAD + SEQ], O[g][:, :], l_up)
                if g % 2:
                    split_hi(L0 + 4 + g // 2, l_u, g + 1)
                if g == 1:
                    grid = t["v_spill"].rearrange("(r c) n -> r c n", c=GRID)
                    for j in range(NBLK):
                        for half in range(2):
                            act.dma_start(vband[:, 2 * j + half, :],
                                          grid[4 * half:4 * half + 4, BAND_START[j]:BAND_START[j] + BAND, :]
                                          ).then_inc(vld[2 * j + half], 16)

            def pooled_hi(g):
                act.wait_ge(l_pool, g + 1)
                copy(pool_hi[:, :], win[:, 0, 0:SEQ], l_phi)

            pooled_hi(0)
            for m in range(4):
                act.wait_ge(l_q, m + 1)
                copy(by_block(nq_hi[:, m, :]), from_rows(E[m][:, :]), l_qhi)
                if m % 2:
                    split_hi(L0 + 6 + m // 2, l_q, m + 1)

            def keys(m):
                act.wait_ge(l_q, m + 5)
                copy(nk_hi[:, m, :], O[m][:, :], l_qhi)
                act.wait_ge(l_mix, m + 1)
                if m < 3:
                    pooled_hi(m + 1)
                copy(mixT[:, m, :], E[m][:, :], l_mo, cols[:, COL_PS + m:COL_PS + m + 1])

            keys(0)
            keys(1)
            split_hi(WO, l_q, 6)
            keys(2)

            def band_hi(b):
                act.wait_ge(vld[b], 16)
                copy(xhi[:, b, :], vband[:, b, :], l_bhi)

            for i in range(len(steps) + 3):
                if i == 2:
                    keys(3)
                    band_hi(0)
                    band_hi(1)
                if 2 <= i < len(steps) + 2:
                    m = i - 2
                    act.wait_ge(e_t, m + 1)
                    if m >= 2:
                        act.wait_ge(e_o, m - 1)
                    copy(npt_hi[:, m % 2, :], bank[4 + m % 2][:, :], e_thi)
                if i < len(steps):
                    act.wait_ge(e_nb, i + 1)
                    for e in range(2):
                        act.activation(nt[:, i % 3, e, :], nt[:, i % 3, e, :], ACT.Exp, bias=nsm[:, i % 3, 0, e:e + 1],
                                       accum_out=nsm[:, i % 3, 1, e:e + 1]).then_inc(e_exp, 1)
                if 2 <= i < 8:
                    band_hi(i)
                if i == len(steps):
                    act.wait_ge(e_s, len(steps))
                    first_tiles(mixT, cr_hi)
                if i in (9, 10):
                    r = slice((i - 9) * 1024, (i - 8) * 1024)
                    w = (WO + 1) % 2
                    act.wait_ge(landed[w], 16 * ((WO + 1) // 2 + 1))
                    last = act.activation(whi[w][:, r], stage[w][:, r], ACT.Copy)
                    if i == 10:
                        last.then_inc(w_hi, 1)
                if i >= 3:
                    m = i - 3
                    hp, j = steps[m]
                    act.wait_ge(e_o, m + 1)
                    for e in range(2):
                        f = slice(DHN * e, DHN * e + DHN)
                        dst = mixT[f, 4 + hp, :].rearrange("p (r c) -> p r c", r=ROWS)[:, :, j * BLK:(j + 1) * BLK]
                        copy(dst, bank[6 + m % 2][f, e * P:(e + 1) * P].rearrange("p (r c) -> p r c", r=ROWS), e_oc)
            act.wait_ge(e_oc, 2 * len(steps))
            project_out(WO, KX, mixT, cr_hi, HA + 17)
            norms(2 * TT, rms=1, squares_to=h2_tok, round_=3, next_panel=UP, done=HA + 20)

            act.wait_ge(r_h, 2 * TT)
            act.dma_start(grow[:, :], t["grow"][2]).then_inc(aux["grow"], 16)

            def hidden(m, i):
                act.wait_ge(u_m, 4 * i + (m + 1))
                act.wait_ge(u_s, 4 * i + (m + 1))
                act.activation(relu[:, m, :], bank[m][:, :], ACT.Relu).then_inc(u_r, 1)
                if m % 2:
                    split_hi(UP + 2 + m // 2, u_m, 4 * i + (m + 1), PAN, 2 * i)

            with act.Fori(0, KF // 4 - 1) as i:
                for m in range(4):
                    hidden(m, i)
            hidden(0, KF // 4 - 1)
            hidden(1, KF // 4 - 1)
            first_tiles(hid, dr_hi)
            hidden(2, KF // 4 - 1)
            hidden(3, KF // 4 - 1)
            act.wait_ge(u_s, KF + 4)
            project_out(DN, KF, hid, dr_hi, HA + 20)
            norms(3 * TT, rms=2, squares_to=hid[:, 0:2 * TT, :].rearrange("p (t a) n -> p t (a n)", a=2))

        @block.vector
        def _(dve):
            own = Own(dve, dv)

            def lo_of(dst, src, hi, signal):
                dve.tensor_tensor(dst, src, hi.bitcast(F32), ALU.subtract).then_inc(signal, 1)

            def lo_scaled(dst, src, scale, hi, signal):
                dve.scalar_tensor_tensor(out=dst, in0=src, scalar=scale, in1=hi.bitcast(F32), op0=ALU.mult,
                                         op1=ALU.subtract).then_inc(signal, 1)

            def first_tiles(src, hi, lo, a0):
                for kk in range(4):
                    dve.wait_ge(ar_h, a0 + kk + 1)
                    lo_of(lo[:, kk, :], src[:, kk, :], hi[:, kk, :], ar_l)

            def project_out(nk, src, hi, lo, a0):
                with dve.Fori(1, nk // 4) as i:
                    for kk in range(4):
                        dve.wait_ge(ar_h, 4 * i + (a0 + kk + 1))
                        lo_of(lo[:, kk, :], src[:, bass.ds(4 * i + kk, 1), :].rearrange("p a n -> p (a n)"),
                              hi[:, kk, :], ar_l)

            def norms(y0, ln=None, rms=None, gb=None, centred=None, result=None, round_=None):
                def gather(q):
                    for c in range(2):
                        w = slice(c * 512, (c + 1) * 512)
                        dve.wait_ge(y_done, 2 * (y0 + q) + c + 1)
                        y = bank[2 * q + c][:, :]
                        if ln is not None:
                            own.mark(dve.scalar_tensor_tensor(out=xres[:, q, w], in0=xres[:, q, w], scalar=ALPHA,
                                                              in1=y, op0=ALU.mult, op1=ALU.add,
                                                              accum_out=mv[:, q, c:c + 1]))
                        elif c == 0:
                            own.mark(dve.tensor_tensor(xres[:, q, w], xres[:, q, w], y, ALU.add))
                        else:
                            own.settle()
                            dve.tensor_tensor(xres[:, q, w], xres[:, q, w], y, ALU.add).then_inc(n_x, 1)
                    if ln is not None:
                        own.settle()
                        dve.tensor_scalar(small[:, 0, q:q + 1], mv[:, q, 0:1], mv[:, q, 1:2], -1.0 / DM, ALU.add,
                                          ALU.mult).then_inc(n_mu, 1)
                        dve.wait_ge(n_mu, TT * ln + q + 1)
                        own.mark(dve.scalar_tensor_tensor(out=centred[:, q, :], in0=xres[:, q, :],
                                                          scalar=small[:, 0, q:q + 1], in1=gb[:, 0, :], op0=ALU.add,
                                                          op1=ALU.mult))

                def shift(q):
                    dve.wait_ge(n_sd, TT * ln + q + 1)
                    own.mark(dve.reciprocal(small[:, 2, q:q + 1], small[:, 1, q:q + 1]))
                    own.settle()
                    dve.scalar_tensor_tensor(out=xres[:, q, :], in0=centred[:, q, :], scalar=small[:, 2, q:q + 1],
                                             in1=gb[:, 1, :], op0=ALU.mult, op1=ALU.add).then_inc(n_x, 1)

                def scale(q):
                    dve.wait_ge(r_sd, TT * rms + q + 1)
                    own.mark(dve.reciprocal(small[:, 2, 4 + q:5 + q], small[:, 1, 4 + q:5 + q]))
                    own.settle()
                    dve.scalar_tensor_tensor(out=result[:, q, :], in0=xres[:, q, :], scalar=small[:, 2, 4 + q:5 + q],
                                             in1=grow[:, :], op0=ALU.mult, op1=ALU.mult).then_inc(r_h, 1)

                def transposed(q):
                    for c in range(2):
                        dve.wait_ge(xt_hi, KX * round_ + 2 * q + c + 1)
                        lo_of(xlo[:, 4 * c:4 * c + 4, q * P:(q + 1) * P],
                              bank[2 * q + c][:, :].rearrange("p (k n) -> p k n", k=4),
                              xhi[:, 4 * c:4 * c + 4, q * P:(q + 1) * P], xt_lo)

                if ln is None:
                    gather(0)
                    gather(1)
                    scale(0)
                    gather(2)
                    scale(1)
                    if round_:
                        transposed(0)
                    gather(3)
                    if round_:
                        transposed(1)
                    scale(2)
                    scale(3)
                    if round_:
                        transposed(2)
                        transposed(3)
                else:
                    for q in range(TT + 1):
                        if q < TT:
                            gather(q)
                        if q and rms is None:
                            transposed(q - 1)
                        elif q:
                            scale(q - 1)
                        if q < TT:
                            shift(q)
                        if q and rms is not None:
                            transposed(q - 1)

            dve.memset(eps[:, 0:1], LN_EPS)
            dve.memset(eps[:, 1:2], RMS_EPS)
            dve.sem_inc(a_ot, 4)
            dve.sem_inc(a_gt, 4)
            dve.sem_inc(a_dec, 4)
            dve.sem_inc(m_gt, 2)
            dve.sem_inc(m_og, 2)
            dve.sem_inc(m_st[0], 16)
            dve.sem_inc(m_st[1], 16)
            dve.sem_inc(u_s, 4)
            dve.sem_inc(u_r, 4)

            xt_view = xres[:, :, :].rearrange("p t (a n) -> p (t a) n", a=2)
            for k in range(KX):
                dve.wait_ge(xt_hi, k + 1)
                lo_of(xlo[:, k, :], xt_view[:, k, :], xhi[:, k, :], xt_lo)
            A, B, E, O = bank[0:4], bank[4:8], bank[0::2], bank[1::2]
            dve.wait_ge(aux["const"], 48)
            cos, sin = rope_a[:, 0, :], rope_a[:, 1, :]
            with dve.Fori(0, HA) as h:
                own.enter(h, 17)
                for a in range(2):
                    b0, b1 = B[2 * a][:, :], B[2 * a + 1][:, :]
                    dve.wait_ge(a_qk, 4 * h + (2 * a + 2))
                    if a:
                        dve.wait_ge(a_qklo, 4 * h + 2)
                    own.mark(dve.tensor_tensor(work[:, 0, :], b0, cos, ALU.mult))
                    own.mark(dve.tensor_tensor(work[:, 1, :], b1, sin, ALU.mult))
                    own.mark(dve.tensor_tensor(work[:, 2, :], b1, cos, ALU.mult))
                    own.mark(dve.tensor_tensor(work[:, 3, :], b0, sin, ALU.mult))
                    own.settle()
                    dve.tensor_tensor(work[:, 0, :], work[:, 0, :], work[:, 1, :], ALU.subtract).then_inc(a_q32, 1)
                    dve.tensor_tensor(work[:, 2, :], work[:, 2, :], work[:, 3, :], ALU.add).then_inc(a_q32, 1)
                    for m in range(2):
                        dve.wait_ge(a_qkhi, 4 * h + (2 * a + m + 1))
                        lo_of(qk_lo[:, 2 * a + m, :], work[:, 2 * m, :], qk_hi[:, 2 * a + m, :], a_qklo)
                for q in range(TT):
                    dve.wait_ge(a_vhi, 4 * h + (q + 1))
                    lo_of(v_lo[:, q, :], A[q][:, :], v_hi[:, q, :], a_vlo)
                dve.wait_ge(aux["decay"], 16 * h + 16)
                dve.wait_ge(a_qklo, 4 * h + 4)
                for kt in range(TT):
                    w = SEQ - kt * P
                    dve.wait_ge(a_s, 4 * h + (kt + 1))
                    dve.tensor_tensor(work[:, kt, 0:w], B[kt][:, 0:w], decay[:, 0:w], ALU.mult).then_inc(a_dec, 1)
                for kt in range(TT):
                    w = SEQ - kt * P
                    dve.wait_ge(a_shi, 4 * h + (kt + 1))
                    lo_of(s_lo[:, KT_AT[kt]:KT_AT[kt] + w], work[:, kt, 0:w], s_hi[:, KT_AT[kt]:KT_AT[kt] + w], a_slo)

                def gates(m):
                    dve.wait_ge(a_th, 4 * h + (m + 1))
                    dve.scalar_tensor_tensor(out=gate[:, m, :], in0=gate[:, m, :], scalar=1.0, in1=A[m][:, :],
                                             op0=ALU.add, op1=ALU.mult).then_inc(a_gt, 1)

                gates(0)
                gates(1)
                for q in range(TT):
                    dve.wait_ge(a_o, 4 * h + (q + 1))
                    own.mark(dve.bn_stats(stat[:, q, 0, :], B[q][:, :]))
                own.settle()
                dve.memset(small[:, 3, 0:1], 0.0)
                for q in range(TT):
                    own.mark(dve.bn_aggr(mv[:, q, :], stat[:, q, 0, :]))
                own.settle()
                dve.tensor_scalar(small[:, 0, 0:TT], mv[:, :, 1], LN_EPS, 4.0, ALU.add, ALU.mult).then_inc(a_var, 1)
                dve.wait_ge(a_sd, h + 1)
                own.mark(dve.reciprocal(small[:, 2, 0:TT], small[:, 1, 0:TT]))
                own.settle()
                dve.wait_ge(a_slo, 4 * h + 4)
                for q in range(TT):
                    dve.tensor_scalar(work[:, q, :], B[q][:, :], mv[:, q, 0:1], small[:, 2, q:q + 1], ALU.subtract,
                                      ALU.mult).then_inc(a_on, 1)
                gates(2)
                gates(3)
                dve.wait_ge(a_gt, 4 * h + 8)
                for j in range(VT):
                    dve.wait_ge(a_t, 4 * h + (j + 1))
                    dve.tensor_tensor(oT[:, bass.ds(4 * h + j, 1), :].rearrange("p a n -> p (a n)"), B[j][:, :],
                                      gate[:, j, :], ALU.mult).then_inc(a_ot, 1)
            own.leave(HA)
            project_out(HA * VT, oT, ar_hi, ar_lo, 0)
            dve.wait_ge(aux["rows"], 16)
            dve.wait_ge(aux["x"], 16)
            norms(0, ln=0, gb=rows, centred=oT[:, 0:8, :].rearrange("p (t a) n -> p t (a n)", a=2), round_=1)

            dve.wait_ge(b_w, 1)
            lo_of(wkr_lo[:, :, :], wkr[:, :, :], wkr_hi[:, :, :], b_wl)
            dve.wait_ge(b_css, TT)
            dve.tensor_scalar(small[:, 0, 0:TT], small[:, 3, 0:TT], 1.0 / KVLORA, RMS_EPS, ALU.mult, ALU.add
                              ).then_inc(b_cms, 1)
            dve.wait_ge(b_csd, 1)
            dve.reciprocal(small[:, 2, 0:TT], small[:, 1, 0:TT]).then_inc(b_crs, 1)
            dve.wait_ge(aux["ropeb"], 16)

            def rotate(src, signal):
                own.mark(dve.tensor_tensor(rtmp[:, 0, :], src, rope_b[:, 0, :], ALU.mult))
                for g in range(4):
                    a, b = 32 * g, 32 * (g ^ 1)
                    own.mark(dve.tensor_tensor(rtmp[b:b + 32, 1, :], src[a:a + 32, :], rope_b[a:a + 32, 1, :],
                                               ALU.mult))
                own.settle()
                dve.tensor_tensor(rtmp[:, 0, :], rtmp[:, 0, :], rtmp[:, 1, :], ALU.add).then_inc(signal, 1)

            for j in range(KC):
                dve.wait_ge(b_chi, j + 1)
                lo_scaled(c_lo[:, j, :], E[j][:, :], cols[:, COL_CG + j:COL_CG + j + 1], c_hi[:, j, :], b_clo)
            for q in range(TT):
                dve.wait_ge(b_qss, TT + q + 1)
                own.mark(dve.tensor_tensor(small[:, 0, 4 + q:5 + q], small[:, 3, 4 + q:5 + q], small[:, 3, q:q + 1],
                                           ALU.add))
                own.settle()
                dve.tensor_scalar(small[:, 0, 4 + q:5 + q], small[:, 0, 4 + q:5 + q], 1.0 / QLORA, RMS_EPS, ALU.mult,
                                  ALU.add).then_inc(b_qms, 1)
                dve.wait_ge(b_qsd, q + 1)
                dve.reciprocal(small[:, 2, 4 + q:5 + q], small[:, 1, 4 + q:5 + q]).then_inc(b_qrs, 1)
                dve.wait_ge(b_qrs, q + 1)
                dve.tensor_scalar(q_tok[:, q, 512:768], E[q][:, 0:256], small[:, 2, 4 + q:5 + q], None, ALU.mult
                                  ).then_inc(b_qtl, 1)
            for j in range(KQ):
                dve.wait_ge(b_qhi, j + 1)
                lo_scaled(ql_lo[:, j, :], bank[j][:, :], cols[:, COL_QG + j:COL_QG + j + 1], ql_hi[:, j, :], b_qlo)
            dve.wait_ge(b_kr, 1)
            rotate(bank[7][:, :], b_kr32)
            dve.wait_ge(b_krhi, 1)
            lo_of(kr_lo[:, :], rtmp[:, 0, :], kr_hi[:, :], b_krlo)
            dve.wait_ge(b_krlo, 1)

            with dve.Fori(0, PAIRS // 2) as it:
                own.enter(it, 2 * 21)
                for s in range(2):
                    def c(per, k):
                        return 2 * per * it + (per * s + k)

                    for m in range(2):
                        dve.wait_ge(m_qhi, c(3, m + 1))
                        lo_of(qn_lo[:, m, :], bank[4 + m][:, :], qn_hi[:, m, :], m_qlo)
                    dve.wait_ge(m_q, c(3, 3))
                    rotate(bank[6][:, :], m_qr32)
                    dve.wait_ge(m_qhi, c(3, 3))
                    lo_of(qr_lo[:, :], rtmp[:, 0, :], qr_hi[:, :], m_qlo)
                    for m in range(2):
                        dve.wait_ge(m_kvhi, c(4, m + 1))
                        lo_of(kn_lo[:, m, :], bank[m][:, :], kn_hi[:, m, :], m_kvlo)
                    for m in range(2):
                        dve.wait_ge(m_kvhi, c(4, m + 3))
                        lo_of(vb_lo[:, 2 * m:2 * m + 2, :].rearrange("p t n -> p (t n)"), bank[2 + m][:, :],
                              vb_hi[:, 2 * m:2 * m + 2, :].rearrange("p t n -> p (t n)"), m_kvlo)

                    def softmax(e):
                        for q in range(TT):
                            x = 4 * e + q
                            dve.wait_ge(m_s, c(8, x + 1))
                            own.mark(dve.tensor_reduce(sm[:, 0, x:x + 1], bank[4 + q][:, 0:(q + 1) * P], AX, ALU.max))
                            own.settle()
                            dve.tensor_scalar(sm[:, 1, x:x + 1], sm[:, 0, x:x + 1], -SCALE_B, None, ALU.mult
                                              ).then_inc(m_nb, 1)
                        for q in range(TT):
                            x = 4 * e + q
                            at, w = q * (q + 1) // 2 * P, (q + 1) * P
                            dve.wait_ge(m_exp, c(8, x + 1))
                            own.mark(dve.reciprocal(sm[:, 3, x:x + 1], sm[:, 2, x:x + 1]))
                            own.settle()
                            dve.tensor_scalar(prob[:, at:at + w], prob[:, at:at + w], sm[:, 3, x:x + 1], 0.5,
                                              ALU.mult, ALU.mult).then_inc(m_p, 1)

                    def turned(e):
                        for b in range(3):
                            r = slice((0, 512, 896)[b], (512, 896, 1280)[b])
                            dve.wait_ge(m_pthi, c(6, 3 * e + b + 1))
                            lo_of(pt_lo[:, r], bank[1 + e + b][:, 0:r.stop - r.start], pt_hi[:, r], m_ptlo)

                    def gates(m):
                        dve.wait_ge(m_th, c(2, m + 1))
                        dve.scalar_tensor_tensor(out=gt[:, m, :], in0=gt[:, m, :], scalar=1.0, in1=bank[0][:, :],
                                                 op0=ALU.add, op1=ALU.mult).then_inc(m_gt, 1)

                    def gated(e, src):
                        dve.wait_ge(m_o, c(2, e + 1))
                        dve.wait_ge(m_gt, c(2, e + 3))
                        dve.tensor_tensor(gt[:, e, :], src[:, :], gt[:, e, :], ALU.mult).then_inc(m_og, 1)

                    softmax(0)
                    turned(0)
                    gates(0)
                    softmax(1)
                    gated(0, bank[1])
                    turned(1)
                    gates(1)
                    gated(1, bank[7])
            own.leave(PAIRS // 2)
            first_tiles(bT, br_hi, br_lo, HA * VT)
            project_out(HB, bT, br_hi, br_lo, HA * VT)
            dve.wait_ge(aux["rows2"], 16)
            dve.wait_ge(aux["grow"], 16)
            norms(TT, ln=1, rms=0, gb=rows2, centred=h_tok, result=h_tok, round_=2)

            dve.wait_ge(l_w, 1)
            lo_of(wp_lo[:, :, :], wp[:, :, :], wp_hi[:, :, :], l_wl)
            dve.wait_ge(vst, 16)
            own.mark(dve.memset(upad[:, :, 0:PAD], 0.0))
            own.mark(dve.memset(upad[:, :, PAD + SEQ:], 0.0))
            own.settle()
            dve.wait_ge(aux["edge"], 16)

            def pooled(g):
                dve.wait_ge(l_up, g + 1)
                if g:
                    dve.wait_ge(l_plo, g)
                src, lo, hi = upad[:, g, :], 0, SEQ + 2 * PAD
                for level in range(g + 1):
                    dst = win[:, (g + 1 + level) % 2, :]
                    back = 1 if level == 0 else 2 ** (level - 1)
                    ahead = 0 if level == 0 else back
                    lo, hi = lo + back, hi - ahead
                    own.mark(dve.tensor_tensor(dst[:, lo:hi], src[:, lo - back:hi - back],
                                               src[:, lo + ahead:hi + ahead], ALU.add))
                    own.settle()
                    src = dst
                u = upad[:, g, PAD:PAD + SEQ]
                out_ = win[:, 0, 0:SEQ]
                own.mark(dve.tensor_tensor(src[:, PAD:2 * PAD], src[:, PAD:2 * PAD], edge[:, g, 0:PAD], ALU.mult))
                own.mark(dve.tensor_tensor(src[:, SEQ:SEQ + PAD], src[:, SEQ:SEQ + PAD], edge[:, g, PAD:], ALU.mult))
                own.settle()
                dve.scalar_tensor_tensor(out=out_, in0=src[:, PAD:PAD + SEQ], scalar=1.0 / WINDOWS[g], in1=u,
                                         op0=ALU.mult, op1=ALU.subtract).then_inc(l_pool, 1)

            def pooled_lo(g):
                dve.wait_ge(l_phi, g + 1)
                lo_of(pool_lo[:, :], win[:, 0, 0:SEQ], pool_hi[:, :], l_plo)

            pooled(0)
            pooled_lo(0)
            pooled(1)
            for m in range(4):
                dve.wait_ge(l_qhi, m + 1)
                lo_of(by_block(nq_lo[:, m, :]), from_rows(E[m][:, :]), by_block(nq_hi[:, m, :]), l_qlo)
            def keys(m):
                dve.wait_ge(l_qhi, m + 5)
                lo_of(nk_lo[:, m, :], O[m][:, :], nk_hi[:, m, :], l_qlo)
                if m < 3:
                    dve.wait_ge(l_mix, m + 1)
                    pooled_lo(m + 1)
                if m < 2:
                    pooled(m + 2)

            for m in range(3):
                keys(m)

            dve.wait_ge(aux["bias"], 16)
            dve.wait_ge(l_plo, 4)
            for i in range(len(steps) + 2):
                if i == 2:
                    keys(3)
                    dve.wait_ge(l_bhi, 2)
                    lo_of(xlo[:, 1, :], vband[:, 1, :], xhi[:, 1, :], l_blo1)
                if i == len(steps) + 1:
                    first_tiles(mixT, cr_hi, cr_lo, HA * VT + HB)
                if i < len(steps):
                    hp, j = steps[i]
                    at = BAND_START[j] - BLK * j + 16
                    dve.wait_ge(e_s, i + 1)
                    if i >= 3:
                        dve.wait_ge(e_t, i - 2)
                    for e in range(2):
                        last = dve.scalar_tensor_tensor(
                            out=nt[:, i % 3, e, :].rearrange("p (r c) -> p r c", r=ROWS),
                            in0=bank[2 * (i % 2) + e][:, 0:256].rearrange("p (r c) -> p r c", r=ROWS),
                            scalar=SCALE_N, in1=bias[:, 2 * hp + e, :, at:at + BAND], op0=ALU.mult, op1=ALU.add)
                        if e == 0:
                            own.mark(last)
                        else:
                            last.then_inc(e_tk, 1)
                    own.settle()
                    dve.wait_ge(e_tk, i + 1)
                    dve.tensor_reduce(nsm[:, i % 3, 0, :], nt[:, i % 3, :, :], AX, ALU.max, negate=True
                                      ).then_inc(e_nb, 1)
                if 1 <= i <= len(steps):
                    m = i - 1
                    dve.wait_ge(e_exp, 2 * m + 2)
                    dve.reciprocal(nsm[:, m % 3, 2, :], nsm[:, m % 3, 1, :]).then_inc(e_rc, 1)
                    dve.wait_ge(e_rc, m + 1)
                    dve.tensor_scalar(nt[:, m % 3, 1, :], nt[:, m % 3, 1, :], nsm[:, m % 3, 2, 1:2], None, ALU.mult
                                      ).then_inc(e_q, 1)
                if i >= 2:
                    m = i - 2
                    dve.wait_ge(e_thi, m + 1)
                    lo_of(npt_lo[:, m % 2, :], bank[4 + m % 2][:, :], npt_hi[:, m % 2, :], e_tlo)
            project_out(KX, mixT, cr_hi, cr_lo, HA * VT + HB)
            dve.wait_ge(aux["grow"], 32)
            norms(2 * TT, rms=1, result=h2_tok, round_=3)

            def squared(m, i):
                dve.wait_ge(u_r, 4 * i + (m + 5))
                dve.tensor_tensor(hid[:, bass.ds(4 * i + m, 1), :].rearrange("p a n -> p (a n)"), relu[:, m, :],
                                  relu[:, m, :], ALU.mult).then_inc(u_s, 1)

            with dve.Fori(0, KF // 4 - 1) as i:
                for m in range(4):
                    squared(m, i)
            squared(0, KF // 4 - 1)
            squared(1, KF // 4 - 1)
            first_tiles(hid, dr_hi, dr_lo, HA * VT + HB + KX)
            squared(2, KF // 4 - 1)
            squared(3, KF // 4 - 1)
            project_out(KF, hid, dr_hi, dr_lo, HA * VT + HB + KX)
            dve.wait_ge(aux["grow"], 48)
            norms(3 * TT, rms=2, result=xres)


def panels(w, nk, width):
    k, n = w.shape
    x = w.reshape(k // (nk * P), nk, P, n // width, width).transpose(3, 0, 2, 1, 4)
    return x.reshape(-1, P, nk * width)


def kernel(**inputs):
    import concourse.bacc as bacc
    from concourse.bass_utils import run_bass_kernel_spmd

    f = {k: np.asarray(v) for k, v in inputs.items()}
    a_in, b_in, n_in = f["a_w_in"][0], f["b_w_in"][0], f["w_in_2"][0]
    groups = []
    for h in range(HA):
        q, k = a_in[:, h * DKA:(h + 1) * DKA], a_in[:, (HA + h) * DKA:(HA + h + 1) * DKA]
        v = a_in[:, 2 * HA * DKA + h * DVA:2 * HA * DKA + (h + 1) * DVA]
        g = a_in[:, 2 * HA * DKA + HA * DVA + h * DVA:2 * HA * DKA + HA * DVA + (h + 1) * DVA]
        groups += [panels(q, KX, 256), panels(k, KX, 256), panels(v, 4, 512), panels(g, KX, 256)]
    groups += [panels(f["a_w_out"][0], 2, DM)]
    groups += [panels(f["kv_w_down"][:, :KVLORA], 4, 512), panels(b_in[:, :512], 4, 512),
               panels(b_in[:, 512:QLORA], KX, 256)]
    uq = f["b_w_uq"][0].reshape(QLORA, HB, NOPE + ROPE)
    up = f["kv_w_up"].reshape(KVLORA, HB, NOPE + VH)
    for n in range(PAIRS):
        a, b = 2 * n, 2 * n + 1
        groups += [panels(np.concatenate([uq[:, a, :NOPE], uq[:, b, :NOPE], uq[:, a, NOPE:], uq[:, b, NOPE:]], 1),
                          KQ, 384),
                   panels(np.concatenate([up[:, a, :NOPE], up[:, b, :NOPE], up[:, a, NOPE:], up[:, b, NOPE:]], 1),
                          KC, 512),
                   panels(b_in[:, QLORA + n * 256:QLORA + (n + 1) * 256], KX, 256)]
    groups += [panels(f["b_w_out"][0], 2, DM)]
    groups += [panels(n_in[:, 1536:2048], 4, 512), panels(n_in[:, :512], KX, 256), panels(n_in[:, 512:1536], KX, 256)]
    groups += [panels(f["w_out_2"][0], 2, DM), panels(f["w_up_2"][0], KX, 256), panels(f["w_down_2"][0], 2, DM)]
    w = np.zeros((PANELS, P, PANEL), np.float32)
    at = 0
    for g in groups:
        w[at:at + len(g), :, :g.shape[2]] = g
        at += len(g)
    assert at == PANELS

    def column(v):
        return v.reshape(-1, P).T

    x = f["x"].reshape(SEQ, DM)
    a = {"w": w, "x": x.reshape(TT, P, DM).transpose(1, 0, 2), "xT": x.T.reshape(KX, P, SEQ).transpose(1, 0, 2)}
    a["cols"] = np.concatenate([column(f["kv_norm"]), column(f["b_q_norm"][0]), column(f["pool_scale_2"][0])], 1)
    a["ln"] = np.broadcast_to(np.stack([f["ln_g"], f["ln_b"]], 1)[:, None], (2, P, 2, DM))
    a["grow"] = np.broadcast_to(np.stack([f["norm_mix_g_2"][0], f["norm_mlp_g_2"][0], f["final_g_2"]])[:, None],
                                (3, P, DM))
    kr = f["kv_w_down"][:, KVLORA:]
    a["wkr"] = np.concatenate([kr, kr], 1).reshape(KX, P, P).transpose(1, 0, 2)
    a["wp"] = f["w_pool_2"][0].transpose(1, 0, 2)
    rpb = np.pad(f["rpb_2"][0], ((0, 0), (0, 0), (16, 16)))
    strip = np.zeros((ROWS, BLK, HN, ROWS, BIAS_W), np.float32)
    for r in range(ROWS):
        for c in range(BLK):
            strip[r, c] = rpb[:, 7 - r:7 - r + ROWS, 15 - c:15 - c + BIAS_W]
    a["bias"] = strip.reshape(P, HN, ROWS, BIAS_W)

    def angles(half):
        inv = np.float32(10000.0) ** (-np.arange(half, dtype=np.float32) / np.float32(half))
        return (inv[:, None] * np.arange(SEQ, dtype=np.float32)[None, :]).astype(np.float64)

    ang = angles(DKA // 2)
    a["rope_a"] = np.stack([np.cos(ang), np.sin(ang)], 1)
    ang = np.tile(angles(ROPE // 2), (4, 1))
    sign = np.where(np.arange(P) % ROPE < ROPE // 2, 1.0, -1.0)[:, None]
    a["rope_b"] = np.stack([np.cos(ang), np.sin(ang) * sign], 1)
    dist = np.arange(SEQ)[None, :] - np.arange(P)[:, None]
    log_gamma = np.log1p(-np.exp2(-5.0 - np.arange(HA)))
    a["decay"] = np.where(dist >= 0, np.exp(np.maximum(dist, 0)[None] * log_gamma[:, None, None]), 0.0) * DKA ** -0.5
    a["ident"] = np.eye(P)
    a["mask"] = np.where(np.arange(P)[None, :] > np.arange(P)[:, None], MASKED, 0.0)
    q = np.arange(P) % BLK
    nmask = np.zeros((P, NBLK, BAND))
    for j in range(NBLK):
        c0 = np.clip(j * BLK + q - 8, 0, GRID - BLK)[:, None]
        key = BAND_START[j] + np.arange(BAND)[None, :]
        nmask[:, j] = np.where((key >= c0) & (key < c0 + BLK), 0.0, MASKED)
    a["nmask"] = nmask
    tok = np.arange(SEQ)
    edge = np.zeros((4, 2 * PAD))
    for g, wd in enumerate(WINDOWS):
        count = np.clip(tok - wd // 2 + wd, 0, SEQ) - np.clip(tok - wd // 2, 0, SEQ)
        ratio = wd / count
        edge[g] = np.concatenate([ratio[:PAD], ratio[-PAD:]])
    a["edge"] = np.broadcast_to(edge, (P, 4, 2 * PAD))

    nc = bacc.Bacc("TRN2", target_bir_lowering=False, num_devices=1)
    arrays, t = {}, {}
    for name, v in a.items():
        v = np.ascontiguousarray(v, dtype=np.float32)
        arrays[f"in_{name}"] = v
        t[name] = nc.dram_tensor(f"in_{name}", v.shape, F32, kind="ExternalInput").ap()
    t["o_spill"] = nc.dram_tensor("o_spill", (HB, P, SEQ), F32).ap()
    t["v_spill"] = nc.dram_tensor("v_spill", (SEQ, SEQ), F32).ap()
    out = nc.dram_tensor("out_0", (SEQ, DM), F32, kind="ExternalOutput").ap()
    program(nc, t, out)
    r = run_bass_kernel_spmd(nc, [arrays], core_ids=[0])
    return r.results[0]["out_0"].reshape(1, SEQ, DM)
```

```python
from contextlib import ExitStack

import numpy as np

import concourse.bass as bass
from concourse import mybir

F32 = mybir.dt.float32
F32R = mybir.dt.float32r
BF16 = mybir.dt.bfloat16
ALU = mybir.AluOpType
ACT = mybir.ActivationFunctionType
AX = mybir.AxisListType.X

P = 128
SEQ = 512
DM = 1024
TT = SEQ // P
KX = DM // P
ALPHA = 4.0 ** 0.25
LN_EPS = 1e-5
RMS_EPS = 1e-6
MASKED = -1e30

HA, DKA, DVA = 4, 256, 512
VT = DVA // P
HB, NOPE, ROPE, VH = 16, 128, 64, 128
QLORA, KVLORA = 768, 512
KQ, KC = QLORA // P, KVLORA // P
PAIRS = HB // 2
SCALE_B = float(NOPE + ROPE) ** -0.5
WINDOWS = (2, 4, 8, 16)
HN, DHN = 8, 64
GRID = 64
ROWS = SEQ // GRID
BLK = 16
BAND = 32
NBLK = GRID // BLK
SCALE_N = float(DHN) ** -0.5
BAND_START = [min(max(j * BLK - 8, 0), GRID - BAND) for j in range(NBLK)]
BIAS_W = BAND + 16
DFF = 4 * DM
KF = DFF // P
PAD = 8

PANEL = 2304
PAN = 2048
A0 = 0
AO = A0 + 6 * HA
B0 = AO + 8
M0 = B0 + 5
BO = M0 + 3 * PAIRS
L0 = BO + 8
WO = L0 + 8
UP = WO + 4
DN = UP + 16
PANELS = DN + 16

COL_CG, COL_QG, COL_PS = 0, KC, KC + KQ
COLS = COL_PS + 4

KT_AT = [0, 512, 896, 1152]
TRI = 1280


class Own:

    def __init__(self, eng, sem):
        self.eng, self.sem, self.n, self.i, self.per = eng, sem, 0, 0, 0

    def mark(self, ins):
        ins.then_inc(self.sem, 1)
        self.n += 1

    def settle(self):
        self.eng.wait_ge(self.sem, self.i * self.per + self.n)

    def enter(self, i, per):
        self.i, self.per, self.first = i, per, self.n

    def leave(self, times):
        assert self.n - self.first == self.per, (self.n - self.first, self.per)
        self.n, self.i, self.per = self.first + self.per * times, 0, 0


def program(nc, t, out):
    with ExitStack() as ctx:
        def sb(name, shape, dt=F32, where=ctx):
            return where.enter_context(nc.sbuf_tensor(name, shape, dt))

        def sem(name):
            return ctx.enter_context(nc.semaphore(name))

        bank = [ctx.enter_context(nc.psum_tensor(f"bank{i}", [P, 512], F32)) for i in range(8)]

        stage = [sb(f"stage{i}", [P, PANEL]) for i in range(2)]
        whi = [sb(f"whi{i}", [P, PANEL], F32R) for i in range(2)]
        wlo = [sb(f"wlo{i}", [P, PANEL], F32R) for i in range(2)]
        xhi = sb("xhi", [P, KX, SEQ], F32R)
        xlo = sb("xlo", [P, KX, SEQ], F32R)
        xres = sb("xres", [P, TT, DM])
        grow = sb("grow", [P, DM])
        ident = sb("ident", [P, P])
        cols = sb("cols", [P, COLS])
        stat = sb("stat", [P, TT, 2, 6])
        mv = sb("mv", [P, TT, 2])
        small = sb("small", [P, 4, 8])
        eps = sb("eps", [P, 2])
        first_layer = ctx.enter_context(ExitStack())

        oT = sb("oT", [P, HA * VT, SEQ], F32, first_layer)
        with ExitStack() as h:
            qk_hi = sb("qk_hi", [P, 4, SEQ], F32R, h)
            qk_lo = sb("qk_lo", [P, 4, SEQ], F32R, h)
            v_hi = sb("v_hi", [P, TT, DVA], F32R, h)
            v_lo = sb("v_lo", [P, TT, DVA], F32R, h)
            gate = sb("gate", [P, VT, SEQ], F32, h)
            s_hi = sb("s_hi", [P, TRI], F32R, h)
            s_lo = sb("s_lo", [P, TRI], F32R, h)
            decay = sb("decay", [P, SEQ], F32, h)
            rope_a = sb("rope_a", [P, 2, SEQ], F32, h)
            work = sb("work", [P, 4, SEQ], F32, h)
        with ExitStack() as h:
            ar_hi = sb("ar_hi", [P, 4, SEQ], F32R, h)
            ar_lo = sb("ar_lo", [P, 4, SEQ], F32R, h)
            rows = sb("rows", [P, 2, DM], F32, h)
        first_layer.close()
        with ExitStack() as h:
            c_hi = sb("c_hi", [P, KC, SEQ], F32R, h)
            c_lo = sb("c_lo", [P, KC, SEQ], F32R, h)
            ql_hi = sb("ql_hi", [P, KQ, SEQ], F32R, h)
            ql_lo = sb("ql_lo", [P, KQ, SEQ], F32R, h)
            kr_hi = sb("kr_hi", [P, SEQ], F32R, h)
            kr_lo = sb("kr_lo", [P, SEQ], F32R, h)
            rope_b = sb("rope_b", [P, 2, SEQ], F32, h)
            id_b = sb("id_b", [P, P], BF16, h)
            mask_b = sb("mask_b", [P, P], BF16, h)
            rtmp = sb("rtmp", [P, 2, SEQ], F32, h)
            with ExitStack() as g:
                c_tok = sb("c_tok", [P, TT, KVLORA], F32, g)
                q_tok = sb("q_tok", [P, TT, QLORA], F32, g)
                wkr = sb("wkr", [P, KX, P], F32, g)
                wkr_hi = sb("wkr_hi", [P, KX, P], F32R, g)
                wkr_lo = sb("wkr_lo", [P, KX, P], F32R, g)
                mask_f = sb("mask_f", [P, P], F32, g)
            with ExitStack() as g:
                qn_hi = sb("qn_hi", [P, 2, SEQ], F32R, g)
                qn_lo = sb("qn_lo", [P, 2, SEQ], F32R, g)
                qr = sb("qr", [P, 2, SEQ], F32R, g)
                kn_hi = sb("kn_hi", [P, 2, SEQ], F32R, g)
                kn_lo = sb("kn_lo", [P, 2, SEQ], F32R, g)
                vb_hi = sb("vb_hi", [P, TT, 2 * VH], F32R, g)
                vb_lo = sb("vb_lo", [P, TT, 2 * VH], F32R, g)
                gt = sb("gt", [P, 2, SEQ], F32, g)
                prob = sb("prob", [P, TRI], F32, g)
                pt_hi = sb("pt_hi", [P, TRI], F32R, g)
                pt_lo = sb("pt_lo", [P, TRI], F32R, g)
                sm = sb("sm", [P, 4, 8], F32, g)
        with ExitStack() as h:
            bT = sb("bT", [P, HB, SEQ], F32, h)
            br_hi = sb("br_hi", [P, 4, SEQ], F32R, h)
            br_lo = sb("br_lo", [P, 4, SEQ], F32R, h)
            rows2 = sb("rows2", [P, 2, DM], F32, h)
        with ExitStack() as h:
            mixT = sb("mixT", [P, KX, SEQ], F32, h)
            with ExitStack() as f:
                h_tok = sb("h_tok", [P, TT, DM], F32, f)
                vband = h_tok[:, :, :].rearrange("p t (a n) -> p (t a) n", a=2)
                nq_hi = sb("nq_hi", [P, 4, SEQ], F32R, f)
                nq_lo = sb("nq_lo", [P, 4, SEQ], F32R, f)
                nk_hi = sb("nk_hi", [P, 4, SEQ], F32R, f)
                nk_lo = sb("nk_lo", [P, 4, SEQ], F32R, f)
                bias = sb("bias", [P, HN, ROWS, BIAS_W], F32, f)
                nmask = sb("nmask", [P, NBLK, BAND], F32, f)
                nmask_b = sb("nmask_b", [P, NBLK, BAND], BF16, f)
                id_n = sb("id_n", [P, P], BF16, f)
                nsm = sb("nsm", [P, 3, 3, 2], F32, f)
                with ExitStack() as g:
                    v_tok = sb("v_tok", [P, TT, SEQ], F32, g)
                with ExitStack() as g:
                    upad = sb("upad", [P, 4, SEQ + 2 * PAD], F32, g)
                    win = sb("win", [P, 2, SEQ + 2 * PAD], F32, g)
                    pool_hi = sb("pool_hi", [P, SEQ], F32R, g)
                    pool_lo = sb("pool_lo", [P, SEQ], F32R, g)
                    wp = sb("wp", [P, 4, P], F32, g)
                    wp_hi = sb("wp_hi", [P, 4, P], F32R, g)
                    wp_lo = sb("wp_lo", [P, 4, P], F32R, g)
                    edge = sb("edge", [P, 4, 2 * PAD], F32, g)
                with ExitStack() as g:
                    nt = sb("nt", [P, 3, 2, 256], F32, g)
                    npt_hi = sb("npt_hi", [P, 2, SEQ], F32R, g)
                    npt_lo = sb("npt_lo", [P, 2, SEQ], F32R, g)
            with ExitStack() as f:
                h2_tok = sb("h2_tok", [P, TT, DM], F32, f)
                cr_hi = sb("cr_hi", [P, 4, SEQ], F32R, f)
                cr_lo = sb("cr_lo", [P, 4, SEQ], F32R, f)
        with ExitStack() as h:
            hid = sb("hid", [P, KF, SEQ], F32, h)
            relu = sb("relu", [P, 4, SEQ], F32, h)
            dr_hi = sb("dr_hi", [P, 4, SEQ], F32R, h)
            dr_lo = sb("dr_lo", [P, 4, SEQ], F32R, h)

        landed = [sem(f"landed{i}") for i in range(2)]
        first = sem("first")
        w_hi = sem("w_hi")
        w_lo = sem("w_lo")
        half_done = sem("half_done")
        aux = {n: sem(f"ld_{n}") for n in ("x", "const", "decay", "kr", "rows", "rows2", "ropeb", "bias",
                                           "edge", "wp", "nmask", "grow")}
        xt_ld = [sem(f"xt_ld{k}") for k in range(KX)]
        vld = [sem(f"vld{i}") for i in range(8)]
        bld = [sem(f"bld{i}") for i in range(4)]
        m_st = [sem("m_st0"), sem("m_st1")]
        dv = sem("dve_step")
        vst = sem("vst")
        xt_t = sem("xt_t")
        xt_hi = sem("xt_hi")
        xt_lo = sem("xt_lo")
        y_done = sem("y_done")
        ar_h = sem("ar_h")
        ar_l = sem("ar_l")
        n_mu = sem("n_mu")
        n_ss = sem("n_ss")
        n_sd = sem("n_sd")
        n_x = sem("n_x")
        r_ss = sem("r_ss")
        r_sd = sem("r_sd")
        r_h = sem("r_h")
        a_qk = sem("a_qk")
        a_q32 = sem("a_q32")
        a_qkhi = sem("a_qkhi")
        a_qklo = sem("a_qklo")
        a_v = sem("a_v")
        a_vhi = sem("a_vhi")
        a_vlo = sem("a_vlo")
        a_s = sem("a_s")
        a_dec = sem("a_dec")
        a_shi = sem("a_shi")
        a_slo = sem("a_slo")
        a_g = sem("a_g")
        a_th = sem("a_th")
        a_gt = sem("a_gt")
        a_o = sem("a_o")
        a_var = sem("a_var")
        a_sd = sem("a_sd")
        a_on = sem("a_on")
        a_t = sem("a_t")
        a_ot = sem("a_ot")
        b_w = sem("b_w")
        b_wl = sem("b_wl")
        b_c = sem("b_c")
        b_css = sem("b_css")
        b_cms = sem("b_cms")
        b_csd = sem("b_csd")
        b_crs = sem("b_crs")
        b_ctok = sem("b_ctok")
        b_ct = sem("b_ct")
        b_chi = sem("b_chi")
        b_clo = sem("b_clo")
        b_ql = sem("b_ql")
        b_qss = sem("b_qss")
        b_qms = sem("b_qms")
        b_qsd = sem("b_qsd")
        b_qrs = sem("b_qrs")
        b_qtok = sem("b_qtok")
        b_qtl = sem("b_qtl")
        b_qt = sem("b_qt")
        b_qhi = sem("b_qhi")
        b_qlo = sem("b_qlo")
        b_kr = sem("b_kr")
        b_kr32 = sem("b_kr32")
        b_krhi = sem("b_krhi")
        b_krlo = sem("b_krlo")
        m_q = sem("m_q")
        m_qr32 = sem("m_qr32")
        m_qhi = sem("m_qhi")
        m_qlo = sem("m_qlo")
        m_kv = sem("m_kv")
        m_kvhi = sem("m_kvhi")
        m_kvlo = sem("m_kvlo")
        m_s = sem("m_s")
        m_nb = sem("m_nb")
        m_exp = sem("m_exp")
        m_p = sem("m_p")
        m_t = sem("m_t")
        m_pthi = sem("m_pthi")
        m_ptlo = sem("m_ptlo")
        m_g = sem("m_g")
        m_th = sem("m_th")
        m_gt = sem("m_gt")
        m_o = sem("m_o")
        m_og = sem("m_og")
        l_mk = sem("l_mk")
        l_w = sem("l_w")
        l_wl = sem("l_wl")
        l_v = sem("l_v")
        l_vt = sem("l_vt")
        l_u = sem("l_u")
        l_up = sem("l_up")
        l_q = sem("l_q")
        l_qhi = sem("l_qhi")
        l_qlo = sem("l_qlo")
        l_pool = sem("l_pool")
        l_phi = sem("l_phi")
        l_plo = sem("l_plo")
        l_mix = sem("l_mix")
        l_mo = sem("l_mo")
        l_bhi = sem("l_bhi")
        l_blo = sem("l_blo")
        l_blo1 = sem("l_blo1")
        e_s = sem("e_s")
        e_tk = sem("e_tk")
        e_nb = sem("e_nb")
        e_exp = sem("e_exp")
        e_rc = sem("e_rc")
        e_p = sem("e_p")
        e_q = sem("e_q")
        e_t = sem("e_t")
        e_thi = sem("e_thi")
        e_tlo = sem("e_tlo")
        e_o = sem("e_o")
        e_oc = sem("e_oc")
        u_m = sem("u_m")
        u_r = sem("u_r")
        u_s = sem("u_s")
        o_st = sem("o_st")
        steps = [(hp, j) for j in range(NBLK) for hp in range(HN // 2)]

        def by_block(x):
            return x.rearrange("p (j r c) -> p j r c", j=NBLK, r=ROWS)

        def from_rows(x):
            return x.rearrange("p (r j c) -> p j r c", j=NBLK, r=ROWS)

        def split_dots(pe, dst, a_hi, a_lo, b_hi, b_lo, start, stop):
            pe.matmul(dst, a_hi, b_hi, start=start, stop=False)
            pe.matmul(dst, a_hi, b_lo, start=False, stop=False)
            return pe.matmul(dst, a_lo, b_hi, start=False, stop=stop)

        block = ctx.enter_context(nc.Block())

        @block.sync
        def _(sp):
            def load(p, width=PAN, n=0):
                if p >= 2:
                    sp.wait_ge(w_lo, 2 * n + 2 * (p - 1))
                sp.dma_start(stage[p % 2][:, 0:width],
                             t["w"][bass.ds(n + p, 1), :, 0:width].rearrange("a p n -> (a p) n")
                             ).then_inc(landed[p % 2], 16)

            xt_view = xres[:, :, :].rearrange("p t (a n) -> p (t a) n", a=2)
            sp.dma_start(stage[0][:, 0:PAN // 2], t["w"][0, :, 0:PAN // 2]).then_inc(first, 16)
            for k in range(KX):
                if k == 4:
                    sp.dma_start(stage[0][:, PAN // 2:PAN], t["w"][0, :, PAN // 2:PAN]).then_inc(landed[0], 16)
                sp.dma_start(xt_view[:, k, :], t["xT"][:, k, :]).then_inc(xt_ld[k], 16)
            load(1)
            sp.dma_start(rope_a[:, :, :], t["rope_a"]).then_inc(aux["const"], 16)
            sp.dma_start(ident[:, :], t["ident"]).then_inc(aux["const"], 16)
            sp.dma_start(cols[:, :], t["cols"]).then_inc(aux["const"], 16)
            sp.dma_start(grow[:, :], t["grow"][0]).then_inc(aux["grow"], 16)
            with sp.Fori(0, (M0 - 3) // 2) as i:
                for j in range(2):
                    load(2 + j, PAN, 2 * i)
            load(M0 - 1)

            def store(pair):
                for e in range(2):
                    sp.wait_ge(m_og, 2 * pair + (e + 3))
                    sp.dma_start(t["o_spill"][bass.ds(2 * pair + e, 1), :, :].rearrange("a p n -> (a p) n"),
                                 gt[:, e, :]).then_inc(m_st[e], 16)

            for j in range(6):
                load(M0 + j, PANEL if j % 3 == 0 else PAN)
            with sp.Fori(1, PAIRS // 2) as i:
                for s in range(2):
                    load(M0 + 3 * s, PANEL, 6 * i)
                    store(2 * i + (s - 2))
                    load(M0 + 3 * s + 1, PAN, 6 * i)
                    load(M0 + 3 * s + 2, PAN, 6 * i)
            load(BO)
            store(PAIRS - 2)
            load(BO + 1)
            sp.wait_ge(m_kv, 4 * PAIRS)
            for c4 in range(4):
                if c4 == 3:
                    load(BO + 2)
                    store(PAIRS - 1)
                for e in range(2):
                    sp.wait_ge(m_st[e], 32 * (c4 + 1) + 16)
                sp.dma_start(bT[:, 4 * c4:4 * c4 + 4, :], t["o_spill"][4 * c4:4 * c4 + 4, :, :].rearrange(
                    "k p n -> p k n")).then_inc(bld[c4], 16)
            with sp.Fori(0, (PANELS - BO - 4) // 2) as i:
                for j in range(2):
                    load(BO + 3 + j, PAN, 2 * i)
            load(PANELS - 1)
            for q in range(TT):
                sp.wait_ge(r_h, 2 * TT + q + 1)
                sp.dma_start(out[q * P:(q + 1) * P, :], xres[:, q, :]).then_inc(o_st, 16)
            sp.wait_ge(o_st, 16 * TT)

        @block.gpsimd
        def _(pool):
            def split_lo(p, width=PAN, n=0):
                for s in range(2):
                    pool.wait_ge(w_hi, 2 * n + (2 * p + s + 1))
                    r = slice(s * width // 2, (s + 1) * width // 2)
                    pool.tensor_tensor(wlo[p % 2][:, r], stage[p % 2][:, r], whi[p % 2][:, r].bitcast(F32),
                                       ALU.subtract).then_inc(w_lo, 1)

            with pool.Fori(0, AO // 2) as i:
                for j in range(2):
                    split_lo(j, PAN, 2 * i)
            split_lo(AO)
            for kk in range(4):
                pool.wait_ge(ar_h, kk + 1)
                pool.tensor_tensor(ar_lo[:, kk, :], oT[:, kk, :], ar_hi[:, kk, :].bitcast(F32), ALU.subtract
                                   ).then_inc(ar_l, 1)
            split_lo(AO + 1)
            with pool.Fori(0, (M0 - AO - 3) // 2) as i:
                for j in range(2):
                    split_lo(AO + 2 + j, PAN, 2 * i)
            split_lo(M0 - 1)
            with pool.Fori(0, PAIRS // 2) as i:
                for j in range(6):
                    split_lo(M0 + j, PANEL if j % 3 == 0 else PAN, 6 * i)
            with pool.Fori(0, (WO - BO) // 2) as i:
                for j in range(2):
                    split_lo(BO + j, PAN, 2 * i)
            split_lo(WO)

            def band_lo(b):
                pool.wait_ge(l_bhi, b + 1)
                pool.tensor_tensor(xlo[:, b, :], vband[:, b, :], xhi[:, b, :].bitcast(F32), ALU.subtract
                                   ).then_inc(l_blo, 1)

            for m in range(len(steps)):
                pool.wait_ge(e_rc, m + 1)
                pool.tensor_scalar(nt[:, m % 3, 0, :], nt[:, m % 3, 0, :], nsm[:, m % 3, 2, 0:1], None, ALU.mult
                                   ).then_inc(e_p, 1)
                if m == 1:
                    band_lo(0)
                if 2 <= m < 8:
                    band_lo(m)
                if 9 <= m < 13:
                    r = slice((m - 9) * 512, (m - 8) * 512)
                    w = (WO + 1) % 2
                    pool.wait_ge(w_hi, 2 * (WO + 1) + (m - 9) // 2 + 1)
                    last = pool.tensor_tensor(wlo[w][:, r], stage[w][:, r], whi[w][:, r].bitcast(F32), ALU.subtract)
                    if m in (10, 12):
                        last.then_inc(w_lo, 1)
            with pool.Fori(0, (PANELS - WO - 2) // 2) as i:
                for j in range(2):
                    split_lo(WO + 2 + j, PAN, 2 * i)

        @block.tensor
        def _(pe):
            def panel(p, nk):
                return [w[p % 2][:, 0:PANEL // nk * nk if nk == KQ else PAN].rearrange("p (k n) -> p k n", k=nk)
                        for w in (whi, wlo)]

            def need(p, n, nk, k):
                if k in (0, nk // 2):
                    pe.wait_ge(w_lo, 2 * n + (2 * p + 1 + (k > 0)))

            def tiles(p, n, nk, parts, moving, lo, hi, before, signal, each=False):
                wh, wl = panel(p, nk)
                for m in range(lo, hi):
                    before(m)
                    for k in range(nk):
                        if m == lo:
                            need(p, n, nk, k)
                        if each and m == 0:
                            pe.wait_ge(xt_lo, k + 1)
                        c = slice(m * P, (m + 1) * P)
                        last = split_dots(pe, parts[m][:, :], wh[:, k, c], wl[:, k, c],
                                          moving[0][:, k, :], moving[1][:, k, :], k == 0, k == nk - 1)
                    last.then_inc(signal, 1)

            def token_tiles(p, n, nk, k0, dst, start, stop, before, signal):
                wh, wl = panel(p, nk)
                for q in range(TT):
                    before(q)
                    for k in range(nk):
                        if q == 0:
                            need(p, n, nk, k)
                        r = slice(q * P, (q + 1) * P)
                        last = split_dots(pe, dst(q), xhi[:, k0 + k, r], xlo[:, k0 + k, r],
                                          wh[:, k, :], wl[:, k, :], start and k == 0, stop and k == nk - 1)
                    if stop:
                        last.then_inc(signal, 1)
                if not stop:
                    last.then_inc(half_done, 1)

            def nothing(_):
                pass

            def turn_x(src, ready, count, q):
                pe.wait_ge(ready, count + q + 1)
                for k in range(KX):
                    last = pe.transpose(bank[2 * q + k // 4][:, k % 4 * P:k % 4 * P + P],
                                        src[:, q, k * P:(k + 1) * P], ident[:, :])
                    if k % 4 == 3:
                        last.then_inc(xt_t, 1)

            def first_product(src, ready, count, round_, p, signal, turned=False):
                def half(c, q, k0=0, k1=4):
                    wh, wl = panel(p + c, 4)
                    pe.wait_ge(xt_lo, KX * round_ + 2 * q + c + 1)
                    for k in range(k0, k1):
                        if q == 0:
                            need(p + c, 0, 4, k)
                        r = slice(q * P, (q + 1) * P)
                        last = split_dots(pe, bank[2 * q][:, :], xhi[:, 4 * c + k, r], xlo[:, 4 * c + k, r],
                                          wh[:, k, :], wl[:, k, :], c == 0 and k == 0, c == 1 and k == 3)
                    return last

                def turn(q):
                    turn_x(src, ready, count, q)

                if not turned:
                    turn(0)
                half(0, 0)
                turn(1)
                half(1, 0).then_inc(signal, 1)
                half(0, 1)
                turn(2)
                half(1, 1).then_inc(signal, 1)
                half(0, 2)
                turn(3)
                half(1, 2, 0, 2)
                half(0, 3).then_inc(half_done, 1)
                half(1, 2, 2, 4).then_inc(signal, 1)
                half(1, 3).then_inc(signal, 1)

            def project_out(p0, nk, hi, lo, a0, free=None, turn=None):
                def half(n, j, first):
                    wh, wl = panel(p0 + j, 2)
                    for b in range(2):
                        kk = 2 * j + b
                        need(p0 + j, n, 2, b)
                        pe.wait_ge(ar_l, 2 * n + (a0 + kk + 1))
                        for q in range(TT):
                            if first and b == 0 and free:
                                free(q)
                            for c in range(2):
                                w = slice(c * 512, c * 512 + 512)
                                r = slice(q * P, (q + 1) * P)
                                last = split_dots(pe, bank[2 * q + c][:, :], hi[:, kk % 4, r], lo[:, kk % 4, r],
                                                  wh[:, b, w], wl[:, b, w], first and kk == 0, False)
                    last.then_inc(half_done, 1)

                half(0, 0, True)
                if nk > 8:
                    with pe.Fori(0, nk // 4 - 1) as i:
                        half(2 * i, 1, False)
                        half(2 * i, 2, False)
                else:
                    half(0, 1, False)
                    half(0, 2, False)
                wh, wl = panel(p0 + nk // 2 - 1, 2)
                pe.wait_ge(ar_l, a0 + nk)
                for q in range(TT):
                    for c in range(2):
                        if q == TT - 1 and turn:
                            turn(c)
                        for kk in range(2):
                            if q == 0 and c == 0:
                                need(p0 + nk // 2 - 1, 0, 2, kk)
                            w = slice(c * 512, c * 512 + 512)
                            r = slice(q * P, (q + 1) * P)
                            last = split_dots(pe, bank[2 * q + c][:, :], hi[:, 2 + kk, r], lo[:, 2 + kk, r],
                                              wh[:, kk, w], wl[:, kk, w], False, kk == 1)
                        last.then_inc(y_done, 1)

            A, B, E, O = bank[0:4], bank[4:8], bank[0::2], bank[1::2]
            with pe.Fori(0, HA) as h:
                n = 6 * h
                tiles(A0, n, KX, B, (xhi, xlo), 0, 2, lambda m: pe.wait_ge(a_ot, 4 * h + (m + 1)), a_qk,
                      each=True)
                tiles(A0 + 1, n, KX, B[2:], (xhi, xlo), 0, 2, lambda m: pe.wait_ge(a_ot, 4 * h + (m + 3)),
                      a_qk)
                token_tiles(A0 + 2, n, 4, 0, lambda q: A[q][:, :], True, False,
                            lambda q: pe.wait_ge(a_gt, 4 * h + (q + 1)), a_v)
                token_tiles(A0 + 3, n, 4, 4, lambda q: A[q][:, :], False, True, nothing, a_v)
                pe.wait_ge(a_qklo, 4 * h + 4)
                for kt in range(TT):
                    for d in range(2):
                        r = slice(kt * P, (kt + 1) * P)
                        last = split_dots(pe, B[kt][:, 0:SEQ - kt * P], qk_hi[:, 2 + d, r], qk_lo[:, 2 + d, r],
                                          qk_hi[:, d, kt * P:], qk_lo[:, d, kt * P:], d == 0, d == 1)
                    last.then_inc(a_s, 1)
                tiles(A0 + 4, n, KX, A, (xhi, xlo), 0, 2, lambda m: pe.wait_ge(a_vlo, 4 * h + (m + 1)), a_g)
                pe.wait_ge(a_vlo, 4 * h + 4)
                for q in range(TT):
                    pe.wait_ge(a_slo, 4 * h + (q + 1))
                    for kt in range(q + 1):
                        r = slice(KT_AT[kt] + (q - kt) * P, KT_AT[kt] + (q - kt + 1) * P)
                        last = split_dots(pe, B[q][:, :], s_hi[:, r], s_lo[:, r], v_hi[:, kt, :], v_lo[:, kt, :],
                                          kt == 0, kt == q)
                    last.then_inc(a_o, 1)
                tiles(A0 + 5, n, KX, A[2:], (xhi, xlo), 0, 2, nothing, a_g)
                pe.wait_ge(aux["const"], 48)
                pe.wait_ge(a_on, 4 * h + 4)
                for j in range(VT):
                    for q in range(TT):
                        last = pe.transpose(B[j][:, q * P:(q + 1) * P], work[:, q, j * P:(j + 1) * P], ident[:, :])
                    last.then_inc(a_t, 1)
            project_out(AO, HA * VT, ar_hi, ar_lo, 0,
                        lambda q: pe.wait_ge(a_gt if q < 2 else a_ot, 4 * HA + 2 + 2 * (q % 2)),
                        lambda c: turn_x(xres, n_x, 0, 0) if c == 0 else None)

            first_product(xres, n_x, 0, 1, B0, b_c, turned=True)
            token_tiles(B0 + 2, 0, 4, 0, lambda q: O[q][:, :], True, False, nothing, b_ql)
            pe.wait_ge(b_ctok, TT)
            for j in range(KC):
                for q in range(TT):
                    last = pe.transpose(E[j][:, q * P:(q + 1) * P], c_tok[:, q, j * P:(j + 1) * P], ident[:, :])
                last.then_inc(b_ct, 1)
            token_tiles(B0 + 3, 0, 4, 4, lambda q: O[q][:, :], False, True, nothing, b_ql)
            token_tiles(B0 + 4, 0, KX, 0, lambda q: E[q][:, 0:256], True, True,
                        lambda q: pe.wait_ge(b_clo, q + 1), b_ql)
            pe.wait_ge(b_qtok, 3)
            pe.wait_ge(b_qtl, 3)
            for q in range(TT):
                if q == TT - 1:
                    pe.wait_ge(b_qtok, TT)
                    pe.wait_ge(b_qtl, TT)
                for j in range(KQ):
                    last = pe.transpose(bank[j][:, q * P:(q + 1) * P], q_tok[:, q, j * P:(j + 1) * P], ident[:, :])
                    if q == TT - 1:
                        last.then_inc(b_qt, 1)
            pe.wait_ge(b_wl, 1)
            for k in range(KX):
                last = split_dots(pe, bank[7][:, :], wkr_hi[:, k, :], wkr_lo[:, k, :], xhi[:, k, :], xlo[:, k, :],
                                  k == 0, k == KX - 1)
            last.then_inc(b_kr, 1)
            pe.wait_ge(b_qlo, KQ)
            pe.wait_ge(b_w, 3)

            with pe.Fori(0, PAIRS // 2) as it:
                for s in range(2):
                    n = 6 * it
                    p = M0 + 3 * s

                    def c(per, k):
                        return 2 * per * it + (per * s + k)

                    tiles(p, n, KQ, bank[4:7], (ql_hi, ql_lo), 0, 3, nothing, m_q)
                    pe.wait_ge(m_gt, c(2, 2))
                    pe.wait_ge(m_og, c(2, 1))
                    tiles(p + 1, n, KC, bank[0:2], (c_hi, c_lo), 0, 2, nothing, m_kv)
                    wh, wl = panel(p + 1, KC)
                    for q in range(TT):
                        for k in range(KC):
                            r = slice(q * P, (q + 1) * P)
                            last = split_dots(pe, bank[2 + q // 2][:, q % 2 * 256:q % 2 * 256 + 256],
                                              c_hi[:, k, r], c_lo[:, k, r], wh[:, k, 256:512], wl[:, k, 256:512],
                                              k == 0, k == KC - 1)
                        if q % 2:
                            last.then_inc(m_kv, 1)

                    def scores(e):
                        for q in range(TT):
                            w = (q + 1) * P
                            r = slice(q * P, w)
                            dst = bank[4 + q]
                            f = slice(ROPE * e, ROPE * e + ROPE)
                            pe.matmul(dst[:, 0:w], qn_hi[:, e, r], kn_hi[:, e, 0:w], start=True, stop=False)
                            pe.matmul(dst[:, r], id_b[:, :], mask_b[:, :], start=False, stop=False)
                            pe.matmul(dst[:, 0:w], qn_hi[:, e, r], kn_lo[:, e, 0:w], start=False, stop=False)
                            pe.matmul(dst[:, 0:w], qn_lo[:, e, r], kn_hi[:, e, 0:w], start=False, stop=False)
                            pe.matmul(dst[:, 0:w], qr[:, e, r], kr_hi[:, 0:w], start=False, stop=False)
                            pe.matmul(dst[:, 0:w], qr[f, e, r], kr_lo[f, 0:w], start=False, stop=True
                                      ).then_inc(m_s, 1)

                    def turn(e):
                        dst = [bank[1], bank[2], bank[3]] if e == 0 else [bank[2], bank[3], bank[4]]
                        for kt in range(TT):
                            for q in range(kt, TT):
                                at = (q - kt) * P + (256 if kt == 3 else 0)
                                src = q * (q + 1) // 2 * P + kt * P
                                last = pe.transpose(dst[min(kt, 2)][:, at:at + P], prob[:, src:src + P], ident[:, :])
                            if kt != 2:
                                last.then_inc(m_t, 1)

                    def attend(e, dst):
                        for kt in range(TT):
                            r = slice(KT_AT[kt], KT_AT[kt] + SEQ - kt * P)
                            last = split_dots(pe, dst[:, kt * P:], vb_hi[:, kt, e * VH:(e + 1) * VH],
                                              vb_lo[:, kt, e * VH:(e + 1) * VH], pt_hi[:, r], pt_lo[:, r],
                                              kt == 0, kt == TT - 1)
                        last.then_inc(m_o, 1)

                    def gate_part(m, k0, k1):
                        wh, wl = panel(p + 2, KX)
                        for k in range(k0, k1):
                            if m == 0:
                                need(p + 2, n, KX, k)
                            f = slice(m * P, (m + 1) * P)
                            last = split_dots(pe, bank[0][:, :], wh[:, k, f], wl[:, k, f], xhi[:, k, :],
                                              xlo[:, k, :], k == 0, k == KX - 1)
                        return last

                    pe.wait_ge(b_krlo, 1)
                    pe.wait_ge(m_qlo, c(4, 4))
                    pe.wait_ge(m_kvlo, c(4, 1))
                    pe.wait_ge(m_og, c(2, 2))
                    scores(0)
                    gate_part(0, 0, KX).then_inc(m_g, 1)
                    pe.wait_ge(m_kvlo, c(4, 4))
                    pe.wait_ge(m_p, c(8, 4))
                    turn(0)
                    scores(1)
                    pe.wait_ge(m_gt, c(2, 3))
                    gate_part(1, 0, KX // 2)
                    pe.wait_ge(m_ptlo, c(6, 3))
                    attend(0, bank[1])
                    pe.wait_ge(m_p, c(8, 8))
                    turn(1)
                    gate_part(1, KX // 2, KX).then_inc(m_g, 1)
                    pe.wait_ge(m_ptlo, c(6, 6))
                    attend(1, bank[7])
            pe.wait_ge(m_gt, 2 * PAIRS + 2)
            project_out(BO, HB, br_hi, br_lo, HA * VT, lambda q: pe.wait_ge(m_og, 2 * PAIRS + (2 if q == 3 else 1)))

            first_product(h_tok, r_h, 0, 2, L0, l_v)
            for a in range(2):
                tiles(L0 + 2 + a, 0, KX, O[2 * a:], (xhi, xlo), 0, 2, nothing, l_u)
            for a in range(2):
                tiles(L0 + 4 + a, 0, KX, E[2 * a:], (xhi, xlo), 0, 2,
                      lambda m: pe.wait_ge(l_vt, 2 * a + m + 1), l_q)
            pe.wait_ge(l_wl, 1)
            pe.wait_ge(l_mk, 2)

            def keys(g):
                tiles(L0 + 6 + g // 2, 0, KX, O[g // 2 * 2:], (xhi, xlo), g % 2, g % 2 + 1,
                      lambda m: pe.wait_ge(l_up, g + 1), l_q)
                pe.wait_ge(l_qlo, g + 1)
                pe.wait_ge(l_plo, g + 1)
                split_dots(pe, E[g][:, :], wp_hi[:, g, :], wp_lo[:, g, :], pool_hi[:, :], pool_lo[:, :], True, True
                           ).then_inc(l_mix, 1)

            def values(m):
                hp, j = steps[m]
                pe.wait_ge(e_tlo, m + 1)
                if hp == 0:
                    pe.wait_ge(l_blo, 2 * j + 1)
                    pe.wait_ge(l_blo1, 1)
                if m >= 2:
                    pe.wait_ge(e_oc, 2 * (m - 1))
                for half in range(2):
                    p_ = [x[:, m % 2, :].rearrange("p (e a n) -> p e a n", e=2, a=2)[:, :, half, :]
                          for x in (npt_hi, npt_lo)]
                    last = split_dots(pe, bank[6 + m % 2][:, 0:2 * P],
                                      xhi[:, 2 * j + half, hp * P:(hp + 1) * P],
                                      xlo[:, 2 * j + half, hp * P:(hp + 1) * P],
                                      p_[0], p_[1], half == 0, half == 1)
                last.then_inc(e_o, 1)

            for g in range(3):
                keys(g)
            for i in range(len(steps) + 2):
                if i == 2:
                    keys(3)
                if i < len(steps):
                    hp, j = steps[i]
                    if i < 2:
                        pe.wait_ge(l_mo, i + 1)
                    else:
                        pe.wait_ge(e_tk, i - 1)
                    if i < 4:
                        pe.wait_ge(l_qlo, 5 + hp)
                    for e in range(2):
                        f = slice(DHN * e, DHN * e + DHN)
                        o = bank[2 * (i % 2) + e][:, 0:256]
                        q_ = [x[f, hp, j * P:(j + 1) * P] for x in (nq_hi, nq_lo)]
                        k_ = [x[f, hp, :].rearrange("p (r c) -> p r c", r=ROWS)[
                              :, :, BAND_START[j]:BAND_START[j] + BAND] for x in (nk_hi, nk_lo)]
                        pe.matmul(o, id_n[:, :], nmask_b[:, j:j + 1, :].to_broadcast([P, ROWS, BAND]),
                                  start=True, stop=False)
                        last = split_dots(pe, o, q_[0], q_[1], k_[0], k_[1], False, True)
                    last.then_inc(e_s, 1)
                if 2 <= i < len(steps) + 2:
                    m = i - 2
                    if m == 0:
                        pe.wait_ge(l_mo, 4)
                    pe.wait_ge(e_p, m + 1)
                    pe.wait_ge(e_q, m + 1)
                    if m >= 2:
                        pe.wait_ge(e_tlo, m - 1)
                    for e in range(2):
                        for half in range(2):
                            a = (2 * e + half) * P
                            last = pe.transpose(bank[4 + m % 2][:, a:a + P],
                                                nt[:, m % 3, e, half * P:(half + 1) * P], ident[:, :])
                    last.then_inc(e_t, 1)
                if i >= 3:
                    values(i - 3)

            def free(q):
                pe.wait_ge((e_tk, e_tk, e_tlo, e_oc)[q], len(steps) * (1, 1, 1, 2)[q])
                if q == 2:
                    values(len(steps) - 1)

            project_out(WO, KX, cr_hi, cr_lo, HA * VT + HB, free=free, turn=lambda q: turn_x(h2_tok, r_h, TT, q))
            for s in range(2):
                pe.wait_ge(xt_lo, 3 * KX + 4 * (s + 1))
                r = slice(256 * s, 256 * s + 256)
                for m in range(3):
                    if s == 0 and m == 2:
                        turn_x(h2_tok, r_h, TT, 2)
                        turn_x(h2_tok, r_h, TT, 3)
                    wh, wl = panel(UP + m // 2, KX)
                    for k in range(KX):
                        if s == 0 and m % 2 == 0:
                            need(UP + m // 2, 0, KX, k)
                        f = slice(m % 2 * P, m % 2 * P + P)
                        last = split_dots(pe, bank[m][:, r], wh[:, k, f], wl[:, k, f], xhi[:, k, r], xlo[:, k, r],
                                          k == 0, k == KX - 1)
                    if s:
                        last.then_inc(u_m, 1)
            tiles(UP + 1, 0, KX, bank[2:], (xhi, xlo), 1, 2, nothing, u_m)
            with pe.Fori(1, KF // 4) as i:
                for a in range(2):
                    tiles(UP + a, 2 * i, KX, bank[2 * a:], (xhi, xlo), 0, 2,
                          lambda m: pe.wait_ge(u_r, 4 * i + (2 * a + m + 1)), u_m)
            project_out(DN, KF, dr_hi, dr_lo, HA * VT + HB + KX,
                        lambda q: pe.wait_ge(u_r, KF + min(4, 2 * q + 2)))

        @block.scalar
        def _(act):
            def split_hi(p, used=None, count=0, width=PAN, n=0):
                act.wait_ge(landed[p % 2], 8 * n + 16 * (p // 2 + 1))
                if used is not None:
                    act.wait_ge(used, count)
                for s in range(2):
                    r = slice(s * width // 2, (s + 1) * width // 2)
                    act.activation(whi[p % 2][:, r], stage[p % 2][:, r], ACT.Copy).then_inc(w_hi, 1)

            def copy(dst, src, signal, scale=1.0):
                act.activation(dst, src, ACT.Copy, scale=scale).then_inc(signal, 1)

            def first_tiles(src, hi, k0=0, count=4):
                for kk in range(k0, k0 + count):
                    copy(hi[:, kk, :], src[:, kk, :], ar_h)

            def project_out(p0, nk, src, hi, done, ready=None):
                if ready:
                    ready(0)
                    first_tiles(src, hi)
                    for c in range(1, nk // 4):
                        ready(4 * c)

                def half(j, n, k):
                    split_hi(p0 + j, half_done, n + (done + j - 1), PAN, n)
                    for b in range(2):
                        copy(hi[:, (2 * j + b) % 4, :], src[:, bass.ds(k + (2 * j + b), 1), :].rearrange(
                            "p a n -> p (a n)"), ar_h)

                with act.Fori(1, nk // 4) as i:
                    for j in range(2):
                        half(j, 2 * i, 4 * i)

            def norms(y0, ln=None, rms=None, squares_to=None, scratch=None, round_=None, next_panel=None, done=0):
                def deviation(q):
                    act.wait_ge(n_mu, TT * ln + q + 1)
                    act.activation(scratch[:, q % 2, :], xres[:, q, :], ACT.Square, bias=small[:, 0, q:q + 1],
                                   accum_out=small[:, 3, q:q + 1]).then_inc(n_ss, 1)
                    act.wait_ge(n_ss, TT * ln + q + 1)
                    act.activation(small[:, 1, q:q + 1], small[:, 3, q:q + 1], ACT.Sqrt, scale=1.0 / DM,
                                   bias=eps[:, 0:1]).then_inc(n_sd, 1)

                def root_mean_square(q):
                    act.wait_ge(n_x, y0 + q + 1)
                    act.activation(squares_to[:, q, :], xres[:, q, :], ACT.Square, accum_out=small[:, 3, 4 + q:5 + q]
                                   ).then_inc(r_ss, 1)
                    act.wait_ge(r_ss, TT * rms + q + 1)
                    act.activation(small[:, 1, 4 + q:5 + q], small[:, 3, 4 + q:5 + q], ACT.Sqrt, scale=1.0 / DM,
                                   bias=eps[:, 1:2]).then_inc(r_sd, 1)

                def transposed(q):
                    for c in range(2):
                        act.wait_ge(xt_t, KX * (round_ - 1) + 2 * q + c + 1)
                        copy(xhi[:, 4 * c:4 * c + 4, q * P:(q + 1) * P],
                             bank[2 * q + c][:, :].rearrange("p (k n) -> p k n", k=4), xt_hi)

                if next_panel:
                    split_hi(next_panel, half_done, done)
                if ln is None:
                    root_mean_square(0)
                    root_mean_square(1)
                    if round_:
                        transposed(0)
                        transposed(1)
                    root_mean_square(2)
                    if next_panel:
                        split_hi(next_panel + 1, y_done, 2 * (y0 + TT))
                    root_mean_square(3)
                    if round_:
                        transposed(2)
                        transposed(3)
                else:
                    for q in range(TT + 1):
                        if rms is None and q:
                            transposed(q - 1)
                        if q < TT:
                            deviation(q)
                        if rms is not None and q:
                            transposed(q - 1)
                        if q == 1:
                            split_hi(next_panel + 1, y_done, 2 * (y0 + TT))
                        if rms is not None and q < TT:
                            root_mean_square(q)

            xt_view = xres[:, :, :].rearrange("p t (a n) -> p (t a) n", a=2)
            act.wait_ge(first, 16)
            act.activation(whi[0][:, 0:PAN // 2], stage[0][:, 0:PAN // 2], ACT.Copy).then_inc(w_hi, 1)
            for k in range(KX):
                act.wait_ge(xt_ld[k], 16)
                copy(xhi[:, k, :], xt_view[:, k, :], xt_hi)
                if k == 2:
                    act.wait_ge(landed[0], 16)
                    act.activation(whi[0][:, PAN // 2:PAN], stage[0][:, PAN // 2:PAN], ACT.Copy).then_inc(w_hi, 1)
            act.wait_ge(xt_lo, KX)
            act.dma_start(xres[:, :, :], t["x"]).then_inc(aux["x"], 16)
            A, B, E, O = bank[0:4], bank[4:8], bank[0::2], bank[1::2]
            with act.Fori(0, HA) as h:
                n = 6 * h
                split_hi(A0 + 1, a_g, 4 * h + 4, PAN, n)
                act.wait_ge(a_dec, 4 * h + 4)
                act.dma_start(decay[:, :], t["decay"][bass.ds(h, 1), :, :].rearrange("a p n -> (a p) n")
                              ).then_inc(aux["decay"], 16)
                for m in range(4):
                    if m % 2 == 0:
                        split_hi(A0 + 2 + m // 2, a_qk, 4 * h + (m + 2), PAN, n)
                    act.wait_ge(a_q32, 4 * h + (m + 1))
                    copy(qk_hi[:, m, :], work[:, m % 2 * 2, :], a_qkhi)
                split_hi(A0 + 4, half_done, h + 1, PAN, n)
                for q in range(TT):
                    act.wait_ge(a_v, 4 * h + (q + 1))
                    copy(v_hi[:, q, :], A[q][:, :], a_vhi)
                split_hi(A0 + 5, a_v, 4 * h + 4, PAN, n)
                for kt in range(TT):
                    act.wait_ge(a_dec, 4 * h + (kt + 5))
                    copy(s_hi[:, KT_AT[kt]:KT_AT[kt] + SEQ - kt * P], work[:, kt, 0:SEQ - kt * P], a_shi)

                def tanh(m):
                    act.wait_ge(a_g, 4 * h + (m + 5))
                    act.activation(gate[:, m, :], A[m][:, :], ACT.Tanh, scale=0.5).then_inc(a_th, 1)

                tanh(0)
                tanh(1)
                split_hi(A0 + 6, a_g, 4 * h + 6, PAN, n)
                act.wait_ge(a_var, h + 1)
                act.activation(small[:, 1, 0:TT], small[:, 0, 0:TT], ACT.Sqrt).then_inc(a_sd, 1)
                tanh(2)
                tanh(3)
            act.wait_ge(a_o, 4 * HA)

            def outputs(k):
                if k == HA * VT - 4:
                    act.wait_ge(a_ot, 4 * HA + 4)
                elif k == 0:
                    act.wait_ge(a_ot, 4 * HA)
                elif k == 4:
                    act.dma_start(rows[:, :, :], t["ln"][0]).then_inc(aux["rows"], 16)
                    split_hi(AO + 1, a_g, 4 * HA + 4)

            project_out(AO, HA * VT, oT, ar_hi, HA, outputs)
            norms(0, ln=0, scratch=gate[:, :, :].rearrange("p (t a) n -> p t (a n)", a=2), round_=1, next_panel=B0,
                  done=HA + 7)
            act.wait_ge(n_x, TT)
            act.dma_start(wkr[:, :, :], t["wkr"]).then_inc(aux["kr"], 16)
            act.dma_start(mask_f[:, :], t["mask"]).then_inc(aux["kr"], 16)
            act.dma_start(rope_b[:, :, :], t["rope_b"]).then_inc(aux["ropeb"], 16)

            split_hi(B0 + 2, half_done, HA + 8)
            act.wait_ge(aux["kr"], 32)
            copy(wkr_hi[:, :, :], wkr[:, :, :], b_w)
            copy(mask_b[:, :], mask_f[:, :], b_w)
            copy(id_b[:, :], ident[:, :], b_w)
            for q in range(TT):
                act.wait_ge(b_c, q + 1)
                act.activation(c_tok[:, q, :], E[q][:, :], ACT.Square, accum_out=small[:, 3, q:q + 1]
                               ).then_inc(b_css, 1)
            act.wait_ge(b_cms, 1)
            act.activation(small[:, 1, 0:TT], small[:, 0, 0:TT], ACT.Sqrt).then_inc(b_csd, 1)
            act.wait_ge(b_crs, 1)
            for q in range(TT):
                copy(c_tok[:, q, :], E[q][:, :], b_ctok, small[:, 2, q:q + 1])
            split_hi(B0 + 3, b_c, TT)
            for j in range(KC):
                act.wait_ge(b_ct, j + 1)
                copy(c_hi[:, j, :], E[j][:, :], b_chi, cols[:, COL_CG + j:COL_CG + j + 1])
            split_hi(B0 + 4, half_done, HA + 9)
            for q in range(TT):
                act.wait_ge(b_ql, q + 1)
                act.activation(q_tok[:, q, 0:512], O[q][:, :], ACT.Square, accum_out=small[:, 3, 4 + q:5 + q]
                               ).then_inc(b_qss, 1)
            split_hi(M0, b_ql, TT, PANEL)
            for q in range(TT):
                act.wait_ge(b_ql, TT + q + 1)
                act.activation(q_tok[:, q, 512:768], E[q][:, 0:256], ACT.Square, accum_out=small[:, 3, q:q + 1]
                               ).then_inc(b_qss, 1)
                act.wait_ge(b_qms, q + 1)
                act.activation(small[:, 1, 4 + q:5 + q], small[:, 0, 4 + q:5 + q], ACT.Sqrt).then_inc(b_qsd, 1)
                act.wait_ge(b_qrs, q + 1)
                copy(q_tok[:, q, 0:512], O[q][:, :], b_qtok, small[:, 2, 4 + q:5 + q])
            for j in range(KQ):
                act.wait_ge(b_qt, j + 1)
                copy(ql_hi[:, j, :], bank[j][:, :], b_qhi, cols[:, COL_QG + j:COL_QG + j + 1])
            act.wait_ge(b_kr32, 1)
            copy(kr_hi[:, :], rtmp[:, 0, :], b_krhi)

            with act.Fori(0, PAIRS // 2) as it:
                for s in range(2):
                    n = 6 * it
                    p = M0 + 3 * s

                    def c(per, k):
                        return 2 * per * it + (per * s + k)

                    split_hi(p + 1, m_g, c(2, 2), PAN, n)
                    for m in range(2):
                        act.wait_ge(m_q, c(3, m + 1))
                        copy(qn_hi[:, m, :], bank[4 + m][:, :], m_qhi)
                    split_hi(p + 2, m_q, c(3, 3), PAN, n)
                    act.wait_ge(m_qr32, c(1, 1))
                    for e in range(2):
                        f = slice(ROPE * e, ROPE * e + ROPE)
                        copy(qr[f, e, :], rtmp[f, 0, :], m_qhi)
                    for m in range(2):
                        act.wait_ge(m_kv, c(4, m + 1))
                        copy(kn_hi[:, m, :], bank[m][:, :], m_kvhi)
                    for m in range(2):
                        act.wait_ge(m_kv, c(4, m + 3))
                        copy(vb_hi[:, 2 * m:2 * m + 2, :].rearrange("p t n -> p (t n)"), bank[2 + m][:, :], m_kvhi)
                    split_hi(p + 3, m_kv, c(4, 4), PANEL, n)

                    def exps(e):
                        for q in range(TT):
                            w = (q + 1) * P
                            at = q * (q + 1) // 2 * P
                            act.wait_ge(m_nb, c(8, 4 * e + q + 1))
                            act.activation(prob[:, at:at + w], bank[4 + q][:, 0:w], ACT.Exp, scale=SCALE_B,
                                           bias=sm[:, 1, 4 * e + q:4 * e + q + 1],
                                           accum_out=sm[:, 2, 4 * e + q:4 * e + q + 1]).then_inc(m_exp, 1)

                    def turned(e):
                        for b in range(3):
                            w = (512, 384, 384)[b]
                            act.wait_ge(m_t, c(6, 3 * e + b + 1))
                            copy(pt_hi[:, (0, 512, 896)[b]:(0, 512, 896)[b] + w], bank[1 + e + b][:, 0:w], m_pthi)

                    def tanh(m):
                        act.wait_ge(m_g, c(2, m + 3))
                        act.wait_ge(m_st[m], 32 * it + (16 * s + 16))
                        act.activation(gt[:, m, :], bank[0][:, :], ACT.Tanh, scale=0.5).then_inc(m_th, 1)

                    exps(0)
                    tanh(0)
                    turned(0)
                    exps(1)
                    turned(1)
                    tanh(1)

            def outputs_b(k):
                if k == 4:
                    split_hi(BO + 1, m_g, 2 * PAIRS + 2)
                    act.wait_ge(m_og, 2 * PAIRS + 2)
                    act.dma_start(rows2[:, :, :], t["ln"][1]).then_inc(aux["rows2"], 16)
                    act.dma_start(bias[:, :, :, :], t["bias"]).then_inc(aux["bias"], 16)
                    act.dma_start(nmask[:, :, :], t["nmask"]).then_inc(aux["nmask"], 16)
                    act.dma_start(wp[:, :, :], t["wp"]).then_inc(aux["wp"], 16)
                    act.dma_start(edge[:, :, :], t["edge"]).then_inc(aux["edge"], 16)
                act.wait_ge(bld[k // 4], 16)

            project_out(BO, HB, bT, br_hi, HA + 9, outputs_b)
            norms(TT, ln=1, rms=0, squares_to=h_tok, scratch=mixT[:, 0:4, :].rearrange("p (t a) n -> p t (a n)", a=2),
                  round_=2, next_panel=L0, done=HA + 16)
            act.wait_ge(r_h, TT)
            act.dma_start(grow[:, :], t["grow"][1]).then_inc(aux["grow"], 16)

            split_hi(L0 + 2, half_done, HA + 17)
            act.wait_ge(aux["nmask"], 16)
            copy(nmask_b[:, :, :], nmask[:, :, :], l_mk)
            copy(id_n[:, :], ident[:, :], l_mk)
            act.wait_ge(aux["wp"], 16)
            copy(wp_hi[:, :, :], wp[:, :, :], l_w)
            for q in range(TT):
                act.wait_ge(l_v, q + 1)
                copy(v_tok[:, q, :], E[q][:, :], l_vt)
            act.wait_ge(l_vt, TT)
            act.dma_start(t["v_spill"].rearrange("(t p) n -> p t n", p=P), v_tok[:, :, :]).then_inc(vst, 16)
            split_hi(L0 + 3, l_v, TT)
            act.wait_ge(vst, 16)
            for g in range(4):
                act.wait_ge(l_u, g + 1)
                copy(upad[:, g, PAD:PAD + SEQ], O[g][:, :], l_up)
                if g % 2:
                    split_hi(L0 + 4 + g // 2, l_u, g + 1)
                if g == 1:
                    grid = t["v_spill"].rearrange("(r c) n -> r c n", c=GRID)
                    for j in range(NBLK):
                        for half in range(2):
                            act.dma_start(vband[:, 2 * j + half, :],
                                          grid[4 * half:4 * half + 4, BAND_START[j]:BAND_START[j] + BAND, :]
                                          ).then_inc(vld[2 * j + half], 16)

            def pooled_hi(g):
                act.wait_ge(l_pool, g + 1)
                copy(pool_hi[:, :], win[:, 0, 0:SEQ], l_phi)

            pooled_hi(0)
            for m in range(4):
                act.wait_ge(l_q, m + 1)
                copy(by_block(nq_hi[:, m, :]), from_rows(E[m][:, :]), l_qhi)
                if m % 2:
                    split_hi(L0 + 6 + m // 2, l_q, m + 1)

            def keys(m):
                act.wait_ge(l_q, m + 5)
                copy(nk_hi[:, m, :], O[m][:, :], l_qhi)
                act.wait_ge(l_mix, m + 1)
                if m < 3:
                    pooled_hi(m + 1)
                copy(mixT[:, m, :], E[m][:, :], l_mo, cols[:, COL_PS + m:COL_PS + m + 1])

            keys(0)
            keys(1)
            split_hi(WO, l_q, 6)
            keys(2)

            def band_hi(b):
                act.wait_ge(vld[b], 16)
                copy(xhi[:, b, :], vband[:, b, :], l_bhi)

            for i in range(len(steps) + 3):
                if i == 2:
                    keys(3)
                    band_hi(0)
                    band_hi(1)
                if 2 <= i < len(steps) + 2:
                    m = i - 2
                    act.wait_ge(e_t, m + 1)
                    if m >= 2:
                        act.wait_ge(e_o, m - 1)
                    copy(npt_hi[:, m % 2, :], bank[4 + m % 2][:, :], e_thi)
                if i < len(steps):
                    act.wait_ge(e_nb, i + 1)
                    for e in range(2):
                        act.activation(nt[:, i % 3, e, :], nt[:, i % 3, e, :], ACT.Exp,
                                       bias=nsm[:, i % 3, 0, e:e + 1], accum_out=nsm[:, i % 3, 1, e:e + 1]
                                       ).then_inc(e_exp, 1)
                if 2 <= i < 8:
                    band_hi(i)
                if len(steps) <= i < len(steps) + 2:
                    act.wait_ge(e_s, len(steps))
                    first_tiles(mixT, cr_hi, 2 * (i - len(steps)), 2)
                if i in (9, 10):
                    r = slice((i - 9) * 1024, (i - 8) * 1024)
                    w = (WO + 1) % 2
                    act.wait_ge(landed[w], 16 * ((WO + 1) // 2 + 1))
                    act.activation(whi[w][:, r], stage[w][:, r], ACT.Copy).then_inc(w_hi, 1)
                if i >= 3:
                    m = i - 3
                    hp, j = steps[m]
                    act.wait_ge(e_o, m + 1)
                    for e in range(2):
                        f = slice(DHN * e, DHN * e + DHN)
                        dst = mixT[f, 4 + hp, :].rearrange("p (r c) -> p r c", r=ROWS)[:, :, j * BLK:(j + 1) * BLK]
                        copy(dst, bank[6 + m % 2][f, e * P:(e + 1) * P].rearrange("p (r c) -> p r c", r=ROWS), e_oc)
            act.wait_ge(e_oc, 2 * len(steps))
            project_out(WO, KX, mixT, cr_hi, HA + 17)
            norms(2 * TT, rms=1, squares_to=h2_tok, round_=3, next_panel=UP, done=HA + 20)

            act.wait_ge(r_h, 2 * TT)
            act.dma_start(grow[:, :], t["grow"][2]).then_inc(aux["grow"], 16)

            def hidden(m, i):
                act.wait_ge(u_m, 4 * i + (m + 1))
                act.wait_ge(u_s, 4 * i + (m + 1))
                act.activation(relu[:, m, :], bank[m][:, :], ACT.Relu).then_inc(u_r, 1)
                if m % 2:
                    split_hi(UP + 2 + m // 2, u_m, 4 * i + (m + 1), PAN, 2 * i)

            with act.Fori(0, KF // 4 - 1) as i:
                for m in range(4):
                    hidden(m, i)
            hidden(0, KF // 4 - 1)
            hidden(1, KF // 4 - 1)
            first_tiles(hid, dr_hi)
            hidden(2, KF // 4 - 1)
            hidden(3, KF // 4 - 1)
            act.wait_ge(u_s, KF + 4)
            project_out(DN, KF, hid, dr_hi, HA + 20)
            norms(3 * TT, rms=2, squares_to=hid[:, 0:2 * TT, :].rearrange("p (t a) n -> p t (a n)", a=2))

        @block.vector
        def _(dve):
            own = Own(dve, dv)

            def lo_of(dst, src, hi, signal):
                dve.tensor_tensor(dst, src, hi.bitcast(F32), ALU.subtract).then_inc(signal, 1)

            def lo_scaled(dst, src, scale, hi, signal):
                dve.scalar_tensor_tensor(out=dst, in0=src, scalar=scale, in1=hi.bitcast(F32), op0=ALU.mult,
                                         op1=ALU.subtract).then_inc(signal, 1)

            def first_tiles(src, hi, lo, a0, k0=0, count=4):
                for kk in range(k0, k0 + count):
                    dve.wait_ge(ar_h, a0 + kk + 1)
                    lo_of(lo[:, kk, :], src[:, kk, :], hi[:, kk, :], ar_l)

            def project_out(nk, src, hi, lo, a0):
                with dve.Fori(1, nk // 4) as i:
                    for kk in range(4):
                        dve.wait_ge(ar_h, 4 * i + (a0 + kk + 1))
                        lo_of(lo[:, kk, :], src[:, bass.ds(4 * i + kk, 1), :].rearrange("p a n -> p (a n)"),
                              hi[:, kk, :], ar_l)

            def norms(y0, ln=None, rms=None, gb=None, centred=None, result=None, round_=None):
                def gather(q):
                    for c in range(2):
                        w = slice(c * 512, (c + 1) * 512)
                        dve.wait_ge(y_done, 2 * (y0 + q) + c + 1)
                        y = bank[2 * q + c][:, :]
                        if ln is not None:
                            own.mark(dve.scalar_tensor_tensor(out=xres[:, q, w], in0=xres[:, q, w], scalar=ALPHA,
                                                              in1=y, op0=ALU.mult, op1=ALU.add,
                                                              accum_out=mv[:, q, c:c + 1]))
                        elif c == 0:
                            own.mark(dve.tensor_tensor(xres[:, q, w], xres[:, q, w], y, ALU.add))
                        else:
                            own.settle()
                            dve.tensor_tensor(xres[:, q, w], xres[:, q, w], y, ALU.add).then_inc(n_x, 1)
                    if ln is not None:
                        own.settle()
                        dve.tensor_scalar(small[:, 0, q:q + 1], mv[:, q, 0:1], mv[:, q, 1:2], -1.0 / DM, ALU.add,
                                          ALU.mult).then_inc(n_mu, 1)

                def centre(q):
                    dve.wait_ge(n_mu, TT * ln + q + 1)
                    own.mark(dve.scalar_tensor_tensor(out=centred[:, q, :], in0=xres[:, q, :],
                                                      scalar=small[:, 0, q:q + 1], in1=gb[:, 0, :], op0=ALU.add,
                                                      op1=ALU.mult))

                def shift(q):
                    dve.wait_ge(n_sd, TT * ln + q + 1)
                    own.mark(dve.reciprocal(small[:, 2, q:q + 1], small[:, 1, q:q + 1]))
                    own.settle()
                    dve.scalar_tensor_tensor(out=xres[:, q, :], in0=centred[:, q, :], scalar=small[:, 2, q:q + 1],
                                             in1=gb[:, 1, :], op0=ALU.mult, op1=ALU.add).then_inc(n_x, 1)

                def scale(q):
                    dve.wait_ge(r_sd, TT * rms + q + 1)
                    own.mark(dve.reciprocal(small[:, 2, 4 + q:5 + q], small[:, 1, 4 + q:5 + q]))
                    own.settle()
                    dve.scalar_tensor_tensor(out=result[:, q, :], in0=xres[:, q, :], scalar=small[:, 2, 4 + q:5 + q],
                                             in1=grow[:, :], op0=ALU.mult, op1=ALU.mult).then_inc(r_h, 1)

                def transposed(q):
                    for c in range(2):
                        dve.wait_ge(xt_hi, KX * round_ + 2 * q + c + 1)
                        lo_of(xlo[:, 4 * c:4 * c + 4, q * P:(q + 1) * P],
                              bank[2 * q + c][:, :].rearrange("p (k n) -> p k n", k=4),
                              xhi[:, 4 * c:4 * c + 4, q * P:(q + 1) * P], xt_lo)

                if ln is None:
                    gather(0)
                    gather(1)
                    scale(0)
                    scale(1)
                    gather(2)
                    if round_:
                        transposed(0)
                        transposed(1)
                    gather(3)
                    scale(2)
                    scale(3)
                    if round_:
                        transposed(2)
                        transposed(3)
                else:
                    for q in range(TT + 1):
                        if q < TT:
                            gather(q)
                        if q and rms is not None:
                            scale(q - 1)
                        if q < TT:
                            centre(q)
                        early = rms is None or q < TT - 1
                        if q and early:
                            transposed(q - 1)
                        if q < TT:
                            shift(q)
                        if q and not early:
                            transposed(q - 1)

            dve.memset(eps[:, 0:1], LN_EPS)
            dve.memset(eps[:, 1:2], RMS_EPS)
            dve.sem_inc(a_ot, 4)
            dve.sem_inc(a_g, 4)
            dve.sem_inc(a_gt, 4)
            dve.sem_inc(a_dec, 4)
            dve.sem_inc(m_g, 2)
            dve.sem_inc(m_gt, 2)
            dve.sem_inc(m_og, 2)
            dve.sem_inc(m_st[0], 16)
            dve.sem_inc(m_st[1], 16)
            dve.sem_inc(u_s, 4)
            dve.sem_inc(u_r, 4)

            xt_view = xres[:, :, :].rearrange("p t (a n) -> p (t a) n", a=2)
            for k in range(KX):
                dve.wait_ge(xt_hi, k + 1)
                lo_of(xlo[:, k, :], xt_view[:, k, :], xhi[:, k, :], xt_lo)
            A, B, E, O = bank[0:4], bank[4:8], bank[0::2], bank[1::2]
            dve.wait_ge(aux["const"], 48)
            cos, sin = rope_a[:, 0, :], rope_a[:, 1, :]
            with dve.Fori(0, HA) as h:
                own.enter(h, 17)
                for a in range(2):
                    b0, b1 = B[2 * a][:, :], B[2 * a + 1][:, :]
                    dve.wait_ge(a_qk, 4 * h + (2 * a + 2))
                    if a:
                        dve.wait_ge(a_qklo, 4 * h + 2)
                    own.mark(dve.tensor_tensor(work[:, 0, :], b0, cos, ALU.mult))
                    own.mark(dve.tensor_tensor(work[:, 1, :], b1, sin, ALU.mult))
                    own.mark(dve.tensor_tensor(work[:, 2, :], b1, cos, ALU.mult))
                    own.mark(dve.tensor_tensor(work[:, 3, :], b0, sin, ALU.mult))
                    own.settle()
                    dve.tensor_tensor(work[:, 0, :], work[:, 0, :], work[:, 1, :], ALU.subtract).then_inc(a_q32, 1)
                    dve.tensor_tensor(work[:, 2, :], work[:, 2, :], work[:, 3, :], ALU.add).then_inc(a_q32, 1)
                    for m in range(2):
                        dve.wait_ge(a_qkhi, 4 * h + (2 * a + m + 1))
                        lo_of(qk_lo[:, 2 * a + m, :], work[:, 2 * m, :], qk_hi[:, 2 * a + m, :], a_qklo)
                for q in range(TT):
                    dve.wait_ge(a_vhi, 4 * h + (q + 1))
                    lo_of(v_lo[:, q, :], A[q][:, :], v_hi[:, q, :], a_vlo)
                dve.wait_ge(aux["decay"], 16 * h + 16)
                dve.wait_ge(a_qklo, 4 * h + 4)
                for kt in range(TT):
                    w = SEQ - kt * P
                    dve.wait_ge(a_s, 4 * h + (kt + 1))
                    dve.tensor_tensor(work[:, kt, 0:w], B[kt][:, 0:w], decay[:, 0:w], ALU.mult).then_inc(a_dec, 1)
                for kt in range(TT):
                    w = SEQ - kt * P
                    dve.wait_ge(a_shi, 4 * h + (kt + 1))
                    lo_of(s_lo[:, KT_AT[kt]:KT_AT[kt] + w], work[:, kt, 0:w], s_hi[:, KT_AT[kt]:KT_AT[kt] + w], a_slo)

                def gates(m):
                    dve.wait_ge(a_th, 4 * h + (m + 1))
                    dve.scalar_tensor_tensor(out=gate[:, m, :], in0=gate[:, m, :], scalar=1.0, in1=A[m][:, :],
                                             op0=ALU.add, op1=ALU.mult).then_inc(a_gt, 1)

                gates(0)
                gates(1)
                for q in range(TT):
                    dve.wait_ge(a_o, 4 * h + (q + 1))
                    own.mark(dve.bn_stats(stat[:, q, 0, :], B[q][:, :]))
                own.settle()
                dve.memset(small[:, 3, 0:1], 0.0)
                for q in range(TT):
                    own.mark(dve.bn_aggr(mv[:, q, :], stat[:, q, 0, :]))
                own.settle()
                dve.tensor_scalar(small[:, 0, 0:TT], mv[:, :, 1], LN_EPS, 4.0, ALU.add, ALU.mult).then_inc(a_var, 1)
                dve.wait_ge(a_sd, h + 1)
                own.mark(dve.reciprocal(small[:, 2, 0:TT], small[:, 1, 0:TT]))
                own.settle()
                dve.wait_ge(a_slo, 4 * h + 4)
                for q in range(TT):
                    dve.tensor_scalar(work[:, q, :], B[q][:, :], mv[:, q, 0:1], small[:, 2, q:q + 1], ALU.subtract,
                                      ALU.mult).then_inc(a_on, 1)
                def gated(j):
                    dve.wait_ge(a_gt, 4 * h + (j + 5))
                    dve.wait_ge(a_t, 4 * h + (j + 1))
                    dve.tensor_tensor(oT[:, bass.ds(4 * h + j, 1), :].rearrange("p a n -> p (a n)"), B[j][:, :],
                                      gate[:, j, :], ALU.mult).then_inc(a_ot, 1)

                gates(2)
                gated(0)
                gates(3)
                gated(1)
                gated(2)
                gated(3)
            own.leave(HA)
            project_out(HA * VT, oT, ar_hi, ar_lo, 0)
            dve.wait_ge(aux["rows"], 16)
            dve.wait_ge(aux["x"], 16)
            norms(0, ln=0, gb=rows, centred=oT[:, 0:8, :].rearrange("p (t a) n -> p t (a n)", a=2), round_=1)

            dve.wait_ge(b_w, 1)
            lo_of(wkr_lo[:, :, :], wkr[:, :, :], wkr_hi[:, :, :], b_wl)
            dve.wait_ge(b_css, TT)
            dve.tensor_scalar(small[:, 0, 0:TT], small[:, 3, 0:TT], 1.0 / KVLORA, RMS_EPS, ALU.mult, ALU.add
                              ).then_inc(b_cms, 1)
            dve.wait_ge(b_csd, 1)
            dve.reciprocal(small[:, 2, 0:TT], small[:, 1, 0:TT]).then_inc(b_crs, 1)
            dve.wait_ge(aux["ropeb"], 16)

            def rotate(src, signal):
                own.mark(dve.tensor_tensor(rtmp[:, 0, :], src, rope_b[:, 0, :], ALU.mult))
                for g in range(4):
                    a, b = 32 * g, 32 * (g ^ 1)
                    own.mark(dve.tensor_tensor(rtmp[b:b + 32, 1, :], src[a:a + 32, :], rope_b[a:a + 32, 1, :],
                                               ALU.mult))
                own.settle()
                dve.tensor_tensor(rtmp[:, 0, :], rtmp[:, 0, :], rtmp[:, 1, :], ALU.add).then_inc(signal, 1)

            for j in range(KC):
                dve.wait_ge(b_chi, j + 1)
                lo_scaled(c_lo[:, j, :], E[j][:, :], cols[:, COL_CG + j:COL_CG + j + 1], c_hi[:, j, :], b_clo)
            for q in range(TT):
                dve.wait_ge(b_qss, TT + q + 1)
                own.mark(dve.tensor_tensor(small[:, 0, 4 + q:5 + q], small[:, 3, 4 + q:5 + q], small[:, 3, q:q + 1],
                                           ALU.add))
                own.settle()
                dve.tensor_scalar(small[:, 0, 4 + q:5 + q], small[:, 0, 4 + q:5 + q], 1.0 / QLORA, RMS_EPS, ALU.mult,
                                  ALU.add).then_inc(b_qms, 1)
                dve.wait_ge(b_qsd, q + 1)
                dve.reciprocal(small[:, 2, 4 + q:5 + q], small[:, 1, 4 + q:5 + q]).then_inc(b_qrs, 1)
                dve.wait_ge(b_qrs, q + 1)
                dve.tensor_scalar(q_tok[:, q, 512:768], E[q][:, 0:256], small[:, 2, 4 + q:5 + q], None, ALU.mult
                                  ).then_inc(b_qtl, 1)
            for j in range(KQ):
                dve.wait_ge(b_qhi, j + 1)
                lo_scaled(ql_lo[:, j, :], bank[j][:, :], cols[:, COL_QG + j:COL_QG + j + 1], ql_hi[:, j, :], b_qlo)
            dve.wait_ge(b_kr, 1)
            rotate(bank[7][:, :], b_kr32)
            dve.wait_ge(b_krhi, 1)
            lo_of(kr_lo[:, :], rtmp[:, 0, :], kr_hi[:, :], b_krlo)
            dve.wait_ge(b_krlo, 1)

            with dve.Fori(0, PAIRS // 2) as it:
                own.enter(it, 2 * 21)
                for s in range(2):
                    def c(per, k):
                        return 2 * per * it + (per * s + k)

                    for m in range(2):
                        dve.wait_ge(m_qhi, c(4, m + 1))
                        lo_of(qn_lo[:, m, :], bank[4 + m][:, :], qn_hi[:, m, :], m_qlo)
                    dve.wait_ge(m_q, c(3, 3))
                    rotate(bank[6][:, :], m_qr32)
                    for e in range(2):
                        f, other = (slice(ROPE * x, ROPE * x + ROPE) for x in (e, 1 - e))
                        dve.wait_ge(m_qhi, c(4, e + 3))
                        lo_of(qr[other, e, :], rtmp[f, 0, :], qr[f, e, :], m_qlo)
                    for m in range(2):
                        dve.wait_ge(m_kvhi, c(4, m + 1))
                        lo_of(kn_lo[:, m, :], bank[m][:, :], kn_hi[:, m, :], m_kvlo)
                    for m in range(2):
                        dve.wait_ge(m_kvhi, c(4, m + 3))
                        lo_of(vb_lo[:, 2 * m:2 * m + 2, :].rearrange("p t n -> p (t n)"), bank[2 + m][:, :],
                              vb_hi[:, 2 * m:2 * m + 2, :].rearrange("p t n -> p (t n)"), m_kvlo)

                    def softmax(e):
                        for q in range(TT):
                            x = 4 * e + q
                            dve.wait_ge(m_s, c(8, x + 1))
                            own.mark(dve.tensor_reduce(sm[:, 0, x:x + 1], bank[4 + q][:, 0:(q + 1) * P], AX, ALU.max))
                            own.settle()
                            dve.tensor_scalar(sm[:, 1, x:x + 1], sm[:, 0, x:x + 1], -SCALE_B, None, ALU.mult
                                              ).then_inc(m_nb, 1)
                        for q in range(TT):
                            x = 4 * e + q
                            at, w = q * (q + 1) // 2 * P, (q + 1) * P
                            dve.wait_ge(m_exp, c(8, x + 1))
                            own.mark(dve.reciprocal(sm[:, 3, x:x + 1], sm[:, 2, x:x + 1]))
                            own.settle()
                            dve.tensor_scalar(prob[:, at:at + w], prob[:, at:at + w], sm[:, 3, x:x + 1], 0.5,
                                              ALU.mult, ALU.mult).then_inc(m_p, 1)

                    def turned(e):
                        for b in range(3):
                            r = slice((0, 512, 896)[b], (512, 896, 1280)[b])
                            dve.wait_ge(m_pthi, c(6, 3 * e + b + 1))
                            lo_of(pt_lo[:, r], bank[1 + e + b][:, 0:r.stop - r.start], pt_hi[:, r], m_ptlo)

                    def gates(m):
                        dve.wait_ge(m_th, c(2, m + 1))
                        dve.scalar_tensor_tensor(out=gt[:, m, :], in0=gt[:, m, :], scalar=1.0, in1=bank[0][:, :],
                                                 op0=ALU.add, op1=ALU.mult).then_inc(m_gt, 1)

                    def gated(e, src):
                        dve.wait_ge(m_o, c(2, e + 1))
                        dve.wait_ge(m_gt, c(2, e + 3))
                        dve.tensor_tensor(gt[:, e, :], src[:, :], gt[:, e, :], ALU.mult).then_inc(m_og, 1)

                    softmax(0)
                    turned(0)
                    gates(0)
                    softmax(1)
                    gated(0, bank[1])
                    turned(1)
                    gates(1)
                    gated(1, bank[7])
            own.leave(PAIRS // 2)
            first_tiles(bT, br_hi, br_lo, HA * VT)
            project_out(HB, bT, br_hi, br_lo, HA * VT)
            dve.wait_ge(aux["rows2"], 16)
            dve.wait_ge(aux["grow"], 16)
            norms(TT, ln=1, rms=0, gb=rows2, centred=h_tok, result=h_tok, round_=2)

            dve.wait_ge(l_w, 1)
            lo_of(wp_lo[:, :, :], wp[:, :, :], wp_hi[:, :, :], l_wl)
            dve.wait_ge(vst, 16)
            own.mark(dve.memset(upad[:, :, 0:PAD], 0.0))
            own.mark(dve.memset(upad[:, :, PAD + SEQ:], 0.0))
            own.settle()
            dve.wait_ge(aux["edge"], 16)

            def pooled(g):
                dve.wait_ge(l_up, g + 1)
                if g:
                    dve.wait_ge(l_plo, g)
                src, lo, hi = upad[:, g, :], 0, SEQ + 2 * PAD
                for level in range(g + 1):
                    dst = win[:, (g + 1 + level) % 2, :]
                    back = 1 if level == 0 else 2 ** (level - 1)
                    ahead = 0 if level == 0 else back
                    lo, hi = lo + back, hi - ahead
                    own.mark(dve.tensor_tensor(dst[:, lo:hi], src[:, lo - back:hi - back],
                                               src[:, lo + ahead:hi + ahead], ALU.add))
                    own.settle()
                    src = dst
                u = upad[:, g, PAD:PAD + SEQ]
                out_ = win[:, 0, 0:SEQ]
                own.mark(dve.tensor_tensor(src[:, PAD:2 * PAD], src[:, PAD:2 * PAD], edge[:, g, 0:PAD], ALU.mult))
                own.mark(dve.tensor_tensor(src[:, SEQ:SEQ + PAD], src[:, SEQ:SEQ + PAD], edge[:, g, PAD:], ALU.mult))
                own.settle()
                dve.scalar_tensor_tensor(out=out_, in0=src[:, PAD:PAD + SEQ], scalar=1.0 / WINDOWS[g], in1=u,
                                         op0=ALU.mult, op1=ALU.subtract).then_inc(l_pool, 1)

            def pooled_lo(g):
                dve.wait_ge(l_phi, g + 1)
                lo_of(pool_lo[:, :], win[:, 0, 0:SEQ], pool_hi[:, :], l_plo)

            pooled(0)
            pooled_lo(0)
            pooled(1)
            for m in range(4):
                dve.wait_ge(l_qhi, m + 1)
                lo_of(by_block(nq_lo[:, m, :]), from_rows(E[m][:, :]), by_block(nq_hi[:, m, :]), l_qlo)
            def keys(m):
                dve.wait_ge(l_qhi, m + 5)
                lo_of(nk_lo[:, m, :], O[m][:, :], nk_hi[:, m, :], l_qlo)
                if m < 3:
                    dve.wait_ge(l_mix, m + 1)
                    pooled_lo(m + 1)
                if m < 2:
                    pooled(m + 2)

            for m in range(3):
                keys(m)

            dve.wait_ge(aux["bias"], 16)
            dve.wait_ge(l_plo, 4)

            def normalise(m):
                dve.wait_ge(e_exp, 2 * m + 2)
                dve.reciprocal(nsm[:, m % 3, 2, :], nsm[:, m % 3, 1, :]).then_inc(e_rc, 1)
                dve.wait_ge(e_rc, m + 1)
                dve.tensor_scalar(nt[:, m % 3, 1, :], nt[:, m % 3, 1, :], nsm[:, m % 3, 2, 1:2], None, ALU.mult
                                  ).then_inc(e_q, 1)

            def turned(m):
                dve.wait_ge(e_thi, m + 1)
                lo_of(npt_lo[:, m % 2, :], bank[4 + m % 2][:, :], npt_hi[:, m % 2, :], e_tlo)

            for i in range(len(steps) + 2):
                if i == 2:
                    normalise(1)
                    keys(3)
                    dve.wait_ge(l_bhi, 2)
                    lo_of(xlo[:, 1, :], vband[:, 1, :], xhi[:, 1, :], l_blo1)
                    turned(0)
                if i < len(steps):
                    hp, j = steps[i]
                    at = BAND_START[j] - BLK * j + 16
                    dve.wait_ge(e_s, i + 1)
                    if i >= 3:
                        dve.wait_ge(e_t, i - 2)
                    for e in range(2):
                        last = dve.scalar_tensor_tensor(
                            out=nt[:, i % 3, e, :].rearrange("p (r c) -> p r c", r=ROWS),
                            in0=bank[2 * (i % 2) + e][:, 0:256].rearrange("p (r c) -> p r c", r=ROWS),
                            scalar=SCALE_N, in1=bias[:, 2 * hp + e, :, at:at + BAND], op0=ALU.mult, op1=ALU.add)
                        if e == 0:
                            own.mark(last)
                        else:
                            last.then_inc(e_tk, 1)
                if 1 <= i <= len(steps) and i != 2:
                    normalise(i - 1)
                if i < len(steps):
                    own.settle()
                    dve.wait_ge(e_tk, i + 1)
                    dve.tensor_reduce(nsm[:, i % 3, 0, :], nt[:, i % 3, :, :], AX, ALU.max, negate=True
                                      ).then_inc(e_nb, 1)
                if i > 2:
                    turned(i - 2)
                if i >= len(steps):
                    first_tiles(mixT, cr_hi, cr_lo, HA * VT + HB, 2 * (i - len(steps)), 2)
            project_out(KX, mixT, cr_hi, cr_lo, HA * VT + HB)
            dve.wait_ge(aux["grow"], 32)
            norms(2 * TT, rms=1, result=h2_tok, round_=3)

            def squared(m, i):
                dve.wait_ge(u_r, 4 * i + (m + 5))
                dve.tensor_tensor(hid[:, bass.ds(4 * i + m, 1), :].rearrange("p a n -> p (a n)"), relu[:, m, :],
                                  relu[:, m, :], ALU.mult).then_inc(u_s, 1)

            with dve.Fori(0, KF // 4 - 1) as i:
                for m in range(4):
                    squared(m, i)
            squared(0, KF // 4 - 1)
            squared(1, KF // 4 - 1)
            first_tiles(hid, dr_hi, dr_lo, HA * VT + HB + KX)
            squared(2, KF // 4 - 1)
            squared(3, KF // 4 - 1)
            project_out(KF, hid, dr_hi, dr_lo, HA * VT + HB + KX)
            dve.wait_ge(aux["grow"], 48)
            norms(3 * TT, rms=2, result=xres)


def panels(w, nk, width):
    k, n = w.shape
    x = w.reshape(k // (nk * P), nk, P, n // width, width).transpose(3, 0, 2, 1, 4)
    return x.reshape(-1, P, nk * width)


def kernel(**inputs):
    import concourse.bacc as bacc
    from concourse.bass_utils import run_bass_kernel_spmd

    f = {k: np.asarray(v) for k, v in inputs.items()}
    a_in, b_in, n_in = f["a_w_in"][0], f["b_w_in"][0], f["w_in_2"][0]
    groups = []
    for h in range(HA):
        q, k = a_in[:, h * DKA:(h + 1) * DKA], a_in[:, (HA + h) * DKA:(HA + h + 1) * DKA]
        v = a_in[:, 2 * HA * DKA + h * DVA:2 * HA * DKA + (h + 1) * DVA]
        g = a_in[:, 2 * HA * DKA + HA * DVA + h * DVA:2 * HA * DKA + HA * DVA + (h + 1) * DVA]
        groups += [panels(q, KX, 256), panels(k, KX, 256), panels(v, 4, 512), panels(g, KX, 256)]
    groups += [panels(f["a_w_out"][0], 2, DM)]
    groups += [panels(f["kv_w_down"][:, :KVLORA], 4, 512), panels(b_in[:, :512], 4, 512),
               panels(b_in[:, 512:QLORA], KX, 256)]
    uq = f["b_w_uq"][0].reshape(QLORA, HB, NOPE + ROPE)
    up = f["kv_w_up"].reshape(KVLORA, HB, NOPE + VH)
    for n in range(PAIRS):
        a, b = 2 * n, 2 * n + 1
        groups += [panels(np.concatenate([uq[:, a, :NOPE], uq[:, b, :NOPE], uq[:, a, NOPE:], uq[:, b, NOPE:]], 1),
                          KQ, 384),
                   panels(np.concatenate([up[:, a, :NOPE], up[:, b, :NOPE], up[:, a, NOPE:], up[:, b, NOPE:]], 1),
                          KC, 512),
                   panels(b_in[:, QLORA + n * 256:QLORA + (n + 1) * 256], KX, 256)]
    groups += [panels(f["b_w_out"][0], 2, DM)]
    groups += [panels(n_in[:, 1536:2048], 4, 512), panels(n_in[:, :512], KX, 256), panels(n_in[:, 512:1536], KX, 256)]
    groups += [panels(f["w_out_2"][0], 2, DM), panels(f["w_up_2"][0], KX, 256), panels(f["w_down_2"][0], 2, DM)]
    w = np.zeros((PANELS, P, PANEL), np.float32)
    at = 0
    for g in groups:
        w[at:at + len(g), :, :g.shape[2]] = g
        at += len(g)
    assert at == PANELS

    def column(v):
        return v.reshape(-1, P).T

    x = f["x"].reshape(SEQ, DM)
    a = {"w": w, "x": x.reshape(TT, P, DM).transpose(1, 0, 2), "xT": x.T.reshape(KX, P, SEQ).transpose(1, 0, 2)}
    a["cols"] = np.concatenate([column(f["kv_norm"]), column(f["b_q_norm"][0]), column(f["pool_scale_2"][0])], 1)
    a["ln"] = np.broadcast_to(np.stack([f["ln_g"], f["ln_b"]], 1)[:, None], (2, P, 2, DM))
    a["grow"] = np.broadcast_to(np.stack([f["norm_mix_g_2"][0], f["norm_mlp_g_2"][0], f["final_g_2"]])[:, None],
                                (3, P, DM))
    kr = f["kv_w_down"][:, KVLORA:]
    a["wkr"] = np.concatenate([kr, kr], 1).reshape(KX, P, P).transpose(1, 0, 2)
    a["wp"] = f["w_pool_2"][0].transpose(1, 0, 2)
    rpb = np.pad(f["rpb_2"][0], ((0, 0), (0, 0), (16, 16)))
    strip = np.zeros((ROWS, BLK, HN, ROWS, BIAS_W), np.float32)
    for r in range(ROWS):
        for c in range(BLK):
            strip[r, c] = rpb[:, 7 - r:7 - r + ROWS, 15 - c:15 - c + BIAS_W]
    a["bias"] = strip.reshape(P, HN, ROWS, BIAS_W)

    def angles(half):
        inv = np.float32(10000.0) ** (-np.arange(half, dtype=np.float32) / np.float32(half))
        return (inv[:, None] * np.arange(SEQ, dtype=np.float32)[None, :]).astype(np.float64)

    ang = angles(DKA // 2)
    a["rope_a"] = np.stack([np.cos(ang), np.sin(ang)], 1)
    ang = np.tile(angles(ROPE // 2), (4, 1))
    sign = np.where(np.arange(P) % ROPE < ROPE // 2, 1.0, -1.0)[:, None]
    a["rope_b"] = np.stack([np.cos(ang), np.sin(ang) * sign], 1)
    dist = np.arange(SEQ)[None, :] - np.arange(P)[:, None]
    log_gamma = np.log1p(-np.exp2(-5.0 - np.arange(HA)))
    a["decay"] = np.where(dist >= 0, np.exp(np.maximum(dist, 0)[None] * log_gamma[:, None, None]), 0.0) * DKA ** -0.5
    a["ident"] = np.eye(P)
    a["mask"] = np.where(np.arange(P)[None, :] > np.arange(P)[:, None], MASKED, 0.0)
    q = np.arange(P) % BLK
    nmask = np.zeros((P, NBLK, BAND))
    for j in range(NBLK):
        c0 = np.clip(j * BLK + q - 8, 0, GRID - BLK)[:, None]
        key = BAND_START[j] + np.arange(BAND)[None, :]
        nmask[:, j] = np.where((key >= c0) & (key < c0 + BLK), 0.0, MASKED)
    a["nmask"] = nmask
    tok = np.arange(SEQ)
    edge = np.zeros((4, 2 * PAD))
    for g, wd in enumerate(WINDOWS):
        count = np.clip(tok - wd // 2 + wd, 0, SEQ) - np.clip(tok - wd // 2, 0, SEQ)
        ratio = wd / count
        edge[g] = np.concatenate([ratio[:PAD], ratio[-PAD:]])
    a["edge"] = np.broadcast_to(edge, (P, 4, 2 * PAD))

    nc = bacc.Bacc("TRN2", target_bir_lowering=False, num_devices=1)
    arrays, t = {}, {}
    for name, v in a.items():
        v = np.ascontiguousarray(v, dtype=np.float32)
        arrays[f"in_{name}"] = v
        t[name] = nc.dram_tensor(f"in_{name}", v.shape, F32, kind="ExternalInput").ap()
    t["o_spill"] = nc.dram_tensor("o_spill", (HB, P, SEQ), F32).ap()
    t["v_spill"] = nc.dram_tensor("v_spill", (SEQ, SEQ), F32).ap()
    out = nc.dram_tensor("out_0", (SEQ, DM), F32, kind="ExternalOutput").ap()
    program(nc, t, out)
    r = run_bass_kernel_spmd(nc, [arrays], core_ids=[0])
    return r.results[0]["out_0"].reshape(1, SEQ, DM)
```
